# Optimizing a Trainium2 kernel written in Bass

```python
import math
import jax, jax.numpy as jnp
from jax import lax
import numpy as np

D_MODEL = 1024
BATCH = 1
SEQ = 512
DEPTH = 1
DEC_BATCH = 8
DEC_SEQ = 1
PAST_LEN = 1024
PAGE_SIZE = 128

D_RNN = D_MODEL // 2
LRU_BLOCKS = 8
LRU_BW = D_RNN // LRU_BLOCKS
CONV_W = 4
LRU_C = 8.0
N_HEADS = 8
HEAD_DIM = (D_MODEL - D_RNN) // N_HEADS
N_KV = 2
GROUP = N_HEADS // N_KV
D_ATT = N_HEADS * HEAD_DIM
D_MIX = D_RNN + D_ATT
CMP_LEN = 32
CMP_STRIDE = 16
CMP_RATIO = CMP_LEN // CMP_STRIDE
CMP_HID = HEAD_DIM
SEL_BLOCK = 64
SEL_TOP = 16
WINDOW = 512
Q_BLOCK = 128
SCALE = HEAD_DIM ** -0.5
NEG_INF = -1e30
FORCE_SCORE = 1e6
NUM_BUCKETS = 32
MAX_DISTANCE = 1024
PEER_HEADS = 8
PEER_KEYS = 128
PEER_EXPERTS = PEER_KEYS * PEER_KEYS
PEER_DKEY = 256
PEER_TOPK = 16
PEER_CHUNK = 128
NORM_EPS = 1e-6
COL_SIZES = (D_RNN, D_RNN, D_ATT, 2 * N_KV * HEAD_DIM, 2 * N_KV * HEAD_DIM, 2 * N_KV * HEAD_DIM, 3 * N_HEADS)
IN_COLS = sum(COL_SIZES)

kernel_name = 'hymba_rglru_nsa_peer_step'

def rmsnorm(x, g):
    xf = x.astype(jnp.float32)
    y = xf * lax.rsqrt(jnp.mean(xf * xf, axis=-1, keepdims=True) + NORM_EPS)
    return (y * g.astype(jnp.float32)).astype(x.dtype)

def ada_mod(c, w, b):
    m = (jax.nn.silu(c) @ w + b)[:, None, :]
    return jnp.split(m, 6, axis=-1)

def split_columns(z):
    offs = np.cumsum((0,) + COL_SIZES)
    return [z[..., int(offs[i]):int(offs[i + 1])] for i in range(len(COL_SIZES))]

def t5_bucket(dist):
    d = jnp.maximum(dist, 0)
    max_exact = NUM_BUCKETS // 2
    df = jnp.maximum(d, 1).astype(jnp.float32)
    large = max_exact + (jnp.log(df / max_exact) / math.log(MAX_DISTANCE / max_exact)
                         * (NUM_BUCKETS - max_exact)).astype(jnp.int32)
    large = jnp.minimum(large, NUM_BUCKETS - 1)
    return jnp.where(d < max_exact, d, large)

def causal_conv(x, buf, w, b):
    T = x.shape[1]
    xp = jnp.concatenate([buf.astype(x.dtype), x], axis=1)
    y = sum(xp[:, k:k + T] * w[k] for k in range(CONV_W)) + b
    return y, xp[:, -(CONV_W - 1):]

def _linear_combine(left, right):
    a1, b1 = left
    a2, b2 = right
    return a1 * a2, a2 * b1 + b2

def rg_lru(xc, h0, wa, ba, wi, bi, lam):
    B, T, _ = xc.shape
    xb = xc.reshape(B, T, LRU_BLOCKS, LRU_BW)
    r = jax.nn.sigmoid((jnp.einsum('btnd,nde->btne', xb, wa).reshape(B, T, D_RNN) + ba).astype(jnp.float32))
    i = jax.nn.sigmoid((jnp.einsum('btnd,nde->btne', xb, wi).reshape(B, T, D_RNN) + bi).astype(jnp.float32))
    log_a = -LRU_C * r * jax.nn.softplus(-lam.astype(jnp.float32))
    a = jnp.exp(log_a)
    u = jnp.sqrt(-jnp.expm1(2.0 * log_a)) * i * xc.astype(jnp.float32)
    u = u.at[:, 0].add(a[:, 0] * h0.astype(jnp.float32))
    _, h = lax.associative_scan(_linear_combine, (a, u), axis=1)
    return h.astype(xc.dtype), h[:, -1].astype(xc.dtype)

def chunk_proj(rows, w1):
    B, T = rows.shape[:2]
    n = T // CMP_STRIDE
    ch = rows[:, :n * CMP_STRIDE].reshape(B, n, CMP_STRIDE, N_KV, 2, HEAD_DIM)
    w1r = w1.reshape(2, CMP_RATIO, CMP_STRIDE, HEAD_DIM, CMP_HID)
    return jnp.einsum('bnsgcd,cmsdh->bnmgch', ch, w1r)

def compress(proj, w1, w2, pos):
    nb = proj.shape[1] - CMP_RATIO + 1
    hid = jnp.einsum('csd,csdh->ch', pos, w1)
    for m in range(CMP_RATIO):
        hid = hid + proj[:, m:m + nb, m]
    out = jnp.einsum('bngch,che->bngce', jax.nn.gelu(hid), w2)
    ends = jnp.arange(nb, dtype=jnp.int32) * CMP_STRIDE + (CMP_LEN - 1)
    return out, ends

def dense_attend(q, q_pos, k, v, k_pos, rel_bias, window):
    Tq, Nk = q.shape[1], k.shape[1]
    dist = q_pos[:, None] - k_pos[None, :]
    valid = (dist >= 0) & (k_pos[None, :] >= 0)
    if window is not None:
        valid = valid & (dist < window)
    bias = rel_bias[t5_bucket(dist)].reshape(Tq, Nk, N_KV, GROUP).transpose(2, 3, 0, 1)
    s = jnp.einsum('bqgrd,bkgd->bgrqk', q, k).astype(jnp.float32) * SCALE + bias.astype(jnp.float32)
    s = jnp.where(valid, s, NEG_INF)
    p = jax.nn.softmax(s, axis=-1) * jnp.any(valid, axis=-1, keepdims=True)
    o = jnp.einsum('bgrqk,bkgd->bqgrd', p.astype(v.dtype), v)
    return o, p

def select_blocks(p_cmp, q_pos, n_sel):
    n_cmp = p_cmp.shape[-1]
    start = jnp.arange(n_cmp) * CMP_STRIDE
    blk = jnp.arange(n_sel)
    covers = ((start[:, None] < (blk[None, :] + 1) * SEL_BLOCK)
              & (start[:, None] + CMP_LEN > blk[None, :] * SEL_BLOCK)).astype(p_cmp.dtype)
    score = jnp.einsum('bgrqn,nj->bqgj', p_cmp, covers)
    cur = (q_pos // SEL_BLOCK)[:, None]
    forced = (blk[None, :] == 0) | (blk[None, :] == cur) | (blk[None, :] == cur - 1)
    eligible = blk[None, :] * SEL_BLOCK <= q_pos[:, None]
    score = jnp.where(forced[None, :, None, :], FORCE_SCORE,
                      jnp.where(eligible[None, :, None, :], score, -1.0))
    _, idx = lax.top_k(score, min(SEL_TOP, n_sel))
    return idx

def select_attend(q, q_pos, blk, idx, rel_bias):
    B, Tq = q.shape[:2]
    k_pos = idx[..., None] * SEL_BLOCK + jnp.arange(SEL_BLOCK, dtype=jnp.int32)
    dist = q_pos[None, :, None, None, None] - k_pos
    bias = rel_bias.reshape(NUM_BUCKETS, N_KV, GROUP)[t5_bucket(dist), jnp.arange(N_KV)[:, None, None]]
    s = jnp.einsum('bqgrd,bqgjsd->bqgjsr', q, blk[..., 0, :]).astype(jnp.float32) * SCALE + bias.astype(jnp.float32)
    s = jnp.where((dist >= 0)[..., None], s, NEG_INF)
    p = jax.nn.softmax(s.reshape(B, Tq, N_KV, -1, GROUP), axis=3).reshape(s.shape)
    return jnp.einsum('bqgjsr,bqgjsd->bqgrd', p.astype(blk.dtype), blk[..., 1, :])

def nsa_prompt(q, kv_c, kv_s, kv_w, cmp_w, rel_bias):
    B, T = q.shape[:2]
    q_pos = jnp.arange(T, dtype=jnp.int32)
    ck, ends = compress(chunk_proj(kv_c, cmp_w[0]), *cmp_w)
    o_c, p_c = dense_attend(q, q_pos, ck[..., 0, :], ck[..., 1, :], ends, rel_bias, None)
    n_sel = T // SEL_BLOCK
    idx = select_blocks(p_c, q_pos, n_sel)
    win_pad = jnp.pad(kv_w, ((0, 0), (WINDOW, 0), (0, 0), (0, 0), (0, 0)))
    b_ix = jnp.arange(B)[:, None, None, None, None]
    g_ix = jnp.arange(N_KV)[None, None, :, None, None]

    def q_block(c):
        s0 = c * Q_BLOCK
        qb = lax.dynamic_slice_in_dim(q, s0, Q_BLOCK, axis=1)
        pb = s0 + jnp.arange(Q_BLOCK, dtype=jnp.int32)
        ib = lax.dynamic_slice_in_dim(idx, s0, Q_BLOCK, axis=1)
        rows = ib[..., None] * SEL_BLOCK + jnp.arange(SEL_BLOCK)
        o_s = select_attend(qb, pb, kv_s[b_ix, rows, g_ix], ib, rel_bias)
        kw = lax.dynamic_slice_in_dim(win_pad, s0, WINDOW + Q_BLOCK, axis=1)
        kp = s0 - WINDOW + jnp.arange(WINDOW + Q_BLOCK, dtype=jnp.int32)
        o_w, _ = dense_attend(qb, pb, kw[..., 0, :], kw[..., 1, :], kp, rel_bias, WINDOW)
        return o_s, o_w

    o_s, o_w = lax.map(q_block, jnp.arange(T // Q_BLOCK, dtype=jnp.int32))
    o_s = jnp.moveaxis(o_s, 0, 1).reshape(q.shape)
    o_w = jnp.moveaxis(o_w, 0, 1).reshape(q.shape)
    return o_c, o_s, o_w, kv_w[:, -min(WINDOW, T):]

def nsa_sample(q, kv_c, kv_s, kv_w, cache_cmp, cache_sel, cache_win, page_table, layer, cmp_w, rel_bias):
    B, T = q.shape[:2]
    n_pages = page_table.shape[1]
    past = n_pages * PAGE_SIZE
    q_pos = past + jnp.arange(T, dtype=jnp.int32)
    past_c = cache_cmp[layer, page_table].reshape(B, past, N_KV, 2, HEAD_DIM)
    proj = jnp.concatenate([chunk_proj(past_c, cmp_w[0]), chunk_proj(kv_c, cmp_w[0])], axis=1)
    ck, ends = compress(proj, *cmp_w)
    o_c, p_c = dense_attend(q, q_pos, ck[..., 0, :], ck[..., 1, :], ends, rel_bias, None)
    n_sel = -(-(past + T) // SEL_BLOCK)
    idx = select_blocks(p_c, q_pos, n_sel)
    n_past_blk = past // SEL_BLOCK
    n_new_blk = n_sel - n_past_blk
    blk_per_page = PAGE_SIZE // SEL_BLOCK
    b_ix = jnp.arange(B)[:, None, None, None, None]
    g_ix = jnp.arange(N_KV)[None, None, :, None, None]
    phys = page_table[b_ix[..., 0], jnp.minimum(idx // blk_per_page, n_pages - 1)]
    rows = (idx % blk_per_page)[..., None] * SEL_BLOCK + jnp.arange(SEL_BLOCK)
    from_past = cache_sel[layer, phys[..., None], rows, g_ix]
    new_pad = jnp.pad(kv_s, ((0, 0), (0, n_new_blk * SEL_BLOCK - T), (0, 0), (0, 0), (0, 0)))
    rows_new = jnp.clip(idx - n_past_blk, 0, n_new_blk - 1)[..., None] * SEL_BLOCK + jnp.arange(SEL_BLOCK)
    from_new = new_pad[b_ix, rows_new, g_ix].astype(from_past.dtype)
    blk = jnp.where((idx < n_past_blk)[..., None, None, None], from_past, from_new)
    o_s = select_attend(q, q_pos, blk, idx, rel_bias)
    wb = cache_win.shape[1]
    kw = jnp.concatenate([cache_win, kv_w.astype(cache_win.dtype)], axis=1)
    kp = jnp.concatenate([past - wb + jnp.arange(wb, dtype=jnp.int32), q_pos])
    o_w, _ = dense_attend(q, q_pos, kw[..., 0, :], kw[..., 1, :], kp, rel_bias, WINDOW)
    return o_c, o_s, o_w, kw[:, -wb:]

def peer_ffn(x, wq, bq, subkeys, u_tab, v_tab):
    n, d = x.shape
    n_chunks = -(-n // PEER_CHUNK)
    xp = jnp.pad(x, ((0, n_chunks * PEER_CHUNK - n), (0, 0))).reshape(n_chunks, PEER_CHUNK, d)
    half = PEER_DKEY // 2

    def chunk_fn(xc):
        q = (xc @ wq + bq).reshape(PEER_CHUNK, PEER_HEADS, 2, half)
        s = jnp.einsum('nhpd,hpkd->nhpk', q, subkeys).astype(jnp.float32)
        sv, si = lax.top_k(s, PEER_TOPK)
        cand = (sv[:, :, 0, :, None] + sv[:, :, 1, None, :]).reshape(PEER_CHUNK, PEER_HEADS, PEER_TOPK * PEER_TOPK)
        best, ci = lax.top_k(cand, PEER_TOPK)
        e = (jnp.take_along_axis(si[:, :, 0], ci // PEER_TOPK, axis=-1) * PEER_KEYS
             + jnp.take_along_axis(si[:, :, 1], ci % PEER_TOPK, axis=-1))
        g = jax.nn.softmax(best, axis=-1)
        z = jnp.einsum('nd,nhkd->nhk', xc, u_tab[e])
        act = (jax.nn.gelu(z.astype(jnp.float32)) * g).astype(xc.dtype)
        return jnp.einsum('nhk,nhkd->nd', act, v_tab[e])

    return lax.map(chunk_fn, xp).reshape(-1, d)[:n]

def layer_forward(x, c, lw, rel_bias, past):
    (ada_w, ada_b, norm1_g, norm2_g, w_in, conv_w, conv_b, lru_wa, lru_ba, lru_wi, lru_bi,
     lru_lambda, cmp_w1, cmp_w2, cmp_pos, out_norm_lru, out_norm_att, w_out,
     peer_wq, peer_bq, peer_subkeys, peer_u, peer_v) = lw
    B, T, _ = x.shape
    sh1, sc1, gt1, sh2, sc2, gt2 = ada_mod(c, ada_w, ada_b)
    h = rmsnorm(x, norm1_g) * (1.0 + sc1) + sh1
    xr, yg, q, kv_c, kv_s, kv_w, gl = split_columns(h @ w_in)
    kv_shape = (B, T, N_KV, 2, HEAD_DIM)
    kv_c, kv_s, kv_w = kv_c.reshape(kv_shape), kv_s.reshape(kv_shape), kv_w.reshape(kv_shape)
    q = q.reshape(B, T, N_KV, GROUP, HEAD_DIM)
    cmp_w = (cmp_w1, cmp_w2, cmp_pos)
    if past is None:
        conv_buf = jnp.zeros((B, CONV_W - 1, D_RNN), x.dtype)
        h0 = jnp.zeros((B, D_RNN), x.dtype)
        o_c, o_s, o_w, new_win = nsa_prompt(q, kv_c, kv_s, kv_w, cmp_w, rel_bias)
    else:
        cache_cmp, cache_sel, cache_win, h0, conv_buf, page_table, layer = past
        o_c, o_s, o_w, new_win = nsa_sample(q, kv_c, kv_s, kv_w, cache_cmp, cache_sel, cache_win,
                                            page_table, layer, cmp_w, rel_bias)
    xc, new_conv = causal_conv(xr, conv_buf, conv_w, conv_b)
    hs, new_h = rg_lru(xc, h0, lru_wa, lru_ba, lru_wi, lru_bi, lru_lambda)
    o_lru = hs * jax.nn.gelu(yg)
    g = jax.nn.sigmoid(gl).reshape(B, T, 3, N_KV, GROUP, 1)
    o_att = (g[:, :, 0] * o_c + g[:, :, 1] * o_s + g[:, :, 2] * o_w).reshape(B, T, D_ATT)
    mixed = jnp.concatenate([rmsnorm(o_lru, out_norm_lru), rmsnorm(o_att, out_norm_att)], axis=-1) @ w_out
    x = x + gt1 * mixed
    h2 = rmsnorm(x, norm2_g) * (1.0 + sc2) + sh2
    ff = peer_ffn(h2.reshape(B * T, D_MODEL), peer_wq, peer_bq, peer_subkeys, peer_u, peer_v)
    x = x + gt2 * ff.reshape(B, T, D_MODEL)
    return x, (kv_c, kv_s, new_win, new_h, new_conv)

def setup_inputs(seed: int = 0) -> dict:
    key = jax.random.key(seed)
    ks = iter(jax.random.split(key, 48))

    def nrm(shape, scale):
        return jax.random.normal(next(ks), shape, jnp.float32) * scale

    def gain(shape):
        return 1.0 + nrm(shape, 0.02)

    L = DEPTH
    n_pages = PAST_LEN // PAGE_SIZE
    n_pool = (5 * DEC_BATCH * n_pages) // 4
    win_buf = min(WINDOW, PAST_LEN)
    a_init = jax.random.uniform(next(ks), (L, D_RNN), jnp.float32, 0.9, 0.999) ** (1.0 / LRU_C)
    page_table = jax.random.permutation(next(ks), n_pool)[:DEC_BATCH * n_pages].reshape(DEC_BATCH, n_pages).astype(jnp.int32)
    return {
        'x_prompt': nrm((BATCH, SEQ, D_MODEL), 1.0),
        'x_sample': nrm((DEC_BATCH, DEC_SEQ, D_MODEL), 1.0),
        'cache_cmp_kv': nrm((L, n_pool, PAGE_SIZE, N_KV, 2, HEAD_DIM), 1.0),
        'cache_sel_kv': nrm((L, n_pool, PAGE_SIZE, N_KV, 2, HEAD_DIM), 1.0),
        'cache_win_kv': nrm((L, DEC_BATCH, win_buf, N_KV, 2, HEAD_DIM), 1.0),
        'state_lru_h': nrm((L, DEC_BATCH, D_RNN), 0.5),
        'state_conv': nrm((L, DEC_BATCH, CONV_W - 1, D_RNN), 1.0),
        'page_table': page_table,
        'c_prompt': nrm((BATCH, D_MODEL), 1.0),
        'c_sample': nrm((DEC_BATCH, D_MODEL), 1.0),
        'ada_w': nrm((L, D_MODEL, 6 * D_MODEL), 0.5 * D_MODEL ** -0.5),
        'ada_b': nrm((L, 6 * D_MODEL), 0.02),
        'norm1_g': gain((L, D_MODEL)),
        'norm2_g': gain((L, D_MODEL)),
        'w_in': nrm((L, D_MODEL, IN_COLS), D_MODEL ** -0.5),
        'conv_w': nrm((L, CONV_W, D_RNN), CONV_W ** -0.5),
        'conv_b': nrm((L, D_RNN), 0.02),
        'lru_wa': nrm((L, LRU_BLOCKS, LRU_BW, LRU_BW), LRU_BW ** -0.5),
        'lru_ba': nrm((L, D_RNN), 0.02),
        'lru_wi': nrm((L, LRU_BLOCKS, LRU_BW, LRU_BW), LRU_BW ** -0.5),
        'lru_bi': nrm((L, D_RNN), 0.02),
        'lru_lambda': jnp.log(a_init) - jnp.log1p(-a_init),
        'cmp_w1': nrm((L, 2, CMP_LEN, HEAD_DIM, CMP_HID), (CMP_LEN * HEAD_DIM) ** -0.5),
        'cmp_w2': nrm((L, 2, CMP_HID, HEAD_DIM), CMP_HID ** -0.5),
        'cmp_pos': nrm((L, 2, CMP_LEN, HEAD_DIM), 0.1),
        'out_norm_lru': gain((L, D_RNN)),
        'out_norm_att': gain((L, D_ATT)),
        'w_out': nrm((L, D_MIX, D_MODEL), D_MIX ** -0.5),
        'peer_wq': nrm((L, D_MODEL, PEER_HEADS * PEER_DKEY), D_MODEL ** -0.5),
        'peer_bq': nrm((L, PEER_HEADS * PEER_DKEY), 0.02),
        'peer_subkeys': nrm((L, PEER_HEADS, 2, PEER_KEYS, PEER_DKEY // 2), (PEER_DKEY // 2) ** -0.5),
        'peer_u': nrm((L, PEER_EXPERTS, D_MODEL), D_MODEL ** -0.5),
        'peer_v': nrm((L, PEER_EXPERTS, D_MODEL), PEER_HEADS ** -0.5),
        'rel_bias': nrm((NUM_BUCKETS, N_HEADS), 0.3),
        'final_g': gain((D_MODEL,)),
    }

def reference(x_prompt, x_sample, cache_cmp_kv, cache_sel_kv, cache_win_kv, state_lru_h, state_conv,
              page_table, c_prompt, c_sample, ada_w, ada_b, norm1_g, norm2_g, w_in, conv_w, conv_b,
              lru_wa, lru_ba, lru_wi, lru_bi, lru_lambda, cmp_w1, cmp_w2, cmp_pos, out_norm_lru,
              out_norm_att, w_out, peer_wq, peer_bq, peer_subkeys, peer_u, peer_v, rel_bias, final_g):
    y_prompt, y_sample = x_prompt, x_sample
    new_p, new_s = [], []
    for l in range(DEPTH):
        lw = (ada_w[l], ada_b[l], norm1_g[l], norm2_g[l], w_in[l], conv_w[l], conv_b[l], lru_wa[l],
              lru_ba[l], lru_wi[l], lru_bi[l], lru_lambda[l], cmp_w1[l], cmp_w2[l], cmp_pos[l],
              out_norm_lru[l], out_norm_att[l], w_out[l], peer_wq[l], peer_bq[l], peer_subkeys[l],
              peer_u[l], peer_v[l])
        y_prompt, sp = layer_forward(y_prompt, c_prompt, lw, rel_bias, None)
        past = (cache_cmp_kv, cache_sel_kv, cache_win_kv[l], state_lru_h[l], state_conv[l], page_table, l)
        y_sample, ss = layer_forward(y_sample, c_sample, lw, rel_bias, past)
        new_p.append(sp)
        new_s.append(ss)
    y_prompt = rmsnorm(y_prompt, final_g)
    y_sample = rmsnorm(y_sample, final_g)

    def stk(states, i):
        return jnp.stack([s[i] for s in states])

    return (y_prompt, y_sample,
            stk(new_p, 0), stk(new_s, 0),
            stk(new_p, 1), stk(new_s, 1),
            stk(new_p, 2), stk(new_s, 2),
            stk(new_p, 3), stk(new_s, 3),
            stk(new_p, 4), stk(new_s, 4))


_drawn_inputs = setup_inputs


def setup_inputs(seed=0):
    import zlib

    import numpy as np

    out = dict(_drawn_inputs(seed))
    spreads = {}
    factors = {'norm1_g': 2.781,
     'norm2_g': 6.941,
     'lru_ba': 8.0,
     'lru_bi': 6.857,
     'out_norm_lru': 8.0,
     'out_norm_att': 8.0,
     'peer_bq': 7.095,
     'final_g': 2.833}
    for name, (base, spread) in spreads.items():
        noise = np.random.default_rng([zlib.crc32(name.encode()), seed]).standard_normal(out[name].shape)
        drawn = base * np.exp(spread * noise) if base else spread * noise
        out[name] = __import__('jax').numpy.asarray(drawn.astype(out[name].dtype))
    for name, factor in factors.items():
        out[name] = (out[name] * factor).astype(out[name].dtype)
    return out
```

```python
from contextlib import ExitStack

import concourse.bass as bass
from concourse import mybir
import numpy as np

F32 = mybir.dt.float32
U32 = mybir.dt.uint32
ALU = mybir.AluOpType
ACT = mybir.ActivationFunctionType
AX = mybir.AxisListType
ADD, MUL, SUB, MAX, MIN, EQ = ALU.add, ALU.mult, ALU.subtract, ALU.max, ALU.min, ALU.is_equal

P = 128
D = 1024
KD = D // P
SEQ = 512
NB = 8
TOK = SEQ + NB
HALF = TOK // 2
PAST = 1024
PAGE = 128
PAGES = PAST // PAGE
POOL = 5 * NB * PAGES // 4
HD = 64
NH = 8
NKV = 2
GRP = NH // NKV
ROWS = NB * NH
NCMP_P = SEQ // 16 - 1
NCMP_S = PAST // 16 - 1
NSELB = 14
NEG = -1e30
EPS = 1e-6
ZC = 18
XR, YG, QC, KC, VC_, KS, VS, KW, VW = 0, 4, 8, 12, 13, 14, 15, 16, 17
EXP_J = 8
GROUPS = P // EXP_J
AW = 384
AN = 6 * D // AW
TC = 104
OHD_W, OHA_W, OHW_W = 1161, 1024, 512
EDGES = [21, 27, 35, 46, 59, 77, 99, 128, 166, 216, 280, 363, 470, 609, 790]


def build(nc, io):
    ctx = ExitStack()
    with ctx:
        def sem(name):
            return ctx.enter_context(nc.semaphore(name))

        def sb(name, shape, dt=F32):
            return ctx.enter_context(nc.sbuf_tensor(name, shape, dt))

        xT = sb("xT", [P, KD, TOK])
        mT = sb("mT", [P, 48, 9])
        ident = sb("ident", [P, P])
        ones = sb("ones", [P, P])
        par = sb("par", [P, 128])
        posb = sb("posb", [P, 1])
        gates = sb("gates", [P, 5, 24])
        gate_rows = sb("gate_rows", [ROWS, 3])
        cst = sb("cst", [P, 540])
        arena = sb("arena", [P, 46700])
        ps = ctx.enter_context(nc.psum_tensor("ps", [P, 8, 512], F32))

        N1G, N2G, FG, NLG, NAG, CW, CB, BA, BI, LAM, BQ, ADB = 0, 8, 16, 24, 28, 32, 48, 52, 56, 60, 64, 80
        rbx, rb, newmask, gsum = cst[:, 0:64], cst[:, 64:72], cst[:, 72:80], cst[:, 80:144]
        validq, blkno, small = cst[:, 144:145], cst[:, 145:161], cst[:, 161:441]
        lrt, pstt, pcmt = cst[:, 441:481], cst[:, 481:513], cst[:, 513:529]

        def lr(n):
            return lrt[:, 4 * n:4 * n + 4]

        def sm(n):
            return small[0:ROWS, 200 + n:201 + n]

        def pst(u, n):
            return pstt[:, (u % 2) * 16 + 4 * n:(u % 2) * 16 + 4 * n + 4]

        def pcm(n):
            return pcmt[:, 8 * n:8 * n + 8]

        def at(off, *shape):
            n = int(np.prod(shape))
            assert off + n <= 46700
            a = arena[:, off:off + n]
            return a.rearrange("p (a b) -> p a b", b=shape[1]) if len(shape) == 2 else a

        zT = at(0, ZC, TOK)
        hT = at(9360, KD, TOK)
        ada = at(13520, 2 * KD, AW)
        win_w = at(19664, 3 * KD, P)
        X = at(22736, 8736)
        w1 = at(31472, 32, P)
        ohd = at(35568, OHD_W)
        oha = at(36729, OHA_W)
        hid = at(37753, 546)
        ckT = at(38299, 544)
        vc = at(38843, 9, P)
        w2 = at(39995, 2, P)
        biasT = at(40251, NH, 512)
        m9 = at(40251, 2, AW)
        cT = at(41275, KD, 9)
        rsb = at(41475, 640)
        pbias = at(44347, 4, NH * NCMP_P)
        rstd = at(45339, TOK)
        wgate = at(45859, KD, 24)
        stc = at(46051, 4, 3 * NB)
        h0T = at(46147, 4, NB)
        rT, iT_ = at(9360, 4, TOK), at(11440, 4, TOK)
        xcT, aT, uT = at(13520, 4, TOK), at(15600, 4, TOK), at(17680, 4, TOK)
        wlru = at(19760, 8, P)
        outh = at(20912, 4, 9)
        outc = at(20948, 4, 27)
        sel = at(13520, NB * PAGES, 256)
        qz = at(29904, 2 * GRP, SEQ)
        qpad = at(34000, NB, ROWS)
        qs = at(34512, ROWS)
        vnew = at(34576, 2, P)
        vn = at(36729, 8, P)
        ohw = at(9360, OHW_W)
        ss = at(9872, 1032)
        sw = at(10904, 520)
        sc = at(11424, 64)
        gs = at(11488, 64)
        pts = at(11552, 15, ROWS)
        kwin = at(13520, NB, 512)
        vwin = at(17616, NB * 4, P)
        wout = at(21712, KD, D)
        pbuf = at(9360, 2 * GRP, SEQ)
        ptb = at(13520, 4, GRP * P)
        ptcb = at(15568, 1024)
        pcb = at(16592, NH * NCMP_P)
        h2T = at(9360, KD, TOK)
        wq = at(0, 3 * KD, P)
        qT = at(3072, 2, TOK)
        sk = at(4112, 16, P)
        sv = at(6160, 5 * 16, 16)
        si = arena[:, 7440:8720].bitcast(U32).rearrange("p (a b) -> p a b", b=16)
        routeT = at(13520, 3, TOK)
        iota = at(15080, P)
        iota16 = at(15208, 16)
        tmpk = at(15232, 5, P)
        sif = at(15880, 5 * 16, 16)
        cand = at(17160, NH, 256)
        cand2 = at(19208, NH, 256)
        ci = arena[:, 21256:21384].bitcast(U32)
        cab = arena[:, 21384:21640].bitcast(U32).rearrange("p (a b) -> p a b", b=P)
        best = at(21640, NH, 16)
        cabf = at(21768, 2, P)
        isel = at(22024, 3, P)
        gden = at(22408, 2, NH)
        oh = at(3072, 2 * 4, 2 * P)
        stage = at(17160, 2, P * TC)
        ur = at(0, 4 * KD, P)
        acc = at(4096, KD, TOK)
        vr = at(13520, 2 * EXP_J, D)
        av = at(29904, 2 * EXP_J, TOK)
        gr = at(38224, 2 * EXP_J, TOK)
        sq = at(13520, KD, TOK)

        names = """rows_stored c_loaded par_loaded table_loaded const_loaded x_loaded ada_ready z_ready wgate_loaded lrus_loaded
            hi_ready lruw_loaded z_moved kv_stored lru_ready lru_stored lru_norm ohw_loaded gates_ready
            gate_stored gate_moved sel_free win_loaded wout_loaded out_stored proj_done sk_loaded q_ready
            stage_full g_ready a_ready ff_ready zz_ready fin_ready pool_done memset_done w2_loaded w1k_loaded
            pos_loaded page_loaded gather_k hid_ready w1v_loaded pos2_loaded gather_v gather_s rs_copied mt_done
            scratch_stored bias_loaded bias_ready rb_ready rs_ready pb_ready silu_done m9_ready mt_ready sq_done
            sum_ready h_ready zg_ready xc_ready ri_ready gate_ready x_filled gelu_ready ck_ready mix_sum
            cmp_done vt_ready vt_done qpad_ready sc_ready ss_ready sc_soft sum_done ss_p pts_ready pts_done
            sw_ready sw_p ptw_ready ptw_done os_ready os_done u_ttr u_s pc_s pc_p u_tdone pc_t pc_tdone o_done
            u_p u_t u_pv mix_sq mix_ready proj_ready pe_step q_moved s_free s_ready tr_in tr_ready tr_done
            oh_ready g_moved gelu_done ff_free act_step root_in rstd_ready lru_prep exp_ready yg_ready sc_exp
            ss_max ss_exp sw_max sw_exp pc_max pc_exp u_max u_exp u_rs rexp rexp_done dve_step hot_step""".split()
        S = {n: sem(n) for n in names}
        ada_l = [sem(f"ada_loaded{i}") for i in range(2)]
        w_l = [sem(f"w_loaded{i}") for i in range(3)]
        wq_l = [sem(f"wq_loaded{i}") for i in range(3)]
        u_l = [sem(f"u_loaded{i}") for i in range(4)]
        v_l = [sem(f"v_loaded{i}") for i in range(2)]
        g_l = [sem(f"g_loaded{i}") for i in range(2)]
        st_l = [sem(f"stage_stored{i}") for i in range(2)]

        rscratch = io["rscratch"]
        gw = io["gw"]
        block = ctx.enter_context(nc.Block())
        units = [(i, br, g) for i in range(4) for br in range(2) for g in range(2)]

        @block.sync
        def _(sp):
            def load(dst, src, s):
                sp.dma_start(dst, src).then_inc(s, 16)

            load(cT, io["cT"], S["c_loaded"])
            load(par[:, 0:80], io["par"], S["par_loaded"])
            load(par[:, 80:128], io["adab"], S["par_loaded"])
            load(ohd[0:33], io["ohd"], S["table_loaded"])
            load(oha[0:33], io["oha"], S["table_loaded"])
            load(rb[0:32], io["rel_bias"], S["table_loaded"])
            load(rbx[0:32].rearrange("p (b h) -> p b h", h=NH),
                 io["rel_bias"].rearrange("a (o h) -> a o h", o=1).to_broadcast([32, NB, NH]), S["table_loaded"])
            load(newmask[0:ROWS], io["newmask"], S["const_loaded"])
            load(gsum[0:ROWS], io["gsum"], S["const_loaded"])
            load(validq, io["validq"], S["const_loaded"])
            load(blkno[0:ROWS, 0:NSELB], io["blkno"], S["const_loaded"])
            for n in range(2):
                load(ada[:, n * KD:(n + 1) * KD, :], io["ada_w"][:, :, n * AW:(n + 1) * AW], ada_l[n])
            load(xT[:, :, :], io["xT"], S["x_loaded"])
            for n in range(2, AN):
                sp.wait_ge(S["ada_ready"], n - 1)
                load(ada[:, (n % 2) * KD:(n % 2 + 1) * KD, :], io["ada_w"][:, :, n * AW:(n + 1) * AW], ada_l[n % 2])
            for n in range(3):
                load(win_w[:, n * KD:(n + 1) * KD, :], io["w_in"][n], w_l[n])
            for n in range(3, ZC):
                sp.wait_ge(S["z_ready"], n - 2)
                load(win_w[:, (n % 3) * KD:(n % 3 + 1) * KD, :], io["w_in"][n], w_l[n % 3])
            sp.wait_ge(S["ada_ready"], AN)
            load(wgate, io["w_gate"], S["wgate_loaded"])
            load(stc, io["state_conv"], S["lrus_loaded"])
            load(h0T, io["state_h"], S["lrus_loaded"])
            sp.wait_ge(S["hi_ready"], 1)
            for e in range(2):
                load(wlru[e * HD:(e + 1) * HD, :, e * HD:(e + 1) * HD],
                     io["wlru"][e], S["lruw_loaded"])
            sp.wait_ge(S["z_moved"], ZC)
            load(io["o_kv"], zT[:, KC:ZC, :], S["kv_stored"])
            sp.wait_ge(S["lru_ready"], 1)
            load(io["o_h"], outh, S["lru_stored"])
            load(io["o_conv"], outc, S["lru_stored"])
            sp.wait_ge(S["lru_norm"], 1)
            load(ohw[0:33], io["ohw"], S["ohw_loaded"])
            sp.wait_ge(S["gates_ready"], 1)
            load(io["gscratch"].rearrange("(b h) r -> b (h r)", h=NH), gates[0:NB, 4, :], S["gate_stored"])
            sp.wait_ge(S["gate_stored"], 16)
            load(gate_rows[:, :], io["gscratch"], S["gate_moved"])
            sp.wait_ge(S["sel_free"], 1)
            load(kwin, io["win_kT"], S["win_loaded"])
            load(vwin, io["win_v"].rearrange("b (c p) f -> p (b c) f", p=P), S["win_loaded"])
            load(wout, io["w_out"], S["wout_loaded"])
            for b in range(NB):
                load(io["o_winv"][b, 0:511], io["win_v"][b, 1:512], S["out_stored"])
            load(io["o_wink"][:, :, 0:511], io["win_kT"][:, :, 1:512], S["out_stored"])
            sp.wait_ge(S["proj_done"], 1)
            load(sk, io["sk"], S["sk_loaded"])
            for n in range(3):
                load(wq[:, n * KD:(n + 1) * KD, :], io["wq"][n], wq_l[n])
            for n in range(3, 16):
                sp.wait_ge(S["q_ready"], n - 2)
                load(wq[:, (n % 3) * KD:(n % 3 + 1) * KD, :], io["wq"][n], wq_l[n % 3])
            for ch in range(5):
                sp.wait_ge(S["stage_full"], 26 * (ch + 1))
                sp.dma_start(gw[:, :, ch * TC:(ch + 1) * TC].rearrange("j i t -> i j t"),
                             stage[:, ch % 2, :].rearrange("p (j t) -> p j t", t=TC)).then_inc(st_l[ch % 2], 16)
            sp.wait_ge(st_l[0], 48)
            sp.wait_ge(st_l[1], 32)
            sp.wait_ge(S["g_ready"], 132)

            def load_gv(g, par_):
                load(gr[:, par_ * EXP_J:(par_ + 1) * EXP_J, :],
                     gw[bass.ds(g * EXP_J, EXP_J)].rearrange("j i t -> i j t"), g_l[par_])
                load(vr[:, par_ * EXP_J:(par_ + 1) * EXP_J, :],
                     io["v"][:, bass.ds(g * EXP_J, EXP_J), :], v_l[par_])

            def load_u(blk, slot):
                load(ur[:, slot * KD:(slot + 1) * KD, :], io["uT"][blk], u_l[slot])

            def load_group(g, par_):
                sp.wait_ge(S["a_ready"], (g - 1) * EXP_J + 1)
                sp.wait_ge(S["ff_ready"], (g - 1) * KD + 1)
                load_gv(g, par_)
                for jj in range(EXP_J):
                    sp.wait_ge(S["zz_ready"], g * EXP_J + jj - 3)
                    load_u(g * EXP_J + jj, jj % 4)

            load_gv(0, 0)
            for jj in range(EXP_J):
                if jj >= 4:
                    sp.wait_ge(S["zz_ready"], jj - 3)
                load_u(jj, jj % 4)
            with sp.Fori(0, GROUPS // 2 - 1) as it:
                load_group(it * 2 + 1, 1)
                load_group(it * 2 + 2, 0)
            load_group(GROUPS - 1, 1)
            sp.wait_ge(S["fin_ready"], 1)
            load(io["o_y"], h2T, S["out_stored"])
            sp.wait_ge(S["out_stored"], 16 * (NB + 2))

        @block.gpsimd
        def _(pool):
            def load(dst, src, s):
                pool.dma_start(dst, src).then_inc(s, 16)

            pool.memset(ident[:, :], 0.0).then_inc(S["pool_done"], 1)
            pool.memset(w2, 0.0).then_inc(S["pool_done"], 1)
            pool.memset(w1, 0.0).then_inc(S["pool_done"], 1)
            pool.wait_ge(S["pool_done"], 3)
            pool.affine_select(out=ident[:, :], in_=ident[:, :], compare_op=ALU.not_equal, fill=1.0,
                               base=0, pattern=[[-1, P]], channel_multiplier=1).then_inc(S["memset_done"], 1)
            for c in range(2):
                for g in range(2):
                    load(w2[g * HD:(g + 1) * HD, c, g * HD:(g + 1) * HD], io["cmp_w2"][c], S["w2_loaded"])

            def load_w1(c, s):
                for g in range(2):
                    load(w1[g * HD:(g + 1) * HD, :, g * HD:(g + 1) * HD], io["cmp_w1"][c], s)
            load_w1(0, S["w1k_loaded"])
            load(X[:, 8704:8736], io["posT"][0], S["pos_loaded"])
            pgi = small[:, 0:64].bitcast(mybir.dt.int32)
            pid = small[:, 64:65].bitcast(mybir.dt.int32)
            idx = small[:, 128:192].bitcast(mybir.dt.int32)
            pool.dma_start(pgi, io["page_table"].to_broadcast([P, NB * PAGES])).then_inc(S["page_loaded"], 16)
            pool.iota(pid, pattern=[[0, 1]], base=0, channel_multiplier=1).then_inc(S["pool_done"], 1)
            pool.wait_ge(S["page_loaded"], 16)
            pool.tensor_scalar(pgi, pgi, float(P), None, MUL).then_inc(S["pool_done"], 1)
            pool.wait_ge(S["pool_done"], 5)
            pool.tensor_tensor(idx, pgi, pid.to_broadcast([P, 64]), ADD).then_inc(S["pool_done"], 1)
            pool.wait_ge(S["pool_done"], 6)

            def gather(dst, src, w, s):
                for n in range(NB * PAGES):
                    pool.indirect_dma_start(
                        out=dst[:, n * w:(n + 1) * w], out_offset=None, in_=src,
                        in_offset=bass.IndirectOffsetOnAxis(ap=idx[:, n:n + 1].bitcast(U32), axis=0)).then_inc(s, 16)
            gather(X, io["pool_k"], P, S["gather_k"])
            pool.wait_ge(S["hid_ready"], 1)
            load_w1(1, S["w1v_loaded"])
            load(X[:, 8704:8736], io["posT"][1], S["pos2_loaded"])
            gather(X, io["pool_v"], P, S["gather_v"])
            pool.wait_ge(S["hid_ready"], 2)
            pool.wait_ge(S["lru_norm"], 1)
            pool.wait_ge(S["z_ready"], ZC)
            gather(at(13520, 16384), io["pool_s"], 256, S["gather_s"])
            pool.wait_ge(S["rs_copied"], 1)
            pool.wait_ge(S["mt_done"], AN)
            pool.dma_start(rscratch, rsb[0:NH]).then_inc(S["scratch_stored"], 16)
            pool.wait_ge(S["scratch_stored"], 16)
            rows = io["rrows"]
            pool.dma_start(rows.rearrange("p h c -> p (h c)"),
                           rscratch.rearrange("h (o c) -> o (h c)", o=1).to_broadcast([P, NH * 640])
                           ).then_inc(S["rows_stored"], 16)
            pool.wait_ge(S["rows_stored"], 16)
            pool.dma_start(biasT, bass.AP(rows.tensor, 127, [[NH * 640 - 1, P], [640, NH], [1, 512]])
                           ).then_inc(S["bias_loaded"], 16)
            pool.wait_ge(S["proj_done"], 1)
            pool.iota(iota, pattern=[[1, P]], base=0, channel_multiplier=0,
                      allow_small_or_imprecise_dtypes=True).then_inc(S["bias_ready"], 1)
            pool.iota(iota16, pattern=[[1, 16]], base=0, channel_multiplier=0,
                      allow_small_or_imprecise_dtypes=True).then_inc(S["bias_ready"], 1)

        @block.tensor
        def _(pe):
            mm = pe.matmul

            def two(b, lhs, rhs_k, ks):
                for n, k in enumerate(ks):
                    for h in range(2):
                        last = mm(ps[:, b + h, 0:HALF], lhs(k), rhs_k(k)[:, h * HALF:(h + 1) * HALF],
                                  start=(n == 0), stop=(n == len(ks) - 1))
                return last

            pe.wait_ge(S["table_loaded"], 64)
            pe.wait_ge(S["rb_ready"], 1)
            mm(ps[0:NH, 0, 0:512], rb[0:33], ohd[0:33, 513:1025], start=True, stop=True)
            mm(ps[0:NH, 1, 0:128], rb[0:33], ohd[0:33, 1025:1153], start=True, stop=True).then_inc(S["rs_ready"], 1)
            for i in range(4):
                for n in range(NCMP_P):
                    st = 511 + P * i - 16 * n - 31
                    last = mm(ps[:, 2 + i // 2, (i % 2) * 248 + n * NH:(i % 2) * 248 + (n + 1) * NH],
                              oha[0:33, st:st + P], rb[0:33], start=True, stop=True)
            last.then_inc(S["pb_ready"], 1)

            pe.wait_ge(S["silu_done"], 1)
            pe.wait_ge(S["memset_done"], 1)

            def turn_m9(n):
                pe.wait_ge(S["m9_ready"], n + 1)
                if n >= 2:
                    pe.wait_ge(S["mt_done"], n - 1)
                for q in range(AW // P):
                    last = pe.transpose(ps[:, 6 + n % 2, q * 9:(q + 1) * 9], m9[0:9, n % 2, q * P:(q + 1) * P],
                                        ident[0:9, 0:9])
                last.then_inc(S["mt_ready"], 1)
            for n in range(AN):
                pe.wait_ge(ada_l[n % 2], 16 * (n // 2 + 1))
                if n >= 2:
                    pe.wait_ge(S["m9_ready"], n - 1)
                for k in range(KD):
                    last = mm(ps[0:9, 4 + n % 2, 0:AW], cT[:, k, :], ada[:, (n % 2) * KD + k, :],
                              start=(k == 0), stop=(k == KD - 1))
                last.then_inc(S["ada_ready"], 1)
                if n >= 1:
                    turn_m9(n - 1)
            turn_m9(AN - 1)

            pe.wait_ge(S["sq_done"], 1)
            pe.wait_ge(S["rs_copied"], 1)
            two(0, lambda k: ones[:, :], lambda k: hT[:, k, :], range(KD)).then_inc(S["sum_ready"], 1)

            pe.wait_ge(S["h_ready"], 1)
            for n in range(ZC):
                pe.wait_ge(w_l[n % 3], 16 * (n // 3 + 1))
                if n >= 3:
                    pe.wait_ge(S["z_moved"], n - 2)
                two(2 * (n % 3), lambda k: win_w[:, (n % 3) * KD + k, :], lambda k: hT[:, k, :],
                    range(KD)).then_inc(S["z_ready"], 1)
            pe.wait_ge(S["wgate_loaded"], 16)
            for t in range(5):
                m = P if t < 4 else NB
                for k in range(KD):
                    last = mm(ps[0:m, 6, t * 24:(t + 1) * 24], hT[:, k, t * P:t * P + m], wgate[:, k, :],
                              start=(k == 0), stop=(k == KD - 1))
            last.then_inc(S["zg_ready"], 1)

            pe.wait_ge(S["lruw_loaded"], 32)
            pe.wait_ge(S["z_moved"], ZC)
            for c in range(4):
                pe.wait_ge(S["xc_ready"], c + 1)
                if c >= 2:
                    pe.wait_ge(S["ri_ready"], c - 1)
                b = 4 * (c % 2)
                if b == 4:
                    pe.wait_ge(S["gates_ready"], 1)
                for w in range(2):
                    last = two(b + 2 * w, lambda k: wlru[:, 4 * w + c, :], lambda k: xcT[:, c, :], [0])
                last.then_inc(S["gate_ready"], 1)
            pe.wait_ge(S["ri_ready"], 4)

            for c in range(2):
                if c == 0:
                    pe.wait_ge(S["w1k_loaded"], 32)
                    pe.wait_ge(S["pos_loaded"], 16)
                    pe.wait_ge(S["gather_k"], 16 * NB * PAGES)
                else:
                    pe.wait_ge(S["w1v_loaded"], 32)
                    pe.wait_ge(S["pos2_loaded"], 16)
                    pe.wait_ge(S["gather_v"], 16 * NB * PAGES)
                pe.wait_ge(S["x_filled"], c + 1)
                xv = X.rearrange("p (n s) -> p n s", s=16)
                for h, (c0, n) in enumerate(((0, 273), (273, 272))):
                    for ms in range(32):
                        m, s = ms // 16, ms % 16
                        last = mm(ps[:, h, 0:n], w1[:, ms, :], xv[:, c0 + m:c0 + m + n, s],
                                  start=(ms == 0), stop=(ms == 31))
                last.then_inc(S["hid_ready"], 1)
                pe.wait_ge(S["gelu_ready"], c + 1)
                pe.wait_ge(S["w2_loaded"], 64)
                if c == 0:
                    for h in range(2):
                        last = mm(ps[:, 2 + h, 0:272], w2[:, 0, :], hid[:, h * 272:(h + 1) * 272],
                                  start=True, stop=True)
                    last.then_inc(S["ck_ready"], 1)
                else:
                    for b in range(9):
                        m = NCMP_S if b < 8 else NCMP_P
                        last = mm(ps[0:m, 4 + b // 4, (b % 4) * P:(b % 4 + 1) * P], hid[:, b * 64:b * 64 + m],
                                  w2[:, 1, :], start=True, stop=True)
                    last.then_inc(S["ck_ready"], 1)

            pe.wait_ge(S["lru_ready"], 1)
            two(2, lambda k: ones[:, :], lambda k: aT[:, k, :], range(4)).then_inc(S["mix_sum"], 1)

            for br in range(2):
                for kb in range(4):
                    pe.transpose(ps[:, br, kb * P:(kb + 1) * P], zT[:, (VS, VW)[br], kb * P:(kb + 1) * P], ident[:, :])
            pe.wait_ge(S["cmp_done"], 1)
            for br in range(2):
                last = pe.transpose(ps[0:NB, 6, 64 + br * P:64 + (br + 1) * P], zT[:, (VS, VW)[br], SEQ:TOK], ident[:, :])
            last.then_inc(S["vt_ready"], 1)

            pe.wait_ge(S["vt_done"], 1)
            pe.wait_ge(S["qpad_ready"], 1)
            for b in range(NB):
                mm(ps[0:ROWS, 7, 0:NCMP_S], qpad[:, b, :], ckT[:, b * 64:b * 64 + NCMP_S], start=(b == 0), stop=False)
            mm(ps[0:ROWS, 7, 0:NCMP_S], rbx[0:33], ohd[0:33, 31:31 + 16 * (NCMP_S - 1) + 1:16],
               start=False, stop=True).then_inc(S["sc_ready"], 1)
            pe.wait_ge(S["gather_s"], 16 * NB * PAGES)
            for h in range(2):
                for b in range(NB):
                    mm(ps[0:ROWS, h, 0:512], qpad[:, b, :], sel[:, b * 8 + h * 4:b * 8 + h * 4 + 4, 0:P],
                       start=(b == 0), stop=False)
                mm(ps[0:ROWS, h, 0:512], rbx[0:33], ohd[0:33, h * 512:(h + 1) * 512], start=False, stop=True)
            mm(ps[0:ROWS, 2, 0:NB], qs, zT[:, KS, SEQ:TOK], start=True, stop=False)
            mm(ps[0:ROWS, 2, 0:NB], rbx[0:33], ohd[0:33, 1153:1161], start=False, stop=True).then_inc(S["ss_ready"], 1)
            pe.wait_ge(S["sc_soft"], 1)
            mm(ps[0:ROWS, 5, 0:NCMP_S], gsum[0:ROWS], gs[0:ROWS, 0:NCMP_S], start=True, stop=True).then_inc(S["sum_done"], 1)
            pe.wait_ge(S["ss_p"], 1)
            pe.transpose(ps[0:NCMP_S, 3, 0:ROWS], sc[0:ROWS, 0:NCMP_S], ident[0:ROWS, 0:ROWS])
            pe.transpose(ps[0:NB, 3, ROWS:2 * ROWS], ss[0:ROWS, 1024:1032], ident[0:ROWS, 0:ROWS])
            for kb in range(8):
                last = pe.transpose(ps[:, 4, kb * ROWS:(kb + 1) * ROWS], ss[0:ROWS, kb * P:(kb + 1) * P], ident[0:ROWS, 0:ROWS])
            last.then_inc(S["pts_ready"], 1)
            pe.wait_ge(S["pts_done"], 1)
            for b in range(NB):
                r = slice(b * NH, (b + 1) * NH)
                mm(ps[:, 6, r], vc[0:NCMP_S, b, :], pts[0:NCMP_S, 0, r], start=True, stop=False)
                mm(ps[:, 6, r], vnew[0:NB, 0, :], pts[0:NB, 1, r], start=False, stop=False)
                for kb in range(8):
                    last = mm(ps[:, 6, r], sel[:, b * 8 + kb, P:2 * P], pts[:, 2 + kb, r], start=False, stop=(kb == 7))
            last.then_inc(S["sel_free"], 1)
            pe.wait_ge(S["win_loaded"], 32)
            pe.wait_ge(S["ohw_loaded"], 16)
            for b in range(NB):
                mm(ps[0:ROWS, 0, 0:512], qpad[:, b, :], kwin[:, b, :], start=(b == 0), stop=False)
            mm(ps[0:ROWS, 0, 0:512], rbx[0:33], ohw[0:33], start=False, stop=True)
            mm(ps[0:ROWS, 1, 0:NB], qs, zT[:, KW, SEQ:TOK], start=True, stop=False)
            mm(ps[0:ROWS, 1, 0:NB], rbx[0:33], ohd[0:33, 1153:1161], start=False, stop=True).then_inc(S["sw_ready"], 1)
            pe.wait_ge(S["sw_p"], 1)
            pe.transpose(ps[0:NB, 2, 0:ROWS], sw[0:ROWS, 512:520], ident[0:ROWS, 0:ROWS])
            for kb in range(4):
                last = pe.transpose(ps[:, 3, kb * ROWS:(kb + 1) * ROWS], sw[0:ROWS, kb * P:(kb + 1) * P], ident[0:ROWS, 0:ROWS])
            last.then_inc(S["ptw_ready"], 1)
            pe.wait_ge(S["ptw_done"], 1)
            for b in range(NB):
                r = slice(b * NH, (b + 1) * NH)
                mm(ps[:, 7, r], vnew[0:NB, 1, :], pts[0:NB, 10, r], start=True, stop=False)
                for kb in range(4):
                    last = mm(ps[:, 7, r], vwin[:, b * 4 + kb, :], pts[:, 11 + kb, r], start=False, stop=(kb == 3))
            last.then_inc(S["os_ready"], 1)
            pe.wait_ge(S["os_done"], 1)

            def scores(u):
                i, br, g = units[u]
                nk = (i + 1) * P
                for r in range(GRP):
                    if u >= 1:
                        pe.wait_ge(S["u_ttr"], GRP * (u - 1) + r + 1)
                    mm(ps[:, r, 0:nk], qz[:, g * GRP + r, i * P:(i + 1) * P], zT[:, (KS, KW)[br], 0:nk],
                       start=True, stop=True).then_inc(S["u_s"], 1)

            def compressed(i):
                u = 4 * i
                if u >= 1:
                    pe.wait_ge(S["u_ttr"], GRP * u)
                for h in range(NH):
                    last = mm(ps[:, 0, h * NCMP_P:(h + 1) * NCMP_P], qz[:, h, i * P:(i + 1) * P],
                              ckT[:, 512:512 + NCMP_P], start=True, stop=True)
                last.then_inc(S["pc_s"], 1)
                pe.wait_ge(S["pc_p"], i + 1)
                if u >= 1:
                    pe.wait_ge(S["u_tdone"], sum(units[v][0] + 1 for v in range(u)))
                for h in range(NH):
                    last = pe.transpose(ps[0:NCMP_P, 4 + h // 4, (h % 4) * P:(h % 4 + 1) * P],
                                        pcb[:, h * NCMP_P:(h + 1) * NCMP_P], ident[:, :])
                last.then_inc(S["pc_t"], 1)
                pe.wait_ge(S["pc_tdone"], i + 1)
                if i:
                    pe.wait_ge(S["o_done"], i)
                for g in range(2):
                    mm(ps[:, 6 + g, 0:512], vc[0:NCMP_P, 8, :], ptcb[0:NCMP_P, g * 512:(g + 1) * 512],
                       start=True, stop=False)

            tcount = [0]

            def apply(u):
                i, br, g = units[u]
                pe.wait_ge(S["u_p"], GRP * (u + 1))
                for kb in range(i + 1):
                    n = tcount[0]
                    if n >= 2:
                        pe.wait_ge(S["u_tdone"], n - 1)
                    for r in range(GRP):
                        last = pe.transpose(ps[:, 4 + n % 2, r * P:(r + 1) * P],
                                            pbuf[:, (u % 2) * GRP + r, kb * P:(kb + 1) * P], ident[:, :])
                    last.then_inc(S["u_t"], 1)
                    tcount[0] += 1
                for kb in range(i + 1):
                    pe.wait_ge(S["u_tdone"], tcount[0] - i + kb)
                    last = mm(ps[:, 6 + g, 0:512], vn[:, br * 4 + kb, :], ptb[:, kb, :],
                              start=False, stop=(br == 1 and kb == i))
                last.then_inc(S["u_pv"], 1)

            for i in range(4):
                compressed(i)
                scores(4 * i)
                for q in range(4):
                    u = 4 * i + q
                    if q < 3:
                        scores(u + 1)
                    apply(u)

            pe.wait_ge(S["mix_sq"], 1)
            two(0, lambda k: ones[:, :], lambda k: hT[:, k, :], range(4)).then_inc(S["mix_sum"], 1)
            pe.wait_ge(S["mix_ready"], 1)
            pe.wait_ge(S["wout_loaded"], 16)
            for c in range(KD):
                if c >= 3:
                    pe.wait_ge(S["proj_ready"], c - 2)
                two(2 + 2 * (c % 3), lambda k: wout[:, k, c * P:(c + 1) * P], lambda k: zT[:, k, :],
                    range(KD)).then_inc(S["pe_step"], 1)
            pe.wait_ge(S["sq_done"], 2)
            two(0, lambda k: ones[:, :], lambda k: h2T[:, k, :], range(KD)).then_inc(S["sum_ready"], 1)

            pe.wait_ge(S["h_ready"], 2)
            pe.wait_ge(S["sk_loaded"], 16)

            def sub_scores(n):
                pe.wait_ge(S["q_moved"], n + 1)
                if n >= 2:
                    pe.wait_ge(S["s_free"], n - 1)
                b = 4 + 2 * (n % 2)
                for t in range(5):
                    m = P if t < 4 else NB
                    last = mm(ps[0:m, b + t // 4, (t % 4) * P:(t % 4 + 1) * P], qT[:, n % 2, t * P:t * P + m],
                              sk[:, n, :], start=True, stop=True)
                last.then_inc(S["s_ready"], 1)
            for n in range(16):
                pe.wait_ge(wq_l[n % 3], 16 * (n // 3 + 1))
                if n >= 2:
                    pe.wait_ge(S["q_moved"], n - 1)
                two(2 * (n % 2), lambda k: wq[:, (n % 3) * KD + k, :], lambda k: h2T[:, k, :],
                    range(KD)).then_inc(S["q_ready"], 1)
                if n >= 1:
                    sub_scores(n - 1)
            sub_scores(15)
            for t in range(5):
                m = P if t < 4 else NB
                pe.wait_ge(S["tr_in"], t + 1)
                for q in range(3):
                    last = pe.transpose(ps[:, q, 0:m], isel[0:m, q, :], ident[0:m, 0:m])
                last.then_inc(S["tr_ready"], 1)

            pe.wait_ge(S["tr_done"], 5)
            pe.sem_inc(S["g_ready"], 2)
            for ch in range(5):
                with pe.Fori(0, TC // 8) as it:
                    for q in range(2):
                        n = it * 2 + (26 * ch + q)
                        pe.wait_ge(S["oh_ready"], n + 1)
                        pe.wait_ge(S["g_moved"], n + 1)
                        for t in range(4):
                            last = mm(ps[:, q, t * P:(t + 1) * P], oh[:, q * 4 + t, 0:P], oh[:, q * 4 + t, P:2 * P],
                                      start=True, stop=True)
                        last.then_inc(S["g_ready"], 1)

            def up(g, par_, peeled=False):
                for jj in range(EXP_J):
                    pe.wait_ge(u_l[jj % 4], upcount(g, par_, jj) * 16)
                    if not (peeled and jj < 2):
                        pe.wait_ge(S["gelu_done"], g * EXP_J + jj - 1)
                    two(2 * (jj % 2), lambda k: ur[:, (jj % 4) * KD + k, :], lambda k: h2T[:, k, :],
                        range(KD)).then_inc(S["zz_ready"], 1)

            def upcount(g, par_, jj):
                return g * 2 + (jj // 4 + 1)

            def down(g, par_, vcount):
                pe.wait_ge(v_l[par_], vcount * 16)
                pe.wait_ge(S["a_ready"], (g + 1) * EXP_J)
                for dc in range(KD):
                    pe.wait_ge(S["ff_free"], g * KD + dc + 1)
                    two(4 + 2 * (dc % 2), lambda j: vr[:, par_ * EXP_J + j, dc * P:(dc + 1) * P],
                        lambda j: av[:, par_ * EXP_J + j, :], range(EXP_J)).then_inc(S["ff_ready"], 1)

            pe.wait_ge(S["g_moved"], 132)
            pe.sem_inc(S["ff_ready"], 1)
            up(0, 0, peeled=True)
            with pe.Fori(0, GROUPS // 2 - 1) as it:
                up(it * 2 + 1, 1)
                down(it * 2, 0, it + 1)
                up(it * 2 + 2, 0)
                down(it * 2 + 1, 1, it + 1)
            up(GROUPS - 1, 1)
            down(GROUPS - 2, 0, GROUPS // 2)
            down(GROUPS - 1, 1, GROUPS // 2)
            pe.wait_ge(S["sq_done"], 3)
            two(0, lambda k: ones[:, :], lambda k: sq[:, k, :], range(KD)).then_inc(S["sum_ready"], 1)

        @block.scalar
        def _(act):
            steps = [0]

            def link(ins):
                steps[0] += 1
                ins.then_inc(S["act_step"], 1)
                act.wait_ge(S["act_step"], steps[0])

            def fn(out, in_, f, **kw):
                return act.activation(out, in_, f, **kw)

            act.wait_ge(S["c_loaded"], 16)
            fn(cT, cT, ACT.Silu).then_inc(S["silu_done"], 1)
            act.wait_ge(S["rs_ready"], 1)
            act.wait_ge(S["silu_done"], 1)
            link(fn(rsb[0:NH, 0:512], ps[0:NH, 0, 0:512], ACT.Copy))
            fn(rsb[0:NH, 512:640], ps[0:NH, 1, 0:128], ACT.Copy).then_inc(S["rs_copied"], 1)
            for n in range(AN):
                act.wait_ge(S["ada_ready"], n + 1)
                if n >= 2:
                    act.wait_ge(S["mt_ready"], n - 1)
                fn(m9[0:9, n % 2, :], ps[0:9, 4 + n % 2, 0:AW], ACT.Copy).then_inc(S["m9_ready"], 1)
                if n == 1:
                    act.wait_ge(S["x_loaded"], 16)
                    fn(hT, xT[:, :, :], ACT.Square).then_inc(S["sq_done"], 1)

            def root(n):
                act.wait_ge(S["root_in"], n)
                fn(rstd, rstd, ACT.Sqrt).then_inc(S["rstd_ready"], 1)
            root(1)
            for n in range(1, ZC, 2):
                act.wait_ge(S["z_ready"], n + 1)
                act.wait_ge(S["z_moved"], n)
                b = 2 * (n % 3)
                fn(zT[:, n, :].rearrange("p (h t) -> p h t", h=2), ps[:, b:b + 2, 0:HALF], ACT.Copy,
                   scale=0.125 if QC <= n < QC + 4 else 1.0).then_inc(S["z_moved"], 1)
            act.wait_ge(S["zg_ready"], 1)
            link(fn(gates[:, 0:4, :], ps[:, 6, 0:96].rearrange("p (t c) -> p t c", c=24), ACT.Sigmoid))
            fn(gates[0:NB, 4, :].rearrange("p (h r) -> p h r", r=3),
               ps[0:NB, 6, 96:120].rearrange("p (r h) -> p h r", h=NH), ACT.Sigmoid).then_inc(S["gates_ready"], 1)
            for c in range(4):
                act.wait_ge(S["gate_ready"], c + 1)
                b = 4 * (c % 2)
                link(fn(rT[:, c, :].rearrange("p (h t) -> p h t", h=2), ps[:, b:b + 2, 0:HALF], ACT.Sigmoid,
                        bias=par[:, BA + c:BA + c + 1]))
                fn(iT_[:, c, :].rearrange("p (h t) -> p h t", h=2), ps[:, b + 2:b + 4, 0:HALF], ACT.Sigmoid,
                   bias=par[:, BI + c:BI + c + 1]).then_inc(S["ri_ready"], 1)
            act.wait_ge(S["lru_prep"], 1)
            fn(lr(1), lr(0), ACT.Exp, scale=-1.0).then_inc(S["exp_ready"], 1)
            act.wait_ge(S["lru_prep"], 2)
            fn(lr(3), lr(2), ACT.Ln).then_inc(S["exp_ready"], 1)
            act.wait_ge(S["lru_prep"], 3)
            act.wait_ge(S["ri_ready"], 4)
            for c in range(4):
                link(fn(aT[:, c, :], rT[:, c, :], ACT.Exp, scale=lr(9)[:, c:c + 1]))
                link(fn(rT[:, c, :], rT[:, c, :], ACT.Tanh, scale=lr(8)[:, c:c + 1]))
            act.sem_inc(S["exp_ready"], 1)
            act.wait_ge(S["z_moved"], ZC)
            fn(zT[:, YG:YG + 4, :], zT[:, YG:YG + 4, :], ACT.Gelu_apprx_tanh).then_inc(S["yg_ready"], 1)
            act.wait_ge(S["lru_prep"], 4)
            fn(rT, rT, ACT.Sqrt).then_inc(S["exp_ready"], 1)
            for c in range(2):
                act.wait_ge(S["hid_ready"], c + 1)
                link(fn(posb[:, :], ps[:, 1, 271:272], ACT.Copy))
                if c == 1:
                    act.wait_ge(S["ck_ready"], 1)
                link(fn(hid[:, 0:273], ps[:, 0, 0:273], ACT.Gelu_apprx_tanh, bias=posb[:, :]))
                fn(hid[:, 273:545], ps[:, 1, 0:272], ACT.Gelu_apprx_tanh, bias=posb[:, :]).then_inc(S["gelu_ready"], 1)
                act.wait_ge(S["ck_ready"], c + 1)
                if c == 0:
                    link(fn(ckT.rearrange("p (h t) -> p h t", h=2), ps[:, 2:4, 0:272], ACT.Copy))
                else:
                    for q in range(2):
                        link(fn(vc[0:NCMP_S, 4 * q:4 * q + 4, :].rearrange("p a b -> p (a b)"), ps[0:NCMP_S, 4 + q, 0:512], ACT.Copy))
                    fn(vc[0:NCMP_P, 8, :], ps[0:NCMP_P, 6, 0:P], ACT.Copy).then_inc(S["cmp_done"], 1)
            act.wait_ge(S["lru_ready"], 1)
            root(2)
            act.wait_ge(S["sc_exp"], 1)
            fn(sc[0:ROWS, 0:NCMP_S], sc[0:ROWS, 0:NCMP_S], ACT.Exp, bias=sm(0), accum_out=sm(1)).then_inc(S["sc_exp"], 1)
            act.wait_ge(S["ss_max"], 1)
            fn(ss[0:ROWS], ss[0:ROWS], ACT.Exp, bias=sm(4), accum_out=sm(5)).then_inc(S["ss_exp"], 1)
            act.wait_ge(S["sw_max"], 1)
            fn(sw[0:ROWS], sw[0:ROWS], ACT.Exp, bias=sm(8), accum_out=sm(9)).then_inc(S["sw_exp"], 1)
            for u, (i, br, g) in enumerate(units):
                if u % 4 == 0:
                    act.wait_ge(S["pc_max"], i + 1)
                    fn(pcb, pcb, ACT.Exp).then_inc(S["pc_exp"], 1)
                nk = (i + 1) * P
                act.wait_ge(S["u_max"], u + 1)
                for r in range(GRP):
                    fn(pbuf[:, (u % 2) * GRP + r, 0:nk], pbuf[:, (u % 2) * GRP + r, 0:nk], ACT.Exp,
                       bias=pst(u, 1)[:, r:r + 1], accum_out=pst(u, 2)[:, r:r + 1]).then_inc(S["u_exp"], 1)
                act.wait_ge(S["u_exp"], GRP * (u + 1))
                act.wait_ge(S["u_rs"], u + 1)
                for r in range(GRP):
                    fn(pbuf[:, (u % 2) * GRP + r, 0:nk], pbuf[:, (u % 2) * GRP + r, 0:nk], ACT.Copy,
                       scale=pst(u, 3)[:, r:r + 1]).then_inc(S["u_p"], 1)
            act.wait_ge(S["o_done"], 4)
            fn(hT[:, 0:4, :], zT[:, 4:8, :], ACT.Square).then_inc(S["mix_sq"], 1)
            root(3)
            act.wait_ge(S["proj_done"], 1)
            fn(h2T, xT[:, :, :], ACT.Square).then_inc(S["sq_done"], 1)
            root(4)
            for n in range(16):
                act.wait_ge(S["q_ready"], n + 1)
                if n >= 2:
                    act.wait_ge(S["s_ready"], n - 1)
                fn(qT[:, n % 2, :].rearrange("p (h t) -> p h t", h=2), ps[:, 2 * (n % 2):2 * (n % 2) + 2, 0:HALF],
                   ACT.Identity, bias=par[:, BQ + n:BQ + n + 1]).then_inc(S["q_moved"], 1)
            for t in range(5):
                m = P if t < 4 else NB
                act.wait_ge(S["rexp"], t + 1)
                fn(best[0:m], best[0:m], ACT.Exp).then_inc(S["rexp_done"], 1)
            act.wait_ge(S["tr_done"], 5)
            act.sem_inc(S["g_moved"], 2)
            for ch in range(5):
                if ch >= 2:
                    act.wait_ge(st_l[ch % 2], 16 * (ch // 2))
                with act.Fori(0, TC // 8) as it:
                    for q in range(2):
                        n = it * 2 + (26 * ch + q)
                        act.wait_ge(S["g_ready"], n + 3)
                        fn(stage[:, ch % 2, :].rearrange("p (j t) -> p j t", t=TC)[:, :, bass.ds(it * 8 + 4 * q, 4)],
                           ps[:, q, 0:512].rearrange("p (t j) -> p j t", j=P), ACT.Copy).then_inc(S["g_moved"], 1)
                        act.wait_ge(S["g_moved"], n + 3)
                        act.sem_inc(S["stage_full"], 1)

            def gelu(g, par_):
                for jj in range(EXP_J):
                    act.wait_ge(S["zz_ready"], g * EXP_J + jj + 1)
                    if jj == 0 and not isinstance(g, int):
                        act.wait_ge(S["ff_ready"], (g - 1) * KD + 1)
                    elif jj == 0 and g > 1:
                        act.wait_ge(S["ff_ready"], (g - 1) * KD + 1)
                    fn(av[:, par_ * EXP_J + jj, :].rearrange("p (h t) -> p h t", h=2),
                       ps[:, 2 * (jj % 2):2 * (jj % 2) + 2, 0:HALF], ACT.Gelu_apprx_tanh).then_inc(S["gelu_done"], 1)
            act.wait_ge(st_l[0], 48)
            act.wait_ge(st_l[1], 32)
            gelu(0, 0)
            with act.Fori(0, GROUPS // 2 - 1) as it:
                gelu(it * 2 + 1, 1)
                gelu(it * 2 + 2, 0)
            gelu(GROUPS - 1, 1)
            root(5)

        @block.vector
        def _(dve):
            steps = [0]

            def link(*group):
                for ins in group:
                    steps[0] += 1
                    ins.then_inc(S["dve_step"], 1)
                dve.wait_ge(S["dve_step"], steps[0])

            tt, ts, cp = dve.tensor_tensor, dve.tensor_scalar, dve.tensor_copy
            stt = dve.scalar_tensor_tensor

            link(dve.memset(ones[:, :], 1.0))
            dve.wait_ge(S["table_loaded"], 64)
            link(dve.memset(rb[32:33], NEG), dve.memset(rbx[32:33], NEG))
            dve.sem_inc(S["rb_ready"], 1)
            dve.wait_ge(S["pb_ready"], 1)
            for q in range(2):
                link(cp(pbias[:, 2 * q:2 * q + 2, :].rearrange("p i (h n) -> p i h n", h=NH),
                        ps[:, 2 + q, 0:496].rearrange("p (i n h) -> p i h n", i=2, h=NH)))
            dve.wait_ge(S["par_loaded"], 32)
            for n in range(AN):
                dve.wait_ge(S["mt_ready"], n + 1)
                tt(mT[:, 3 * n:3 * n + 3, :], ps[:, 6 + n % 2, 0:27].rearrange("p (q c) -> p q c", c=9),
                   par[:, ADB + 3 * n:ADB + 3 * n + 3].to_broadcast([P, 3, 9]), ADD).then_inc(S["mt_done"], 1)
            dve.wait_ge(S["mt_done"], AN)
            for part, gain in ((1, N1G), (4, N2G)):
                v = mT[:, 8 * part:8 * part + 8, :]
                link(ts(v, v, 1.0, None, ADD))
                link(tt(v, v, par[:, gain:gain + 8].to_broadcast([P, 8, 9]), MUL))

            def inverse_ms(width, b):
                r = rstd.rearrange("p (h t) -> p h t", h=2)
                link(ts(r, ps[:, b:b + 2, 0:HALF], 1.0 / width, EPS, MUL, ADD))
                dve.reciprocal(rstd, rstd).then_inc(S["root_in"], 1)

            def modulate(dst, n, part_shift):
                dve.wait_ge(S["sum_ready"], n)
                inverse_ms(D, 0)
                dve.wait_ge(S["rstd_ready"], n if n == 1 else n + 2)
                link(tt(dst, xT[:, :, :], rstd.rearrange("p (o t) -> p o t", o=1).to_broadcast([P, KD, TOK]), MUL))
                sh, scl = mT[:, 8 * part_shift:8 * part_shift + 8, :], mT[:, 8 * part_shift + 8:8 * part_shift + 16, :]
                link(tt(dst[:, :, SEQ:TOK], dst[:, :, SEQ:TOK], scl[:, :, 1:9], MUL))
                link(tt(dst[:, :, SEQ:TOK], dst[:, :, SEQ:TOK], sh[:, :, 1:9], ADD))
                link(*[ts(dst[:, k, 0:SEQ], dst[:, k, 0:SEQ], scl[:, k, 0:1], sh[:, k, 0:1], MUL, ADD)
                       for k in range(KD)])
                dve.sem_inc(S["h_ready"], 1)
            modulate(hT, 1, 0)
            for n in range(0, ZC, 2):
                dve.wait_ge(S["z_ready"], n + 1)
                if n:
                    dve.wait_ge(S["z_moved"], n)
                b = 2 * (n % 3)
                ts(zT[:, n, :].rearrange("p (h t) -> p h t", h=2), ps[:, b:b + 2, 0:HALF],
                   0.125 if QC <= n < QC + 4 else 1.0, None, MUL).then_inc(S["z_moved"], 1)
            dve.wait_ge(S["z_moved"], ZC)
            link(dve.memset(wlru, 0.0))
            dve.sem_inc(S["hi_ready"], 1)
            cp(X[:, 8192:8704], zT[:, KC, 0:SEQ]).then_inc(S["x_filled"], 1)

            dve.wait_ge(S["lrus_loaded"], 32)

            def cw(k, c):
                return par[:, CW + 4 * k + c:CW + 4 * k + c + 1]
            for c in range(4):
                x = zT[:, XR + c, :]
                link(ts(xcT[:, c, :], x, cw(3, c), par[:, CB + c:CB + c + 1], MUL, ADD))
                for k in (2, 1, 0):
                    s = 3 - k
                    link(stt(xcT[:, c, s:SEQ], x[:, 0:SEQ - s], cw(k, c), xcT[:, c, s:SEQ], MUL, ADD),
                         stt(xcT[:, c, SEQ:TOK], stc[:, c, k * NB:(k + 1) * NB], cw(k, c), xcT[:, c, SEQ:TOK], MUL, ADD))
                dve.sem_inc(S["xc_ready"], 1)
            oc = outc.rearrange("p c (k s) -> p c k s", s=9)
            link(cp(oc[:, :, :, 0], zT[:, XR:XR + 4, SEQ - 3:SEQ]),
                 cp(oc[:, :, 0:2, 1:9], stc.rearrange("p c (k s) -> p c k s", s=NB)[:, :, 1:3, :]),
                 cp(oc[:, :, 2, 1:9], zT[:, XR:XR + 4, SEQ:TOK]))
            lam = par[:, LAM:LAM + 4]
            link(ts(lr(0), lam, -1.0, None, MUL))
            link(tt(lr(0), lr(0), lam, MAX))
            dve.sem_inc(S["lru_prep"], 1)
            dve.wait_ge(S["exp_ready"], 1)
            link(ts(lr(2), lr(1), 1.0, None, ADD))
            dve.sem_inc(S["lru_prep"], 1)
            link(ts(lr(4), lr(2), 1.0, None, SUB))
            link(ts(lr(5), lr(4), 0.0, None, EQ))
            link(tt(lr(4), lr(4), lr(5), ADD))
            link(dve.reciprocal(lr(4), lr(4)))
            link(tt(lr(4), lr(4), lr(1), MUL))
            link(tt(lr(5), lr(5), lr(1), MUL))
            dve.wait_ge(S["exp_ready"], 2)
            link(tt(lr(3), lr(3), lr(4), MUL))
            link(tt(lr(3), lr(3), lr(5), ADD))
            link(ts(lr(6), lam, -1.0, 0.0, MUL, MAX))
            link(tt(lr(3), lr(3), lr(6), ADD))
            link(ts(lr(8), lr(3), 8.0, None, MUL), ts(lr(9), lr(3), -8.0, None, MUL))
            dve.sem_inc(S["lru_prep"], 1)
            dve.wait_ge(S["exp_ready"], 3)
            link(ts(uT, rT, 1.0, None, ADD))
            link(dve.reciprocal(uT, uT))
            link(stt(rT, rT, 2.0, uT, MUL, MUL))
            dve.sem_inc(S["lru_prep"], 1)
            link(tt(iT_, iT_, xcT, MUL))
            dve.wait_ge(S["exp_ready"], 4)
            link(tt(uT, rT, iT_, MUL))
            link(*[dve.tensor_tensor_scan(xcT[:, c, 0:SEQ], aT[:, c, 0:SEQ], uT[:, c, 0:SEQ], 0.0, MUL, ADD)
                   for c in range(4)])
            link(tt(xcT[:, :, SEQ:TOK], aT[:, :, SEQ:TOK], h0T, MUL))
            link(tt(xcT[:, :, SEQ:TOK], xcT[:, :, SEQ:TOK], uT[:, :, SEQ:TOK], ADD))
            link(cp(outh, xcT[:, :, SEQ - 1:TOK]))
            dve.wait_ge(S["yg_ready"], 1)
            link(tt(zT[:, 0:4, :], xcT, zT[:, YG:YG + 4, :], MUL))
            link(tt(aT, zT[:, 0:4, :], zT[:, 0:4, :], MUL))
            dve.sem_inc(S["lru_ready"], 1)
            dve.wait_ge(S["hid_ready"], 1)
            cp(X[:, 8192:8704], zT[:, VC_, 0:SEQ]).then_inc(S["x_filled"], 1)
            dve.wait_ge(S["mix_sum"], 1)
            inverse_ms(512, 2)
            dve.wait_ge(S["rstd_ready"], 2)
            link(*[stt(zT[:, c, :], zT[:, c, :], par[:, NLG + c:NLG + c + 1], rstd, MUL, MUL) for c in range(4)])
            dve.wait_ge(S["lru_stored"], 32)
            dve.sem_inc(S["lru_norm"], 1)

            dve.wait_ge(S["x_filled"], 2)
            dve.wait_ge(S["hid_ready"], 2)
            link(dve.memset(qz, 0.0), dve.memset(qpad, 0.0), dve.memset(qs, 0.0))
            qpf = qpad.rearrange("p b r -> p (b r)")
            grp = []
            for g in range(2):
                rows = slice(g * HD, (g + 1) * HD)
                for r in range(GRP):
                    c = g * GRP + r
                    grp.append(cp(qz[rows, c, :], zT[rows, QC + r, 0:SEQ]))
                    grp.append(cp(qs[rows, c:ROWS:NH], zT[rows, QC + r, SEQ:TOK]))
                    grp.append(cp(qpf[rows, c:NB * ROWS:ROWS + NH], zT[rows, QC + r, SEQ:TOK]))
            link(*grp)
            dve.sem_inc(S["qpad_ready"], 1)
            dve.wait_ge(S["vt_ready"], 1)
            grp = []
            for br in range(2):
                grp.append(cp(vn[:, br * 4:(br + 1) * 4, :].rearrange("p k c -> p (k c)"), ps[:, br, 0:512]))
            grp.append(cp(vnew[0:NB].rearrange("p a b -> p (a b)"), ps[0:NB, 6, 64:64 + 2 * P]))
            link(*grp)
            dve.sem_inc(S["vt_done"], 1)

            R = slice(0, ROWS)
            dve.wait_ge(S["const_loaded"], 64)
            dve.wait_ge(S["gate_moved"], 16)
            dve.wait_ge(S["sc_ready"], 1)
            link(cp(sc[R, 0:NCMP_S], ps[R, 7, 0:NCMP_S]))
            link(dve.tensor_reduce(sm(0), sc[R, 0:NCMP_S], AX.X, MAX, negate=True))
            dve.sem_inc(S["sc_exp"], 1)
            dve.wait_ge(S["sc_exp"], 2)
            link(dve.reciprocal(sm(2), sm(1)))
            link(ts(gs[R, 0:NCMP_S], sc[R, 0:NCMP_S], sm(2), None, MUL))
            dve.sem_inc(S["sc_soft"], 1)
            link(ts(sc[R, 0:NCMP_S], gs[R, 0:NCMP_S], gate_rows[:, 0:1], None, MUL))
            dve.wait_ge(S["sum_done"], 1)
            link(cp(gs[R, 0:NCMP_S], ps[R, 5, 0:NCMP_S]))
            bs, flag, pen = small[R, 220:234], small[R, 240:254], small[R, 260:274]

            def cover(t):
                return gs[R, 3 + t:3 + t + 4 * (NSELB - 1) + 1:4]
            link(tt(bs, cover(0), cover(1), ADD))
            for t in range(2, 5):
                link(tt(bs, bs, cover(t), ADD))
            link(dve.tensor_reduce(sm(12), bs, AX.X, MIN))
            link(ts(flag, bs, sm(12), None, EQ))
            link(tt(flag, flag, blkno[R, 0:NSELB], MUL))
            link(dve.tensor_reduce(sm(13), flag, AX.X, MAX))
            link(ts(pen, blkno[R, 0:NSELB], sm(13), NEG, EQ, MUL))
            dve.wait_ge(S["ss_ready"], 1)
            link(cp(ss[R, 0:1024], ps[R, 0:2, 0:512]), tt(ss[R, 1024:1032], ps[R, 2, 0:NB], newmask[R], ADD))
            mid = ss[R, 64:64 + NSELB * 64].rearrange("p (j s) -> p j s", s=64)
            link(tt(mid, mid, pen.to_broadcast([ROWS, NSELB, 64]), ADD))
            link(dve.tensor_reduce(sm(4), ss[R, 0:1032], AX.X, MAX, negate=True))
            dve.sem_inc(S["ss_max"], 1)
            dve.wait_ge(S["ss_exp"], 1)
            link(dve.reciprocal(sm(6), sm(5)))
            link(tt(sm(6), sm(6), gate_rows[:, 1:2], MUL))
            link(ts(ss[R, 0:1032], ss[R, 0:1032], sm(6), None, MUL))
            dve.sem_inc(S["ss_p"], 1)
            dve.wait_ge(S["pts_ready"], 1)
            link(cp(pts[0:NCMP_S, 0, :], ps[0:NCMP_S, 3, 0:ROWS]), cp(pts[0:NB, 1, :], ps[0:NB, 3, ROWS:2 * ROWS]),
                 cp(pts[:, 2:10, :].rearrange("p a b -> p (a b)"), ps[:, 4, 0:512]))
            dve.sem_inc(S["pts_done"], 1)
            dve.wait_ge(S["sw_ready"], 1)
            link(cp(sw[R, 0:512], ps[R, 0, 0:512]), tt(sw[R, 512:520], ps[R, 1, 0:NB], newmask[R], ADD))
            link(dve.tensor_reduce(sm(8), sw[R, 0:520], AX.X, MAX, negate=True))
            dve.sem_inc(S["sw_max"], 1)
            dve.wait_ge(S["sw_exp"], 1)
            link(dve.reciprocal(sm(10), sm(9)))
            link(tt(sm(10), sm(10), gate_rows[:, 2:3], MUL))
            link(ts(sw[R, 0:520], sw[R, 0:520], sm(10), None, MUL))
            dve.sem_inc(S["sw_p"], 1)
            dve.wait_ge(S["ptw_ready"], 1)
            link(cp(pts[0:NB, 10, :], ps[0:NB, 2, 0:ROWS]),
                 cp(pts[:, 11:15, :].rearrange("p a b -> p (a b)"), ps[:, 3, 0:256]))
            dve.sem_inc(S["ptw_done"], 1)
            dve.wait_ge(S["os_ready"], 1)
            grp, grp2 = [], []
            for g in range(2):
                rows = slice(g * HD, (g + 1) * HD)
                o_ = ps[rows, 6:8, 0:ROWS].rearrange("p a (b g r) -> p a g r b", g=2, r=GRP)
                dst = zT[rows, 4:8, SEQ:TOK]
                grp.append(cp(dst, o_[:, 0, g]))
                grp2.append((dst, o_[:, 1, g]))
            link(*grp)
            link(*[tt(a, a, b, ADD) for a, b in grp2])
            dve.sem_inc(S["os_done"], 1)

            dve.wait_ge(S["bias_loaded"], 16)

            def ttr(u):
                i, br, g = units[u]
                nk = (i + 1) * P
                if u >= 2:
                    dve.wait_ge(S["u_t"], sum(units[v][0] + 1 for v in range(u - 1)))
                for r in range(GRP):
                    dve.wait_ge(S["u_s"], GRP * u + r + 1)
                    dve.tensor_tensor_reduce(pbuf[:, (u % 2) * GRP + r, 0:nk], ps[:, r, 0:nk],
                                             biasT[:, g * GRP + r, 384 - P * i:384 - P * i + nk],
                                             1.0, -3e38, ADD, MAX, pst(u, 0)[:, r:r + 1]).then_inc(S["u_ttr"], 1)
                dve.wait_ge(S["u_ttr"], GRP * (u + 1))
                ts(pst(u, 1), pst(u, 0), -1.0, None, MUL).then_inc(S["u_max"], 1)

            def scale(u):
                i, br, g = units[u]
                dve.wait_ge(S["u_exp"], GRP * (u + 1))
                link(dve.reciprocal(pst(u, 3), pst(u, 2)))
                h = (br + 1) * NH + g * GRP
                tt(pst(u, 3), pst(u, 3), gates[:, i, h:h + GRP], MUL).then_inc(S["u_rs"], 1)

            tcount = [0]

            def evac(u):
                for kb in range(units[u][0] + 1):
                    tcount[0] += 1
                    dve.wait_ge(S["u_t"], tcount[0])
                    if u >= 1:
                        dve.wait_ge(S["u_pv"], u)
                    cp(ptb[:, kb, :], ps[:, 4 + (tcount[0] - 1) % 2, 0:512]).then_inc(S["u_tdone"], 1)

            for i in range(4):
                dve.wait_ge(S["pc_s"], i + 1)
                pv3 = pcb.rearrange("p (h n) -> p h n", h=NH)
                link(tt(pcb, ps[:, 0, 0:NH * NCMP_P], pbias[:, i, :], ADD))
                link(dve.tensor_reduce(pcm(0), pv3, AX.X, MAX))
                link(tt(pv3, pv3, pcm(0).to_broadcast([P, NH, NCMP_P]), SUB))
                dve.sem_inc(S["pc_max"], 1)
                dve.wait_ge(S["pc_exp"], i + 1)
                link(dve.tensor_reduce(pcm(1), pv3, AX.X, ADD))
                link(dve.reciprocal(pcm(1), pcm(1)))
                link(tt(pcm(1), pcm(1), gates[:, i, 0:NH], MUL))
                if i == 0:
                    link(ts(pcm(1), pcm(1), validq, None, MUL))
                link(tt(pv3, pv3, pcm(1).to_broadcast([P, NH, NCMP_P]), MUL))
                dve.sem_inc(S["pc_p"], 1)
                dve.wait_ge(S["pc_t"], i + 1)
                link(*[cp(ptcb[0:NCMP_P, q * 512:(q + 1) * 512], ps[0:NCMP_P, 4 + q, 0:512]) for q in range(2)])
                dve.sem_inc(S["pc_tdone"], 1)
                ttr(4 * i)
                for q in range(4):
                    u = 4 * i + q
                    scale(u)
                    if q < 3:
                        ttr(u + 1)
                    evac(u)
                dve.wait_ge(S["u_pv"], 4 * i + 4)
                link(*[cp(zT[g * HD:(g + 1) * HD, 4:8, i * P:(i + 1) * P],
                          ps[g * HD:(g + 1) * HD, 6 + g, 0:512].rearrange("p (r q) -> p r q", q=P)) for g in range(2)])
                dve.sem_inc(S["o_done"], 1)
            dve.wait_ge(S["mix_sum"], 2)
            inverse_ms(512, 0)
            dve.wait_ge(S["rstd_ready"], 3)
            link(*[stt(zT[:, 4 + c, :], zT[:, 4 + c, :], par[:, NAG + c:NAG + c + 1], rstd, MUL, MUL) for c in range(4)])
            dve.sem_inc(S["mix_ready"], 1)

            def add_gated(c, src0, src1, part):
                gcol = mT[:, 8 * part + c, :]
                link(*[stt(xT[:, c, a:b], s, gcol[:, 0:1], xT[:, c, a:b], MUL, ADD) for a, b, s in src0])
                link(tt(small[:, 0:NB], src1, gcol[:, 1:9], MUL))
                link(tt(xT[:, c, SEQ:TOK], xT[:, c, SEQ:TOK], small[:, 0:NB], ADD))
            for c in range(KD):
                dve.wait_ge(S["pe_step"], c + 1)
                b = 2 + 2 * (c % 3)
                add_gated(c, [(0, HALF, ps[:, b, 0:HALF]), (HALF, SEQ, ps[:, b + 1, 0:SEQ - HALF])],
                          ps[:, b + 1, SEQ - HALF:HALF], 2)
                dve.sem_inc(S["proj_ready"], 1)
            dve.sem_inc(S["proj_done"], 1)
            dve.wait_ge(S["kv_stored"], 16)
            modulate(h2T, 2, 3)

            for n in range(16):
                dve.wait_ge(S["s_ready"], n + 1)
                b = 4 + 2 * (n % 2)
                tiles = []
                for t in range(5):
                    m = P if t < 4 else NB
                    tiles.append((slice(0, m), t, ps[0:m, b + t // 4, (t % 4) * P:(t % 4 + 1) * P]))
                link(*[dve.max(sv[r, 16 * t + n, 0:8], s) for r, t, s in tiles])
                link(*[dve.max_index(si[r, 16 * t + n, 0:8], sv[r, 16 * t + n, 0:8], s) for r, t, s in tiles])
                link(*[dve.match_replace(tmpk[r, t, :], sv[r, 16 * t + n, 0:8], s, -3e38) for r, t, s in tiles])
                dve.sem_inc(S["s_free"], 1)
                link(*[dve.max(sv[r, 16 * t + n, 8:16], tmpk[r, t, :]) for r, t, s in tiles])
                link(*[dve.max_index(si[r, 16 * t + n, 8:16], sv[r, 16 * t + n, 8:16], tmpk[r, t, :]) for r, t, s in tiles])
            dve.wait_ge(S["bias_ready"], 2)
            for t in range(5):
                r = slice(0, P if t < 4 else NB)
                m = r.stop
                link(cp(sif[r, 16 * t:16 * t + 16, :], si[r, 16 * t:16 * t + 16, :]))
                s0, s1 = sv[r, 16 * t:16 * t + 16:2, :], sv[r, 16 * t + 1:16 * t + 16:2, :]
                link(*[tt(cand[r, h, :].rearrange("p (a b) -> p a b", a=16), s0[:, h, :].to_broadcast([m, 16, 16]),
                          s1[:, h, :].rearrange("p (o b) -> p o b", o=1).to_broadcast([m, 16, 16]), ADD) for h in range(NH)])
                ci3 = ci[r].rearrange("p (h k) -> p h k", k=16)
                link(*[dve.max(best[r, h, 0:8], cand[r, h, :]) for h in range(NH)])
                link(*[dve.max_index(ci3[:, h, 0:8], best[r, h, 0:8], cand[r, h, :]) for h in range(NH)])
                link(*[dve.match_replace(cand2[r, h, :], best[r, h, 0:8], cand[r, h, :], -3e38) for h in range(NH)])
                link(*[dve.max(best[r, h, 8:16], cand2[r, h, :]) for h in range(NH)])
                link(*[dve.max_index(ci3[:, h, 8:16], best[r, h, 8:16], cand2[r, h, :]) for h in range(NH)])
                link(ts(cab[r, 0, :], ci[r], 4, None, ALU.logical_shift_right), ts(cab[r, 1, :], ci[r], 15, None, ALU.bitwise_and))
                link(cp(cabf[r], cab[r]))
                for w in range(2):
                    eqv = cand[r].rearrange("p h (k a) -> p (h k) a", a=16)
                    link(tt(eqv, cabf[r, w, :].to_broadcast([m, P, 16]),
                            iota16[r].rearrange("p (o a) -> p o a", o=1).to_broadcast([m, P, 16]), EQ))
                    link(*[tt(cand2[r, h, :].rearrange("p (k a) -> p k a", a=16), cand[r, h, :].rearrange("p (k a) -> p k a", a=16),
                              sif[r, 16 * t + 2 * h + w, :].rearrange("p (o a) -> p o a", o=1).to_broadcast([m, 16, 16]), MUL)
                           for h in range(NH)])
                    if t and w == 0:
                        dve.wait_ge(S["tr_ready"], t)
                    link(dve.tensor_reduce(isel[r, w, :], cand2[r].rearrange("p h (k a) -> p (h k) a", a=16), AX.X, ADD))
                link(cp(gden[r, 0, :], best[r, :, 0]))
                link(tt(best[r], best[r], gden[r, 0, :].to_broadcast([m, NH, 16]), SUB))
                dve.sem_inc(S["rexp"], 1)
                dve.wait_ge(S["rexp_done"], t + 1)
                link(dve.tensor_reduce(gden[r, 1, :], best[r], AX.X, ADD))
                link(dve.reciprocal(gden[r, 1, :], gden[r, 1, :]))
                link(tt(isel[r, 2, :].rearrange("p (h k) -> p h k", k=16), best[r], gden[r, 1, :].to_broadcast([m, NH, 16]), MUL))
                dve.sem_inc(S["tr_in"], 1)
                dve.wait_ge(S["tr_ready"], t + 1)
                link(cp(routeT[:, :, t * P:t * P + m], ps[:, 0:3, 0:m]))
                dve.sem_inc(S["tr_done"], 1)

            for ch in range(5):
                with dve.Fori(0, TC // 8) as it:
                    for q in range(2):
                        n = it * 2 + (26 * ch + q)
                        dve.wait_ge(S["g_ready"], n + 1)
                        for t in range(4):
                            tok = it * 8 + (ch * TC + 4 * q + t)
                            dst = oh[:, 4 * q + t, :]
                            ts(dst[:, 0:P], iota, routeT[:, 0, bass.ds(tok, 1)], None, EQ).then_inc(S["hot_step"], 1)
                            ts(dst[:, P:2 * P], iota, routeT[:, 1, bass.ds(tok, 1)], routeT[:, 2, bass.ds(tok, 1)],
                               EQ, MUL).then_inc(S["hot_step"], 1)
                        dve.wait_ge(S["hot_step"], n * 8 + 8)
                        dve.sem_inc(S["oh_ready"], 1)

            dve.wait_ge(S["g_ready"], 132)
            link(dve.memset(acc, 0.0))
            dve.sem_inc(S["ff_free"], 2)

            def weigh(g, par_, gcount):
                dve.wait_ge(g_l[par_], gcount * 16)
                for jj in range(EXP_J):
                    dve.wait_ge(S["gelu_done"], g * EXP_J + jj + 1)
                    a = av[:, par_ * EXP_J + jj, :]
                    tt(a, a, gr[:, par_ * EXP_J + jj, :], MUL).then_inc(S["a_ready"], 1)

            def collect(g):
                for dc in range(KD):
                    dve.wait_ge(S["ff_ready"], g * KD + dc + 2)
                    dve.wait_ge(S["ff_free"], g * KD + dc + 1)
                    a = acc[:, dc, :].rearrange("p (h t) -> p h t", h=2)
                    tt(a, a, ps[:, 4 + 2 * (dc % 2):6 + 2 * (dc % 2), 0:HALF], ADD).then_inc(S["ff_free"], 1)

            weigh(0, 0, 1)
            with dve.Fori(0, GROUPS // 2 - 1) as it:
                weigh(it * 2 + 1, 1, it + 1)
                collect(it * 2)
                weigh(it * 2 + 2, 0, it + 2)
                collect(it * 2 + 1)
            weigh(GROUPS - 1, 1, GROUPS // 2)
            collect(GROUPS - 2)
            collect(GROUPS - 1)
            dve.wait_ge(S["ff_free"], 2 + GROUPS * KD)
            for c in range(KD):
                add_gated(c, [(0, SEQ, acc[:, c, 0:SEQ])], acc[:, c, SEQ:TOK], 5)
            link(tt(sq, xT[:, :, :], xT[:, :, :], MUL))
            dve.sem_inc(S["sq_done"], 1)
            dve.wait_ge(S["sum_ready"], 3)
            inverse_ms(D, 0)
            dve.wait_ge(S["rstd_ready"], 5)
            link(*[stt(h2T[:, k, :], xT[:, k, :], par[:, FG + k:FG + k + 1], rstd, MUL, MUL) for k in range(KD)])
            dve.sem_inc(S["fin_ready"], 1)


def one_hot_buckets(dist):
    dist = np.asarray(dist)
    b = np.where(dist < 16, dist, 16 + np.searchsorted(EDGES, dist, side="right"))
    b = np.where(dist < 0, 32, b)
    return (np.arange(33)[:, None] == b[None, :]).astype(np.float32)


def kernel(**a):
    import concourse.bacc as bacc
    from concourse.bass_utils import run_bass_kernel_spmd

    a = {k: np.asarray(v) for k, v in a.items()}
    cols = np.cumsum((0, 512, 512, 512, 256, 256, 256, 24))

    def feat(v):
        return v.reshape(-1, P).T

    def chunks(w):
        return w.reshape(KD, P, -1, P).transpose(2, 1, 0, 3)

    w = a["w_in"][0]
    qw = w[:, cols[2]:cols[3]].reshape(D, NKV, GRP, HD).transpose(0, 2, 1, 3).reshape(D, 512)
    kvw = [w[:, cols[i]:cols[i + 1]].reshape(D, NKV, 2, HD).transpose(0, 2, 1, 3).reshape(D, 256) for i in (3, 4, 5)]
    w_all = np.concatenate([w[:, :1024], qw] + kvw, axis=1)
    wout = a["w_out"][0]
    wout = np.concatenate([wout[:512], wout[512:].reshape(NKV, GRP, HD, D).transpose(1, 0, 2, 3).reshape(512, D)])
    nag = a["out_norm_att"][0].reshape(NKV, GRP, HD).transpose(1, 0, 2).reshape(512)
    par = np.concatenate([feat(v) for v in (a["norm1_g"][0], a["norm2_g"][0], a["final_g"], a["out_norm_lru"][0], nag,
                          a["conv_w"][0].reshape(-1), a["conv_b"][0], a["lru_ba"][0], a["lru_bi"][0],
                          a["lru_lambda"][0], a["peer_bq"][0])], axis=1)
    x = np.concatenate([a["x_prompt"].reshape(SEQ, D), a["x_sample"].reshape(NB, D)])
    c = np.concatenate([a["c_prompt"], a["c_sample"]])

    def pool(cache, which):
        return cache[0, :, :, :, which].transpose(0, 2, 3, 1).reshape(POOL * P, P)

    selk, selv = pool(a["cache_sel_kv"], 0), a["cache_sel_kv"][0, :, :, :, 1].reshape(POOL * P, P)
    win = a["cache_win_kv"][0]
    cw1 = a["cmp_w1"][0].transpose(0, 2, 1, 3)
    pos = np.concatenate([a["cmp_pos"][0].transpose(0, 2, 1)] * 2, axis=1)
    rows = np.arange(ROWS)
    ins = {
        "xT": x.T.reshape(KD, P, TOK).transpose(1, 0, 2), "cT": c.T.reshape(KD, P, 9).transpose(1, 0, 2),
        "par": par, "adab": feat(a["ada_b"][0]), "rel_bias": a["rel_bias"],
        "ada_w": a["ada_w"][0].reshape(KD, P, 6 * D).transpose(1, 0, 2),
        "w_in": chunks(w_all), "w_gate": w[:, cols[6]:].reshape(KD, P, 24).transpose(1, 0, 2),
        "w_out": wout.reshape(KD, P, D).transpose(1, 0, 2), "wq": chunks(a["peer_wq"][0]),
        "sk": a["peer_subkeys"][0].reshape(16, P, P).transpose(2, 0, 1),
        "state_conv": a["state_conv"][0].reshape(NB, 3, 4, P).transpose(3, 2, 1, 0).reshape(P, 4, 3 * NB),
        "state_h": a["state_lru_h"][0].reshape(NB, 4, P).transpose(2, 1, 0),
        "wlru": np.stack([a["lru_wa"][0].reshape(4, 2, HD, HD), a["lru_wi"][0].reshape(4, 2, HD, HD)])
                  .transpose(2, 3, 0, 1, 4).reshape(2, HD, 8, HD),
        "cmp_w1": cw1, "cmp_w2": a["cmp_w2"][0], "posT": pos, "page_table": a["page_table"].reshape(1, NB * PAGES),
        "pool_k": pool(a["cache_cmp_kv"], 0), "pool_v": pool(a["cache_cmp_kv"], 1),
        "pool_s": np.concatenate([selk, selv], axis=1),
        "win_kT": win[:, :, :, 0].transpose(2, 3, 0, 1).reshape(P, NB, 512), "win_v": win[:, :, :, 1].reshape(NB, 512, P),
        "uT": a["peer_u"][0].reshape(P, P, KD, P).transpose(1, 3, 2, 0), "v": a["peer_v"][0].reshape(P, P, D),
        "ohd": one_hot_buckets(np.concatenate([1024 - np.arange(1153), np.zeros(8, np.int64)])),
        "oha": one_hot_buckets(np.arange(OHA_W) - 511),
        "ohw": one_hot_buckets(np.concatenate([[-1], 512 - np.arange(1, 512)])),
        "newmask": np.where(rows[:, None] // NH == np.arange(NB)[None, :], 0.0, NEG).astype(np.float32),
        "gsum": (rows[:, None] // GRP == rows[None, :] // GRP).astype(np.float32),
        "validq": (np.arange(P)[:, None] >= 31).astype(np.float32),
        "blkno": np.broadcast_to(np.arange(1, NSELB + 1, dtype=np.float32), (ROWS, NSELB)),
    }
    ins = {k: np.ascontiguousarray(v) for k, v in ins.items()}
    outs = {"o_y": (P, KD, TOK), "o_kv": (P, 6, TOK), "o_h": (P, 4, 9), "o_conv": (P, 4, 27),
            "o_wink": (P, NB, 512), "o_winv": (NB, 512, P)}
    nc = bacc.Bacc("TRN2", target_bir_lowering=False, num_devices=1)
    io = {k: nc.dram_tensor("in_" + k, v.shape, mybir.dt.from_np(v.dtype), kind="ExternalInput").ap() for k, v in ins.items()}
    for k, shape in outs.items():
        io[k] = nc.dram_tensor("out_" + k, shape, F32, kind="ExternalOutput").ap()
    io["rscratch"] = nc.dram_tensor("rscratch", (NH, 640), F32).ap()
    io["rrows"] = nc.dram_tensor("rrows", (P, NH, 640), F32).ap()
    io["gscratch"] = nc.dram_tensor("gscratch", (ROWS, 3), F32).ap()
    io["gw"] = nc.dram_tensor("gw", (P, P, TOK), F32).ap()
    build(nc, io)
    got = run_bass_kernel_spmd(nc, [{"in_" + k: v for k, v in ins.items()}], core_ids=[0]).results[0]
    r = {k: got["out_" + k] for k in outs}

    y = r["o_y"].transpose(2, 1, 0).reshape(TOK, D)
    kv = r["o_kv"].reshape(NKV, HD, 3, 2, TOK).transpose(2, 4, 0, 3, 1)
    wk = r["o_wink"].reshape(NKV, HD, NB, 512).transpose(2, 3, 0, 1)
    wv = r["o_winv"].reshape(NB, 512, NKV, HD)
    old = np.stack([wk, wv], axis=3)[:, :511]
    new_win = np.concatenate([old, kv[2, SEQ:][:, None]], axis=1)
    h = r["o_h"].transpose(2, 1, 0).reshape(9, 512)
    conv = r["o_conv"].reshape(P, 4, 3, 9).transpose(3, 2, 1, 0).reshape(9, 3, 512)
    return (y[:SEQ][None], y[SEQ:][:, None],
            kv[0, :SEQ][None, None], kv[0, SEQ:][None, :, None],
            kv[1, :SEQ][None, None], kv[1, SEQ:][None, :, None],
            kv[2, :SEQ][None, None], new_win[None],
            h[0:1][None], h[1:][None], conv[0:1][None], conv[1:][None])
```

```python
from contextlib import ExitStack

import concourse.bass as bass
from concourse import mybir
import numpy as np

F32 = mybir.dt.float32
U32 = mybir.dt.uint32
ALU = mybir.AluOpType
ACT = mybir.ActivationFunctionType
AX = mybir.AxisListType
ADD, MUL, SUB, MAX, MIN, EQ = ALU.add, ALU.mult, ALU.subtract, ALU.max, ALU.min, ALU.is_equal

P = 128
D = 1024
KD = D // P
SEQ = 512
NB = 8
TOK = SEQ + NB
HALF = TOK // 2
PAST = 1024
PAGE = 128
PAGES = PAST // PAGE
POOL = 5 * NB * PAGES // 4
HD = 64
NH = 8
NKV = 2
GRP = NH // NKV
ROWS = NB * NH
NCMP_P = SEQ // 16 - 1
NCMP_S = PAST // 16 - 1
NSELB = 14
NEG = -1e30
EPS = 1e-6
ZC = 18
XR, YG, QC, KC, VC_, KS, VS, KW, VW = 0, 4, 8, 12, 13, 14, 15, 16, 17
F32R = mybir.dt.float32r
EXP_J = 4
GROUPS = P // EXP_J
TILE_U = (6, 6, 6, 6, 4)
TOPK_U = 16 + sum(TILE_U)
HOT_U = TOPK_U + 32
TAIL_U = 8
SPILL = HOT_U + TAIL_U
SPILL_G = SPILL // EXP_J
AW = 384
AN = 6 * D // AW
TC = 64
OHD_W, OHA_W, OHW_W = 1161, 1024, 512
EDGES = [21, 27, 35, 46, 59, 77, 99, 128, 166, 216, 280, 363, 470, 609, 790]


def build(nc, io):
    ctx = ExitStack()
    with ctx:
        def sem(name):
            return ctx.enter_context(nc.semaphore(name))

        def sb(name, shape, dt=F32):
            return ctx.enter_context(nc.sbuf_tensor(name, shape, dt))

        xT = sb("xT", [P, KD, TOK])
        mT = sb("mT", [P, 48, 9])
        ident = sb("ident", [P, P])
        ones = sb("ones", [P, P])
        par = sb("par", [P, 128])
        posb = sb("posb", [P, 1])
        gates = sb("gates", [P, 5, 24])
        gate_rows = sb("gate_rows", [ROWS, 3])
        cst = sb("cst", [P, 540])
        with nc.sbuf_tensor("arena", [P, 46700], F32) as arena:
            pass
        uh, ul = sb("uh", [P, 2 * KD, P], F32R), sb("ul", [P, 2 * KD, P], F32R)
        vh, vl = sb("vh", [P, 2 * EXP_J, D], F32R), sb("vl", [P, 2 * EXP_J, D], F32R)
        ah, al = sb("ah", [P, 2 * EXP_J, TOK], F32R), sb("al", [P, 2 * EXP_J, TOK], F32R)
        hh, hl = sb("hh", [P, KD, TOK], F32R), sb("hl", [P, KD, TOK], F32R)
        raw = sb("raw", [P, 4, D])
        zbuf = sb("zbuf", [P, 2, TOK])
        gr = sb("gr", [P, 2, EXP_J * TOK])
        ztail = gr[:, 1, 0:2 * TOK].rearrange("p (s t) -> p s t", t=TOK)
        ps = ctx.enter_context(nc.psum_tensor("ps", [P, 8, 512], F32))

        N1G, N2G, FG, NLG, NAG, CW, CB, BA, BI, LAM, BQ, ADB = 0, 8, 16, 24, 28, 32, 48, 52, 56, 60, 64, 80
        rbx, rb, newmask, gsum = cst[:, 0:64], cst[:, 64:72], cst[:, 72:80], cst[:, 80:144]
        validq, blkno, small = cst[:, 144:145], cst[:, 145:161], cst[:, 161:441]
        lrt, pstt, pcmt = cst[:, 441:481], cst[:, 481:513], cst[:, 513:529]

        def lr(n):
            return lrt[:, 4 * n:4 * n + 4]

        def sm(n):
            return small[0:ROWS, 200 + n:201 + n]

        def pst(u, n):
            return pstt[:, (u % 2) * 16 + 4 * n:(u % 2) * 16 + 4 * n + 4]

        def pcm(n):
            return pcmt[:, 8 * n:8 * n + 8]

        def at(off, *shape):
            n = int(np.prod(shape))
            assert off + n <= 46700
            a = arena[:, off:off + n]
            return a.rearrange("p (a b) -> p a b", b=shape[1]) if len(shape) == 2 else a

        zT = at(0, ZC, TOK)
        hT = at(9360, KD, TOK)
        ada = at(13520, 2 * KD, AW)
        win_w = at(19664, 3 * KD, P)
        X = at(22736, 8736)
        w1 = at(31472, 32, P)
        ohd = at(35568, OHD_W)
        oha = at(36729, OHA_W)
        hid = at(37753, 546)
        ckT = at(38299, 544)
        vc = at(38843, 9, P)
        w2 = at(39995, 2, P)
        biasT = at(40251, NH, 512)
        m9 = at(40251, 2, AW)
        cT = at(41275, KD, 9)
        rsb = at(41475, 640)
        pbias = at(44347, 4, NH * NCMP_P)
        rstd = at(45339, TOK)
        wgate = at(45859, KD, 24)
        stc = at(46051, 4, 3 * NB)
        h0T = at(46147, 4, NB)
        rT, iT_ = at(9360, 4, TOK), at(11440, 4, TOK)
        xcT, aT, uT = at(13520, 4, TOK), at(15600, 4, TOK), at(17680, 4, TOK)
        wlru = at(19760, 8, P)
        outh = at(20912, 4, 9)
        outc = at(20948, 4, 27)
        sel = at(13520, NB * PAGES, 256)
        qz = at(29904, 2 * GRP, SEQ)
        qpad = at(34000, NB, ROWS)
        qs = at(34512, ROWS)
        vnew = at(34576, 2, P)
        vn = at(36729, 8, P)
        ohw = at(9360, OHW_W)
        ss = at(9872, 1032)
        sw = at(10904, 520)
        sc = at(11424, 64)
        gs = at(11488, 64)
        pts = at(11552, 15, ROWS)
        kwin = at(13520, NB, 512)
        vwin = at(17616, NB * 4, P)
        wout = at(21712, KD, D)
        pbuf = at(9360, 2 * GRP, SEQ)
        ptb = at(13520, 4, GRP * P)
        ptcb = at(15568, 1024)
        pcb = at(16592, NH * NCMP_P)
        h2T = at(20480, KD, TOK)
        wq = at(4096, 3 * KD, P)
        qT = at(7168, TOK)
        sk = at(8208, 16, P)
        tmpk = at(10256, 5, P)
        cand = at(10896, NH, 256)
        cand2 = at(12944, NH, 256)
        best = at(14992, NH, 16)
        cabf = at(15120, 2, P)
        isel = at(15376, 3, P)
        gden = at(15760, 2, NH)
        sif = at(15776, 5 * 16, 16)
        sv = at(24640, 5 * 16, 16)
        si = arena[:, 25920:27200].bitcast(U32).rearrange("p (a b) -> p a b", b=16)
        ci = arena[:, 27200:27328].bitcast(U32)
        cab = arena[:, 27328:27584].bitcast(U32).rearrange("p (a b) -> p a b", b=P)
        routeT = at(42256, 3, TOK)
        iota = at(43816, P)
        iota16 = at(43944, 16)
        oh = at(20480, 4 * 4, 2 * P)
        stage = at(4096, 2, P * TC)
        acc = xT[:, :, :]
        x2 = at(28800, KD, TOK)
        sq = at(4160, KD, TOK)

        names = """c_loaded par_loaded table_loaded const_loaded x_loaded ada_ready z_ready wgate_loaded lrus_loaded
            hi_ready lruw_loaded z_moved kv_stored lru_ready lru_stored lru_norm ohw_loaded gates_ready
            gate_stored gate_moved sel_free win_loaded wout_loaded out_stored proj_done sk_loaded h_ready
            x_spilled q_ready lo_done zz_ready x_back fin_ready pool_done memset_done w2_loaded w1k_loaded
            pos_loaded page_loaded gather_k hid_ready w1v_loaded pos2_loaded gather_v gather_s rs_copied mt_done
            scratch_stored rows_stored bias_loaded bias_ready gelu_done g_moved g_ready a_ready rb_ready
            rs_ready pb_ready silu_done m9_ready mt_ready sq_done sum_ready zg_ready xc_ready ri_ready
            gate_ready x_filled gelu_ready ck_ready mix_sum cmp_done vt_ready vt_done qpad_ready sc_ready
            ss_ready sc_soft sum_done ss_p pts_ready pts_done sw_ready sw_p ptw_ready ptw_done os_ready os_done
            u_ttr u_s pc_s pc_p u_tdone pc_t pc_tdone o_done u_p u_t u_pv mix_sq mix_ready proj_ready pe_step
            q_moved s_free s_ready tr_in tr_ready tr_done oh_ready ff_free ff_ready act_step root_in rstd_ready
            lru_prep exp_ready yg_ready sc_exp ss_max ss_exp sw_max sw_exp pc_max pc_exp u_max u_exp u_rs
            hi_done rexp rexp_done dve_step a_step""".split()
        S = {n: sem(n) for n in names}
        ada_l = [sem(f"ada_loaded{i}") for i in range(2)]
        w_l = [sem(f"w_loaded{i}") for i in range(3)]
        wq_l = [sem(f"wq_loaded{i}") for i in range(3)]
        raw_l = [sem(f"raw_loaded{i}") for i in range(4)]
        gt_l = [sem(f"g_tail_loaded{i}") for i in range(2)]
        zst = [sem(f"z_stored{i}") for i in range(2)]
        zl = [sem(f"z_loaded{i}") for i in range(2)]
        g_l = [sem(f"g_loaded{i}") for i in range(2)]
        st_l = [sem(f"stage_stored{i}") for i in range(2)]

        rscratch = io["rscratch"]
        block = ctx.enter_context(nc.Block())
        units = [(i, br, g) for i in range(4) for br in range(2) for g in range(2)]

        @block.sync
        def _(sp):
            def load(dst, src, s):
                sp.dma_start(dst, src).then_inc(s, 16)

            load(cT, io["cT"], S["c_loaded"])
            load(par[:, 0:80], io["par"], S["par_loaded"])
            load(par[:, 80:128], io["adab"], S["par_loaded"])
            load(ohd[0:33], io["ohd"], S["table_loaded"])
            load(oha[0:33], io["oha"], S["table_loaded"])
            load(rb[0:32], io["rel_bias"], S["table_loaded"])
            load(rbx[0:32].rearrange("p (b h) -> p b h", h=NH),
                 io["rel_bias"].rearrange("a (o h) -> a o h", o=1).to_broadcast([32, NB, NH]), S["table_loaded"])
            load(newmask[0:ROWS], io["newmask"], S["const_loaded"])
            load(gsum[0:ROWS], io["gsum"], S["const_loaded"])
            load(validq, io["validq"], S["const_loaded"])
            load(blkno[0:ROWS, 0:NSELB], io["blkno"], S["const_loaded"])
            for n in range(2):
                load(ada[:, n * KD:(n + 1) * KD, :], io["ada_w"][:, :, n * AW:(n + 1) * AW], ada_l[n])
            load(xT[:, :, :], io["xT"], S["x_loaded"])
            for n in range(2, AN):
                sp.wait_ge(S["ada_ready"], n - 1)
                load(ada[:, (n % 2) * KD:(n % 2 + 1) * KD, :], io["ada_w"][:, :, n * AW:(n + 1) * AW], ada_l[n % 2])
            for n in range(3):
                load(win_w[:, n * KD:(n + 1) * KD, :], io["w_in"][n], w_l[n])
            for n in range(3, ZC):
                sp.wait_ge(S["z_ready"], n - 2)
                load(win_w[:, (n % 3) * KD:(n % 3 + 1) * KD, :], io["w_in"][n], w_l[n % 3])
            sp.wait_ge(S["ada_ready"], AN)
            load(wgate, io["w_gate"], S["wgate_loaded"])
            load(stc, io["state_conv"], S["lrus_loaded"])
            load(h0T, io["state_h"], S["lrus_loaded"])
            sp.wait_ge(S["hi_ready"], 1)
            for e in range(2):
                load(wlru[e * HD:(e + 1) * HD, :, e * HD:(e + 1) * HD],
                     io["wlru"][e], S["lruw_loaded"])
            sp.wait_ge(S["z_moved"], ZC)
            load(io["o_kv"], zT[:, KC:ZC, :], S["kv_stored"])
            sp.wait_ge(S["lru_ready"], 1)
            load(io["o_h"], outh, S["lru_stored"])
            load(io["o_conv"], outc, S["lru_stored"])
            sp.wait_ge(S["lru_norm"], 1)
            load(ohw[0:33], io["ohw"], S["ohw_loaded"])
            sp.wait_ge(S["gates_ready"], 1)
            load(io["gscratch"].rearrange("(b h) r -> b (h r)", h=NH), gates[0:NB, 4, :], S["gate_stored"])
            sp.wait_ge(S["gate_stored"], 16)
            load(gate_rows[:, :], io["gscratch"], S["gate_moved"])
            sp.wait_ge(S["sel_free"], 1)
            load(kwin, io["win_kT"], S["win_loaded"])
            load(vwin, io["win_v"].rearrange("b (c p) f -> p (b c) f", p=P), S["win_loaded"])
            load(wout, io["w_out"], S["wout_loaded"])
            for b in range(NB):
                load(io["o_winv"][b, 0:511], io["win_v"][b, 1:512], S["out_stored"])
            load(io["o_wink"][:, :, 0:511], io["win_kT"][:, :, 1:512], S["out_stored"])
            sp.wait_ge(S["proj_done"], 1)
            load(sk, io["sk"], S["sk_loaded"])
            sp.wait_ge(S["kv_stored"], 16)
            for n in range(3):
                load(wq[:, n * KD:(n + 1) * KD, :], io["wq"][n], wq_l[n])

            def load_raw(slot, src):
                sp.dma_start(raw[:, slot, :], src).then_inc(raw_l[slot], 16)

            def u_block(blk):
                return io["uT"][blk]

            def v_block(blk):
                return io["v"][:, blk, :]

            for b in range(4):
                load_raw(b, u_block(b))
            sp.wait_ge(S["h_ready"], 2)
            sp.dma_start(io["xspill"], xT[:, :, :]).then_inc(S["x_spilled"], 16)
            for n in range(3, 16):
                sp.wait_ge(S["q_ready"], n - 2)
                load(wq[:, (n % 3) * KD:(n % 3 + 1) * KD, :], io["wq"][n], wq_l[n % 3])
                sp.wait_ge(S["lo_done"], n - 2)
                load_raw((n + 1) % 4, u_block(n + 1))
            for b in range(17, 20):
                sp.wait_ge(S["lo_done"], b - 3)
                load_raw(b % 4, u_block(b))
            with sp.Fori(5, SPILL // 4) as it:
                for b in range(4):
                    sp.wait_ge(S["lo_done"], it * 4 + (b - 3))
                    load_raw(b, u_block(it * 4 + b))
            with sp.Fori(0, SPILL_G) as it:
                for b in range(4):
                    sp.wait_ge(S["lo_done"], it * 4 + (SPILL + b - 3))
                    load_raw(b, v_block(it * 4 + b))
            with sp.Fori(0, GROUPS - SPILL_G) as it:
                for w, block_of in enumerate((u_block, v_block)):
                    for b in range(4):
                        sp.wait_ge(S["lo_done"], it * 8 + (2 * SPILL + 4 * w + b - 3))
                        load_raw(b, block_of(it * 4 + (SPILL + b)))
            sp.wait_ge(S["zz_ready"], P)
            load(x2, io["xspill"], S["x_back"])
            sp.wait_ge(S["fin_ready"], 1)
            load(io["o_y"], h2T, S["out_stored"])
            sp.wait_ge(S["out_stored"], 16 * (NB + 2))

        @block.gpsimd
        def _(pool):
            def load(dst, src, s):
                pool.dma_start(dst, src).then_inc(s, 16)

            pool.memset(ident[:, :], 0.0).then_inc(S["pool_done"], 1)
            pool.memset(w2, 0.0).then_inc(S["pool_done"], 1)
            pool.memset(w1, 0.0).then_inc(S["pool_done"], 1)
            pool.wait_ge(S["pool_done"], 3)
            pool.affine_select(out=ident[:, :], in_=ident[:, :], compare_op=ALU.not_equal, fill=1.0,
                               base=0, pattern=[[-1, P]], channel_multiplier=1).then_inc(S["memset_done"], 1)
            for c in range(2):
                for g in range(2):
                    load(w2[g * HD:(g + 1) * HD, c, g * HD:(g + 1) * HD], io["cmp_w2"][c], S["w2_loaded"])

            def load_w1(c, s):
                for g in range(2):
                    load(w1[g * HD:(g + 1) * HD, :, g * HD:(g + 1) * HD], io["cmp_w1"][c], s)
            load_w1(0, S["w1k_loaded"])
            load(X[:, 8704:8736], io["posT"][0], S["pos_loaded"])
            pgi = small[:, 0:64].bitcast(mybir.dt.int32)
            pid = small[:, 64:65].bitcast(mybir.dt.int32)
            idx = small[:, 128:192].bitcast(mybir.dt.int32)
            pool.dma_start(pgi, io["page_table"].to_broadcast([P, NB * PAGES])).then_inc(S["page_loaded"], 16)
            pool.iota(pid, pattern=[[0, 1]], base=0, channel_multiplier=1).then_inc(S["pool_done"], 1)
            pool.wait_ge(S["page_loaded"], 16)
            pool.tensor_scalar(pgi, pgi, float(P), None, MUL).then_inc(S["pool_done"], 1)
            pool.wait_ge(S["pool_done"], 5)
            pool.tensor_tensor(idx, pgi, pid.to_broadcast([P, 64]), ADD).then_inc(S["pool_done"], 1)
            pool.wait_ge(S["pool_done"], 6)

            def gather(dst, src, w, s):
                for n in range(NB * PAGES):
                    pool.indirect_dma_start(
                        out=dst[:, n * w:(n + 1) * w], out_offset=None, in_=src,
                        in_offset=bass.IndirectOffsetOnAxis(ap=idx[:, n:n + 1].bitcast(U32), axis=0)).then_inc(s, 16)
            gather(X, io["pool_k"], P, S["gather_k"])
            pool.wait_ge(S["hid_ready"], 1)
            load_w1(1, S["w1v_loaded"])
            load(X[:, 8704:8736], io["posT"][1], S["pos2_loaded"])
            gather(X, io["pool_v"], P, S["gather_v"])
            pool.wait_ge(S["hid_ready"], 2)
            pool.wait_ge(S["lru_norm"], 1)
            pool.wait_ge(S["z_ready"], ZC)
            gather(at(13520, 16384), io["pool_s"], 256, S["gather_s"])
            pool.wait_ge(S["rs_copied"], 1)
            pool.wait_ge(S["mt_done"], AN)
            pool.dma_start(rscratch, rsb[0:NH]).then_inc(S["scratch_stored"], 16)
            pool.wait_ge(S["scratch_stored"], 16)
            rows = io["rrows"]
            pool.dma_start(rows.rearrange("p h c -> p (h c)"),
                           rscratch.rearrange("h (o c) -> o (h c)", o=1).to_broadcast([P, NH * 640])
                           ).then_inc(S["rows_stored"], 16)
            pool.wait_ge(S["rows_stored"], 16)
            pool.dma_start(biasT, bass.AP(rows.tensor, 127, [[NH * 640 - 1, P], [640, NH], [1, 512]])
                           ).then_inc(S["bias_loaded"], 16)
            pool.wait_ge(S["proj_done"], 1)
            pool.iota(iota, pattern=[[1, P]], base=0, channel_multiplier=0,
                      allow_small_or_imprecise_dtypes=True).then_inc(S["bias_ready"], 1)
            pool.iota(iota16, pattern=[[1, 16]], base=0, channel_multiplier=0,
                      allow_small_or_imprecise_dtypes=True).then_inc(S["bias_ready"], 1)

            def store_z(b, slot):
                pool.wait_ge(S["gelu_done"], b + 1)
                pool.dma_start(io["zs"][b], zbuf[:, slot, :]).then_inc(zst[slot], 16)

            def store_stage(ch, par_):
                pool.wait_ge(S["g_moved"], ch * 16 + 20)
                pool.dma_start(io["gw"][ch], stage[:, par_, :]).then_inc(st_l[par_], 16)
            for b in range(TOPK_U):
                store_z(b, b % 2)
            with pool.Fori(0, 4) as it:
                for c in range(2):
                    for b in range(4):
                        store_z(it * 8 + (TOPK_U + 4 * c + b), b % 2)
                    store_stage(it * 2 + c, c)
            pool.wait_ge(S["g_moved"], 134)
            pool.dma_start(io["gwt"], stage[:, 0, 0:8 * P]).then_inc(st_l[0], 16)

            def store_tail(b):
                pool.wait_ge(S["gelu_done"], HOT_U + b + 1)
                pool.dma_start(io["zs"][HOT_U + b], ztail[:, b % 2, :]).then_inc(zst[b % 2], 16)
            store_tail(0)
            store_tail(1)
            pool.wait_ge(st_l[0], 80)
            pool.wait_ge(st_l[1], 64)
            pool.wait_ge(zst[0], 16 * HOT_U // 2)
            pool.wait_ge(zst[1], 16 * HOT_U // 2)
            pool.wait_ge(S["g_ready"], 134)

            def load_g(s, par_):
                w = EXP_J * TC
                pool.dma_start(gr[:, par_, 0:8 * w].rearrange("p (c w) -> p c w", w=w),
                               io["gw"][:, :, bass.ds(s * w, w)].rearrange("c i w -> i c w")).then_inc(g_l[par_], 16)
                pool.dma_start(gr[:, par_, 8 * w:8 * w + 8 * EXP_J],
                               io["gwt"][:, bass.ds(s * (8 * EXP_J), 8 * EXP_J)]).then_inc(gt_l[par_], 16)

            def load_z(s, jj):
                pool.dma_start(zbuf[:, jj % 2, :], io["zs"][s * EXP_J + jj]).then_inc(zl[jj % 2], 16)

            def load_step(s, par_):
                for jj in range(EXP_J):
                    pool.wait_ge(S["a_ready"], s * EXP_J + (jj - 1))
                    load_z(s, jj)
                    if jj == 1:
                        load_g(s + 1, 1 - par_)
            load_g(0, 0)
            load_z(0, 0)
            load_z(0, 1)
            for b in range(2, TAIL_U - 2):
                store_tail(b)
            for jj in range(2, EXP_J):
                pool.wait_ge(S["a_ready"], jj - 1)
                load_z(0, jj)
            for b in range(TAIL_U - 2, TAIL_U):
                store_tail(b)
            pool.wait_ge(zst[0], 16 * SPILL // 2)
            pool.wait_ge(zst[1], 16 * SPILL // 2)
            load_g(1, 1)
            with pool.Fori(0, SPILL_G // 2) as it:
                load_step(it * 2 + 1, 1)
                load_step(it * 2 + 2, 0)
            with pool.Fori(0, (GROUPS - SPILL_G - 1) // 2) as it:
                pool.wait_ge(S["a_ready"], it * 8 + (SPILL_G * EXP_J + 4))
                load_g(it * 2 + (SPILL_G + 1), 0)
                pool.wait_ge(S["a_ready"], it * 8 + (SPILL_G * EXP_J + 8))
                load_g(it * 2 + (SPILL_G + 2), 1)

        @block.tensor
        def _(pe):
            mm = pe.matmul

            def two(b, lhs, rhs_k, ks):
                for n, k in enumerate(ks):
                    for h in range(2):
                        last = mm(ps[:, b + h, 0:HALF], lhs(k), rhs_k(k)[:, h * HALF:(h + 1) * HALF],
                                  start=(n == 0), stop=(n == len(ks) - 1))
                return last

            pe.wait_ge(S["table_loaded"], 64)
            pe.wait_ge(S["rb_ready"], 1)
            mm(ps[0:NH, 0, 0:512], rb[0:33], ohd[0:33, 513:1025], start=True, stop=True)
            mm(ps[0:NH, 1, 0:128], rb[0:33], ohd[0:33, 1025:1153], start=True, stop=True).then_inc(S["rs_ready"], 1)
            for i in range(4):
                for n in range(NCMP_P):
                    st = 511 + P * i - 16 * n - 31
                    last = mm(ps[:, 2 + i // 2, (i % 2) * 248 + n * NH:(i % 2) * 248 + (n + 1) * NH],
                              oha[0:33, st:st + P], rb[0:33], start=True, stop=True)
            last.then_inc(S["pb_ready"], 1)

            pe.wait_ge(S["silu_done"], 1)
            pe.wait_ge(S["memset_done"], 1)

            def turn_m9(n):
                pe.wait_ge(S["m9_ready"], n + 1)
                if n >= 2:
                    pe.wait_ge(S["mt_done"], n - 1)
                for q in range(AW // P):
                    last = pe.transpose(ps[:, 6 + n % 2, q * 9:(q + 1) * 9], m9[0:9, n % 2, q * P:(q + 1) * P],
                                        ident[0:9, 0:9])
                last.then_inc(S["mt_ready"], 1)
            for n in range(AN):
                pe.wait_ge(ada_l[n % 2], 16 * (n // 2 + 1))
                if n >= 2:
                    pe.wait_ge(S["m9_ready"], n - 1)
                for k in range(KD):
                    last = mm(ps[0:9, 4 + n % 2, 0:AW], cT[:, k, :], ada[:, (n % 2) * KD + k, :],
                              start=(k == 0), stop=(k == KD - 1))
                last.then_inc(S["ada_ready"], 1)
                if n >= 1:
                    turn_m9(n - 1)
            turn_m9(AN - 1)

            pe.wait_ge(S["sq_done"], 1)
            pe.wait_ge(S["rs_copied"], 1)
            two(0, lambda k: ones[:, :], lambda k: hT[:, k, :], range(KD)).then_inc(S["sum_ready"], 1)

            pe.wait_ge(S["h_ready"], 1)
            for n in range(ZC):
                pe.wait_ge(w_l[n % 3], 16 * (n // 3 + 1))
                if n >= 3:
                    pe.wait_ge(S["z_moved"], n - 2)
                two(2 * (n % 3), lambda k: win_w[:, (n % 3) * KD + k, :], lambda k: hT[:, k, :],
                    range(KD)).then_inc(S["z_ready"], 1)
            pe.wait_ge(S["wgate_loaded"], 16)
            for t in range(5):
                m = P if t < 4 else NB
                for k in range(KD):
                    last = mm(ps[0:m, 6, t * 24:(t + 1) * 24], hT[:, k, t * P:t * P + m], wgate[:, k, :],
                              start=(k == 0), stop=(k == KD - 1))
            last.then_inc(S["zg_ready"], 1)

            pe.wait_ge(S["lruw_loaded"], 32)
            pe.wait_ge(S["z_moved"], ZC)
            for c in range(4):
                pe.wait_ge(S["xc_ready"], c + 1)
                if c >= 2:
                    pe.wait_ge(S["ri_ready"], c - 1)
                b = 4 * (c % 2)
                if b == 4:
                    pe.wait_ge(S["gates_ready"], 1)
                for w in range(2):
                    last = two(b + 2 * w, lambda k: wlru[:, 4 * w + c, :], lambda k: xcT[:, c, :], [0])
                last.then_inc(S["gate_ready"], 1)
            pe.wait_ge(S["ri_ready"], 4)

            for c in range(2):
                if c == 0:
                    pe.wait_ge(S["w1k_loaded"], 32)
                    pe.wait_ge(S["pos_loaded"], 16)
                    pe.wait_ge(S["gather_k"], 16 * NB * PAGES)
                else:
                    pe.wait_ge(S["w1v_loaded"], 32)
                    pe.wait_ge(S["pos2_loaded"], 16)
                    pe.wait_ge(S["gather_v"], 16 * NB * PAGES)
                pe.wait_ge(S["x_filled"], c + 1)
                xv = X.rearrange("p (n s) -> p n s", s=16)
                for h, (c0, n) in enumerate(((0, 273), (273, 272))):
                    for ms in range(32):
                        m, s = ms // 16, ms % 16
                        last = mm(ps[:, h, 0:n], w1[:, ms, :], xv[:, c0 + m:c0 + m + n, s],
                                  start=(ms == 0), stop=(ms == 31))
                last.then_inc(S["hid_ready"], 1)
                pe.wait_ge(S["gelu_ready"], c + 1)
                pe.wait_ge(S["w2_loaded"], 64)
                if c == 0:
                    for h in range(2):
                        last = mm(ps[:, 2 + h, 0:272], w2[:, 0, :], hid[:, h * 272:(h + 1) * 272],
                                  start=True, stop=True)
                    last.then_inc(S["ck_ready"], 1)
                else:
                    for b in range(9):
                        m = NCMP_S if b < 8 else NCMP_P
                        last = mm(ps[0:m, 4 + b // 4, (b % 4) * P:(b % 4 + 1) * P], hid[:, b * 64:b * 64 + m],
                                  w2[:, 1, :], start=True, stop=True)
                    last.then_inc(S["ck_ready"], 1)

            pe.wait_ge(S["lru_ready"], 1)
            two(2, lambda k: ones[:, :], lambda k: aT[:, k, :], range(4)).then_inc(S["mix_sum"], 1)

            for br in range(2):
                for kb in range(4):
                    pe.transpose(ps[:, br, kb * P:(kb + 1) * P], zT[:, (VS, VW)[br], kb * P:(kb + 1) * P], ident[:, :])
            pe.wait_ge(S["cmp_done"], 1)
            for br in range(2):
                last = pe.transpose(ps[0:NB, 6, 64 + br * P:64 + (br + 1) * P], zT[:, (VS, VW)[br], SEQ:TOK], ident[:, :])
            last.then_inc(S["vt_ready"], 1)

            pe.wait_ge(S["vt_done"], 1)
            pe.wait_ge(S["qpad_ready"], 1)
            for b in range(NB):
                mm(ps[0:ROWS, 7, 0:NCMP_S], qpad[:, b, :], ckT[:, b * 64:b * 64 + NCMP_S], start=(b == 0), stop=False)
            mm(ps[0:ROWS, 7, 0:NCMP_S], rbx[0:33], ohd[0:33, 31:31 + 16 * (NCMP_S - 1) + 1:16],
               start=False, stop=True).then_inc(S["sc_ready"], 1)
            pe.wait_ge(S["gather_s"], 16 * NB * PAGES)
            for h in range(2):
                for b in range(NB):
                    mm(ps[0:ROWS, h, 0:512], qpad[:, b, :], sel[:, b * 8 + h * 4:b * 8 + h * 4 + 4, 0:P],
                       start=(b == 0), stop=False)
                mm(ps[0:ROWS, h, 0:512], rbx[0:33], ohd[0:33, h * 512:(h + 1) * 512], start=False, stop=True)
            mm(ps[0:ROWS, 2, 0:NB], qs, zT[:, KS, SEQ:TOK], start=True, stop=False)
            mm(ps[0:ROWS, 2, 0:NB], rbx[0:33], ohd[0:33, 1153:1161], start=False, stop=True).then_inc(S["ss_ready"], 1)
            pe.wait_ge(S["sc_soft"], 1)
            mm(ps[0:ROWS, 5, 0:NCMP_S], gsum[0:ROWS], gs[0:ROWS, 0:NCMP_S], start=True, stop=True).then_inc(S["sum_done"], 1)
            pe.wait_ge(S["ss_p"], 1)
            pe.transpose(ps[0:NCMP_S, 3, 0:ROWS], sc[0:ROWS, 0:NCMP_S], ident[0:ROWS, 0:ROWS])
            pe.transpose(ps[0:NB, 3, ROWS:2 * ROWS], ss[0:ROWS, 1024:1032], ident[0:ROWS, 0:ROWS])
            for kb in range(8):
                last = pe.transpose(ps[:, 4, kb * ROWS:(kb + 1) * ROWS], ss[0:ROWS, kb * P:(kb + 1) * P], ident[0:ROWS, 0:ROWS])
            last.then_inc(S["pts_ready"], 1)
            pe.wait_ge(S["pts_done"], 1)
            for b in range(NB):
                r = slice(b * NH, (b + 1) * NH)
                mm(ps[:, 6, r], vc[0:NCMP_S, b, :], pts[0:NCMP_S, 0, r], start=True, stop=False)
                mm(ps[:, 6, r], vnew[0:NB, 0, :], pts[0:NB, 1, r], start=False, stop=False)
                for kb in range(8):
                    last = mm(ps[:, 6, r], sel[:, b * 8 + kb, P:2 * P], pts[:, 2 + kb, r], start=False, stop=(kb == 7))
            last.then_inc(S["sel_free"], 1)
            pe.wait_ge(S["win_loaded"], 32)
            pe.wait_ge(S["ohw_loaded"], 16)
            for b in range(NB):
                mm(ps[0:ROWS, 0, 0:512], qpad[:, b, :], kwin[:, b, :], start=(b == 0), stop=False)
            mm(ps[0:ROWS, 0, 0:512], rbx[0:33], ohw[0:33], start=False, stop=True)
            mm(ps[0:ROWS, 1, 0:NB], qs, zT[:, KW, SEQ:TOK], start=True, stop=False)
            mm(ps[0:ROWS, 1, 0:NB], rbx[0:33], ohd[0:33, 1153:1161], start=False, stop=True).then_inc(S["sw_ready"], 1)
            pe.wait_ge(S["sw_p"], 1)
            pe.transpose(ps[0:NB, 2, 0:ROWS], sw[0:ROWS, 512:520], ident[0:ROWS, 0:ROWS])
            for kb in range(4):
                last = pe.transpose(ps[:, 3, kb * ROWS:(kb + 1) * ROWS], sw[0:ROWS, kb * P:(kb + 1) * P], ident[0:ROWS, 0:ROWS])
            last.then_inc(S["ptw_ready"], 1)
            pe.wait_ge(S["ptw_done"], 1)
            for b in range(NB):
                r = slice(b * NH, (b + 1) * NH)
                mm(ps[:, 7, r], vnew[0:NB, 1, :], pts[0:NB, 10, r], start=True, stop=False)
                for kb in range(4):
                    last = mm(ps[:, 7, r], vwin[:, b * 4 + kb, :], pts[:, 11 + kb, r], start=False, stop=(kb == 3))
            last.then_inc(S["os_ready"], 1)
            pe.wait_ge(S["os_done"], 1)

            def scores(u):
                i, br, g = units[u]
                nk = (i + 1) * P
                for r in range(GRP):
                    if u >= 1:
                        pe.wait_ge(S["u_ttr"], GRP * (u - 1) + r + 1)
                    mm(ps[:, r, 0:nk], qz[:, g * GRP + r, i * P:(i + 1) * P], zT[:, (KS, KW)[br], 0:nk],
                       start=True, stop=True).then_inc(S["u_s"], 1)

            def compressed(i):
                u = 4 * i
                if u >= 1:
                    pe.wait_ge(S["u_ttr"], GRP * u)
                for h in range(NH):
                    last = mm(ps[:, 0, h * NCMP_P:(h + 1) * NCMP_P], qz[:, h, i * P:(i + 1) * P],
                              ckT[:, 512:512 + NCMP_P], start=True, stop=True)
                last.then_inc(S["pc_s"], 1)
                pe.wait_ge(S["pc_p"], i + 1)
                if u >= 1:
                    pe.wait_ge(S["u_tdone"], sum(units[v][0] + 1 for v in range(u)))
                for h in range(NH):
                    last = pe.transpose(ps[0:NCMP_P, 4 + h // 4, (h % 4) * P:(h % 4 + 1) * P],
                                        pcb[:, h * NCMP_P:(h + 1) * NCMP_P], ident[:, :])
                last.then_inc(S["pc_t"], 1)
                pe.wait_ge(S["pc_tdone"], i + 1)
                if i:
                    pe.wait_ge(S["o_done"], i)
                for g in range(2):
                    mm(ps[:, 6 + g, 0:512], vc[0:NCMP_P, 8, :], ptcb[0:NCMP_P, g * 512:(g + 1) * 512],
                       start=True, stop=False)

            tcount = [0]

            def apply(u):
                i, br, g = units[u]
                pe.wait_ge(S["u_p"], GRP * (u + 1))
                for kb in range(i + 1):
                    n = tcount[0]
                    if n >= 2:
                        pe.wait_ge(S["u_tdone"], n - 1)
                    for r in range(GRP):
                        last = pe.transpose(ps[:, 4 + n % 2, r * P:(r + 1) * P],
                                            pbuf[:, (u % 2) * GRP + r, kb * P:(kb + 1) * P], ident[:, :])
                    last.then_inc(S["u_t"], 1)
                    tcount[0] += 1
                for kb in range(i + 1):
                    pe.wait_ge(S["u_tdone"], tcount[0] - i + kb)
                    last = mm(ps[:, 6 + g, 0:512], vn[:, br * 4 + kb, :], ptb[:, kb, :],
                              start=False, stop=(br == 1 and kb == i))
                last.then_inc(S["u_pv"], 1)

            for i in range(4):
                compressed(i)
                scores(4 * i)
                for q in range(4):
                    u = 4 * i + q
                    if q < 3:
                        scores(u + 1)
                    apply(u)

            pe.wait_ge(S["mix_sq"], 1)
            two(0, lambda k: ones[:, :], lambda k: hT[:, k, :], range(4)).then_inc(S["mix_sum"], 1)
            pe.wait_ge(S["mix_ready"], 1)
            pe.wait_ge(S["wout_loaded"], 16)
            for c in range(KD):
                if c >= 3:
                    pe.wait_ge(S["proj_ready"], c - 2)
                two(2 + 2 * (c % 3), lambda k: wout[:, k, c * P:(c + 1) * P], lambda k: zT[:, k, :],
                    range(KD)).then_inc(S["pe_step"], 1)
            pe.wait_ge(S["sq_done"], 2)
            two(0, lambda k: ones[:, :], lambda k: h2T[:, k, :], range(KD)).then_inc(S["sum_ready"], 1)

            pe.wait_ge(S["h_ready"], 2)
            pe.wait_ge(S["sk_loaded"], 16)

            def products(b, weights, moving, ks, first=True, stop=True):
                for n, k in enumerate(ks):
                    for w, m in ((0, 0), (0, 1), (1, 0)):
                        for h in range(2):
                            last = mm(ps[:, b + h, 0:HALF], weights[w](k), moving[m](k)[:, h * HALF:(h + 1) * HALF],
                                      start=(first and n == 0 and w == 0 and m == 0),
                                      stop=(stop and n == len(ks) - 1 and w == 1))
                return last

            def up(blk, slot, item, b, moved, part=0, parts=1):
                if part == 0:
                    pe.wait_ge(S["lo_done"], item + 1)
                    if moved is not None:
                        pe.wait_ge(S["gelu_done"], moved)
                n = KD // parts
                last = products(b, [lambda k: uh[:, slot * KD + k, :], lambda k: ul[:, slot * KD + k, :]],
                                [lambda k: hh[:, k, :], lambda k: hl[:, k, :]], range(n * part, n * part + n),
                                part == 0, part == parts - 1)
                if part == parts - 1:
                    last.then_inc(S["zz_ready"], 1)

            def up_topk(b):
                up(b, b % 2, b, 2, b if b else None)

            def sub_scores(n):
                pe.wait_ge(S["q_moved"], n + 1)
                if n >= 2:
                    pe.wait_ge(S["s_free"], n - 1)
                b = 4 + 2 * (n % 2)
                for t in range(5):
                    m = P if t < 4 else NB
                    last = mm(ps[0:m, b + t // 4, (t % 4) * P:(t % 4 + 1) * P], qT[:, t * P:t * P + m],
                              sk[:, n, :], start=True, stop=True)
                last.then_inc(S["s_ready"], 1)
            for n in range(16):
                pe.wait_ge(wq_l[n % 3], 16 * (n // 3 + 1))
                if n >= 1:
                    pe.wait_ge(S["q_moved"], n)
                two(0, lambda k: wq[:, (n % 3) * KD + k, :], lambda k: h2T[:, k, :],
                    range(KD)).then_inc(S["q_ready"], 1)
                up_topk(n)
                sub_scores(n)
            for t in range(5):
                m = P if t < 4 else NB
                for q in range(TILE_U[t]):
                    up_topk(16 + sum(TILE_U[:t]) + q)
                pe.wait_ge(S["tr_in"], t + 1)
                if t == 0:
                    pe.wait_ge(S["s_free"], 16)
                for q in range(3):
                    last = pe.transpose(ps[:, 4 + q, 0:m], isel[0:m, q, :], ident[0:m, 0:m])
                last.then_inc(S["tr_ready"], 1)

            pe.wait_ge(S["tr_done"], 5)
            pe.sem_inc(S["g_ready"], 4)

            def quad(n, q):
                pe.wait_ge(S["oh_ready"], n * 8 + 8)
                pe.wait_ge(S["g_moved"], n + 1)
                for t in range(4):
                    last = mm(ps[:, 4 + q, t * P:(t + 1) * P], oh[:, q * 4 + t, 0:P], oh[:, q * 4 + t, P:2 * P],
                              start=True, stop=True)
                last.then_inc(S["g_ready"], 1)
            with pe.Fori(0, 4) as it:
                for b in range(8):
                    blk = it * 8 + (TOPK_U + b)
                    for q in range(4):
                        quad(it * 32 + (4 * b + q), q)
                        up(blk, b % 2, blk, 2 * (b % 2), blk - 1, q, 4)
            for q in range(2):
                quad(128 + q, q)
            for b in range(TAIL_U):
                blk = HOT_U + b
                up(blk, b % 2, blk, 2 * (b % 2), blk - 1)
            pe.wait_ge(S["g_moved"], 134)

            def up_live(s, jj):
                blk = s * EXP_J + jj
                up(blk, jj % 2, (s - SPILL_G) * 8 + (2 * SPILL + jj), 2 * (jj % 2), blk - 1)

            def down(s, par_, item):
                pe.wait_ge(S["lo_done"], item)
                pe.wait_ge(S["a_ready"], (s + 1) * EXP_J)
                for dc in range(KD):
                    pe.wait_ge(S["ff_free"], s * KD + dc + 1)
                    cols = slice(dc * P, (dc + 1) * P)
                    products(4 + 2 * (dc % 2), [lambda j: vh[:, par_ * EXP_J + j, cols], lambda j: vl[:, par_ * EXP_J + j, cols]],
                             [lambda j: ah[:, par_ * EXP_J + j, :], lambda j: al[:, par_ * EXP_J + j, :]],
                             range(EXP_J)).then_inc(S["ff_ready"], 1)

            pe.sem_inc(S["ff_ready"], 1)
            with pe.Fori(0, SPILL_G // 2) as it:
                for q in range(2):
                    down(it * 2 + q, q, it * 8 + (SPILL + 4 * (q + 1)))
            with pe.Fori(0, (GROUPS - SPILL_G - 1) // 2) as it:
                for q in range(2):
                    s = it * 2 + (SPILL_G + q)
                    for jj in range(EXP_J):
                        up_live(s, jj)
                    down(s - 1, q, it * 16 + (2 * SPILL + 8 * q))
            last = GROUPS - 1
            for jj in range(EXP_J):
                up_live(last, jj)
            down(last - 1, 0, 2 * SPILL + 8 * (last - SPILL_G))
            down(last, 1, 2 * SPILL + 8 * (last - SPILL_G + 1))
            pe.wait_ge(S["sq_done"], 3)
            two(0, lambda k: ones[:, :], lambda k: sq[:, k, :], range(KD)).then_inc(S["sum_ready"], 1)

        @block.scalar
        def _(act):
            steps = [0]

            def link(ins):
                steps[0] += 1
                ins.then_inc(S["act_step"], 1)
                act.wait_ge(S["act_step"], steps[0])

            def fn(out, in_, f, **kw):
                return act.activation(out, in_, f, **kw)

            act.wait_ge(S["c_loaded"], 16)
            fn(cT, cT, ACT.Silu).then_inc(S["silu_done"], 1)
            act.wait_ge(S["rs_ready"], 1)
            act.wait_ge(S["silu_done"], 1)
            link(fn(rsb[0:NH, 0:512], ps[0:NH, 0, 0:512], ACT.Copy))
            fn(rsb[0:NH, 512:640], ps[0:NH, 1, 0:128], ACT.Copy).then_inc(S["rs_copied"], 1)
            for n in range(AN):
                act.wait_ge(S["ada_ready"], n + 1)
                if n >= 2:
                    act.wait_ge(S["mt_ready"], n - 1)
                fn(m9[0:9, n % 2, :], ps[0:9, 4 + n % 2, 0:AW], ACT.Copy).then_inc(S["m9_ready"], 1)
                if n == 1:
                    act.wait_ge(S["x_loaded"], 16)
                    fn(hT, xT[:, :, :], ACT.Square).then_inc(S["sq_done"], 1)

            def root(n):
                act.wait_ge(S["root_in"], n)
                fn(rstd, rstd, ACT.Sqrt).then_inc(S["rstd_ready"], 1)
            root(1)
            for n in range(1, ZC, 2):
                act.wait_ge(S["z_ready"], n + 1)
                act.wait_ge(S["z_moved"], n)
                b = 2 * (n % 3)
                fn(zT[:, n, :].rearrange("p (h t) -> p h t", h=2), ps[:, b:b + 2, 0:HALF], ACT.Copy,
                   scale=0.125 if QC <= n < QC + 4 else 1.0).then_inc(S["z_moved"], 1)
            act.wait_ge(S["zg_ready"], 1)
            link(fn(gates[:, 0:4, :], ps[:, 6, 0:96].rearrange("p (t c) -> p t c", c=24), ACT.Sigmoid))
            fn(gates[0:NB, 4, :].rearrange("p (h r) -> p h r", r=3),
               ps[0:NB, 6, 96:120].rearrange("p (r h) -> p h r", h=NH), ACT.Sigmoid).then_inc(S["gates_ready"], 1)
            for c in range(4):
                act.wait_ge(S["gate_ready"], c + 1)
                b = 4 * (c % 2)
                link(fn(rT[:, c, :].rearrange("p (h t) -> p h t", h=2), ps[:, b:b + 2, 0:HALF], ACT.Sigmoid,
                        bias=par[:, BA + c:BA + c + 1]))
                fn(iT_[:, c, :].rearrange("p (h t) -> p h t", h=2), ps[:, b + 2:b + 4, 0:HALF], ACT.Sigmoid,
                   bias=par[:, BI + c:BI + c + 1]).then_inc(S["ri_ready"], 1)
            act.wait_ge(S["lru_prep"], 1)
            fn(lr(1), lr(0), ACT.Exp, scale=-1.0).then_inc(S["exp_ready"], 1)
            act.wait_ge(S["lru_prep"], 2)
            fn(lr(3), lr(2), ACT.Ln).then_inc(S["exp_ready"], 1)
            act.wait_ge(S["lru_prep"], 3)
            act.wait_ge(S["ri_ready"], 4)
            for c in range(4):
                link(fn(aT[:, c, :], rT[:, c, :], ACT.Exp, scale=lr(9)[:, c:c + 1]))
                link(fn(rT[:, c, :], rT[:, c, :], ACT.Tanh, scale=lr(8)[:, c:c + 1]))
            act.sem_inc(S["exp_ready"], 1)
            act.wait_ge(S["z_moved"], ZC)
            fn(zT[:, YG:YG + 4, :], zT[:, YG:YG + 4, :], ACT.Gelu_apprx_tanh).then_inc(S["yg_ready"], 1)
            act.wait_ge(S["lru_prep"], 4)
            fn(rT, rT, ACT.Sqrt).then_inc(S["exp_ready"], 1)
            for c in range(2):
                act.wait_ge(S["hid_ready"], c + 1)
                link(fn(posb[:, :], ps[:, 1, 271:272], ACT.Copy))
                if c == 1:
                    act.wait_ge(S["ck_ready"], 1)
                link(fn(hid[:, 0:273], ps[:, 0, 0:273], ACT.Gelu_apprx_tanh, bias=posb[:, :]))
                fn(hid[:, 273:545], ps[:, 1, 0:272], ACT.Gelu_apprx_tanh, bias=posb[:, :]).then_inc(S["gelu_ready"], 1)
                act.wait_ge(S["ck_ready"], c + 1)
                if c == 0:
                    link(fn(ckT.rearrange("p (h t) -> p h t", h=2), ps[:, 2:4, 0:272], ACT.Copy))
                else:
                    for q in range(2):
                        link(fn(vc[0:NCMP_S, 4 * q:4 * q + 4, :].rearrange("p a b -> p (a b)"), ps[0:NCMP_S, 4 + q, 0:512], ACT.Copy))
                    fn(vc[0:NCMP_P, 8, :], ps[0:NCMP_P, 6, 0:P], ACT.Copy).then_inc(S["cmp_done"], 1)
            act.wait_ge(S["lru_ready"], 1)
            root(2)
            act.wait_ge(S["sc_exp"], 1)
            fn(sc[0:ROWS, 0:NCMP_S], sc[0:ROWS, 0:NCMP_S], ACT.Exp, bias=sm(0), accum_out=sm(1)).then_inc(S["sc_exp"], 1)
            act.wait_ge(S["ss_max"], 1)
            fn(ss[0:ROWS], ss[0:ROWS], ACT.Exp, bias=sm(4), accum_out=sm(5)).then_inc(S["ss_exp"], 1)
            act.wait_ge(S["sw_max"], 1)
            fn(sw[0:ROWS], sw[0:ROWS], ACT.Exp, bias=sm(8), accum_out=sm(9)).then_inc(S["sw_exp"], 1)
            for u, (i, br, g) in enumerate(units):
                if u % 4 == 0:
                    act.wait_ge(S["pc_max"], i + 1)
                    fn(pcb, pcb, ACT.Exp).then_inc(S["pc_exp"], 1)
                nk = (i + 1) * P
                act.wait_ge(S["u_max"], u + 1)
                for r in range(GRP):
                    fn(pbuf[:, (u % 2) * GRP + r, 0:nk], pbuf[:, (u % 2) * GRP + r, 0:nk], ACT.Exp,
                       bias=pst(u, 1)[:, r:r + 1], accum_out=pst(u, 2)[:, r:r + 1]).then_inc(S["u_exp"], 1)
                act.wait_ge(S["u_exp"], GRP * (u + 1))
                act.wait_ge(S["u_rs"], u + 1)
                for r in range(GRP):
                    fn(pbuf[:, (u % 2) * GRP + r, 0:nk], pbuf[:, (u % 2) * GRP + r, 0:nk], ACT.Copy,
                       scale=pst(u, 3)[:, r:r + 1]).then_inc(S["u_p"], 1)
            act.wait_ge(S["o_done"], 4)
            fn(hT[:, 0:4, :], zT[:, 4:8, :], ACT.Square).then_inc(S["mix_sq"], 1)
            root(3)
            act.wait_ge(S["proj_done"], 1)
            fn(h2T, xT[:, :, :], ACT.Square).then_inc(S["sq_done"], 1)
            root(4)
            def high(dst, slot, item_round):
                act.wait_ge(raw_l[slot], item_round * 16)
                fn(dst, raw[:, slot, :], ACT.Copy).then_inc(S["hi_done"], 1)

            def high_u(b, jj, item_round):
                fn_dst = uh[:, (jj % 2) * KD:(jj % 2 + 1) * KD, :].rearrange("p k i -> p (k i)")
                if not isinstance(b, int) or b >= 2:
                    act.wait_ge(S["zz_ready"], b - 1)
                high(fn_dst, jj % 4, item_round)

            def gelu(blk, slot, b, dst=zbuf):
                act.wait_ge(S["zz_ready"], blk + 1)
                fn(dst[:, slot, :].rearrange("p (h t) -> p h t", h=2),
                   ps[:, b:b + 2, 0:HALF], ACT.Gelu_apprx_tanh).then_inc(S["gelu_done"], 1)

            def topk_block(b):
                if b >= 2:
                    act.wait_ge(zst[b % 2], 16 * (b // 2))
                gelu(b, b % 2, 2)
                high_u(b + 2, b + 2, (b + 2) // 4 + 1)
            act.wait_ge(S["h_ready"], 2)
            high_u(0, 0, 1)
            high_u(1, 1, 1)
            for n in range(16):
                act.wait_ge(S["q_ready"], n + 1)
                if n >= 1:
                    act.wait_ge(S["s_ready"], n)
                fn(qT.rearrange("p (h t) -> p h t", h=2), ps[:, 0:2, 0:HALF],
                   ACT.Identity, bias=par[:, BQ + n:BQ + n + 1]).then_inc(S["q_moved"], 1)
                topk_block(n)
            for t in range(5):
                m = P if t < 4 else NB
                for q in range(TILE_U[t]):
                    topk_block(16 + sum(TILE_U[:t]) + q)
                act.wait_ge(S["rexp"], t + 1)
                fn(best[0:m], best[0:m], ACT.Exp).then_inc(S["rexp_done"], 1)
            act.wait_ge(S["tr_done"], 5)
            act.sem_inc(S["g_moved"], 4)

            def move_quad(n, q, dst):
                act.wait_ge(S["g_ready"], n + 5)
                fn(dst, ps[:, 4 + q, 0:512].rearrange("p (t j) -> p j t", j=P), ACT.Copy).then_inc(S["g_moved"], 1)

            def stage_round(it, c, first=False):
                st = stage[:, c, :].rearrange("p (j t) -> p j t", t=TC)
                if not first:
                    act.wait_ge(st_l[c], it * 16)
                for b in range(4):
                    for q in range(4):
                        t0 = 16 * b + 4 * q
                        move_quad(it * 32 + (16 * c + 4 * b + q), q, st[:, :, t0:t0 + 4])
                    blk = it * 8 + (TOPK_U + 4 * c + b)
                    act.wait_ge(zst[b % 2], it * 64 + (8 * (TOPK_U + 4 * c + b - b % 2)))
                    gelu(blk, b % 2, 2 * (b % 2))
                    high_u(blk + 2, b + 2, it * 2 + ((TOPK_U + 4 * c + b + 2) // 4 + 1))
            for c in range(2):
                stage_round(0, c, first=True)
            with act.Fori(1, 4) as it:
                for c in range(2):
                    stage_round(it, c)
            act.wait_ge(st_l[0], 64)
            for q in range(2):
                move_quad(128 + q, q, stage[:, 0, 0:8 * P].rearrange("p (j t) -> p j t", t=8)[:, :, 4 * q:4 * q + 4])

            def high_v(s, par_, jj, item_round):
                high(vh[:, par_ * EXP_J + jj, :], jj, item_round)

            def tail_gelu(b):
                act.wait_ge(zst[b % 2], 16 * ((HOT_U + b) // 2))
                gelu(HOT_U + b, b % 2, 2 * (b % 2), ztail)
            for b in range(TAIL_U - 2):
                tail_gelu(b)
                high_u(HOT_U + b + 2, b + 2, (HOT_U + b + 2) // 4 + 1)
            act.wait_ge(st_l[0], 80)
            act.wait_ge(st_l[1], 64)
            for jj in range(EXP_J):
                high_v(0, 0, jj, SPILL // 4 + 1)
            for b in range(TAIL_U - 2, TAIL_U):
                tail_gelu(b)

            def free_v(s):
                act.wait_ge(S["ff_ready"], (s - 1) * KD + 1)
            with act.Fori(0, SPILL_G // 2) as it:
                for q in range(2):
                    s = it * 2 + (q + 1)
                    free_v(s)
                    for jj in range(EXP_J):
                        high_v(s, 1 - q, jj, it * 2 + (SPILL // 4 + q + 2))
            r0 = 2 * SPILL // 4 + 1
            for jj in range(2):
                high_u(SPILL + jj, jj, r0)

            def live(s, par_, rnd, more):
                for jj in range(EXP_J):
                    blk = s * EXP_J + jj
                    act.wait_ge(S["a_ready"], blk - 1)
                    gelu(blk, jj % 2, 2 * (jj % 2))
                    if jj < 2:
                        high_u(blk + 2, jj + 2, rnd)
                    else:
                        if jj == 2:
                            free_v(s)
                        high_v(s, par_, jj - 2, rnd + 1)
                for jj in range(2, EXP_J):
                    high_v(s, par_, jj, rnd + 1)
                if more:
                    for jj in range(2):
                        high_u((s + 1) * EXP_J + jj, jj, rnd + 2)
            with act.Fori(0, (GROUPS - SPILL_G - 1) // 2) as it:
                for q in range(2):
                    live(it * 2 + (SPILL_G + q), 1 - q, it * 4 + (r0 + 2 * q), True)
            live(GROUPS - 1, 1, r0 + 2 * (GROUPS - 1 - SPILL_G), False)
            root(5)

        @block.vector
        def _(dve):
            steps = [0]

            def link(*group):
                for ins in group:
                    steps[0] += 1
                    ins.then_inc(S["dve_step"], 1)
                dve.wait_ge(S["dve_step"], steps[0])

            tt, ts, cp = dve.tensor_tensor, dve.tensor_scalar, dve.tensor_copy
            stt = dve.scalar_tensor_tensor

            link(dve.memset(ones[:, :], 1.0))
            dve.wait_ge(S["table_loaded"], 64)
            link(dve.memset(rb[32:33], NEG), dve.memset(rbx[32:33], NEG))
            dve.sem_inc(S["rb_ready"], 1)
            dve.wait_ge(S["pb_ready"], 1)
            for q in range(2):
                link(cp(pbias[:, 2 * q:2 * q + 2, :].rearrange("p i (h n) -> p i h n", h=NH),
                        ps[:, 2 + q, 0:496].rearrange("p (i n h) -> p i h n", i=2, h=NH)))
            dve.wait_ge(S["par_loaded"], 32)
            for n in range(AN):
                dve.wait_ge(S["mt_ready"], n + 1)
                tt(mT[:, 3 * n:3 * n + 3, :], ps[:, 6 + n % 2, 0:27].rearrange("p (q c) -> p q c", c=9),
                   par[:, ADB + 3 * n:ADB + 3 * n + 3].to_broadcast([P, 3, 9]), ADD).then_inc(S["mt_done"], 1)
            dve.wait_ge(S["mt_done"], AN)
            for part, gain in ((1, N1G), (4, N2G)):
                v = mT[:, 8 * part:8 * part + 8, :]
                link(ts(v, v, 1.0, None, ADD))
                link(tt(v, v, par[:, gain:gain + 8].to_broadcast([P, 8, 9]), MUL))

            def inverse_ms(width, b):
                r = rstd.rearrange("p (h t) -> p h t", h=2)
                link(ts(r, ps[:, b:b + 2, 0:HALF], 1.0 / width, EPS, MUL, ADD))
                dve.reciprocal(rstd, rstd).then_inc(S["root_in"], 1)

            def modulate(dst, n, part_shift):
                dve.wait_ge(S["sum_ready"], n)
                inverse_ms(D, 0)
                dve.wait_ge(S["rstd_ready"], n if n == 1 else n + 2)
                link(tt(dst, xT[:, :, :], rstd.rearrange("p (o t) -> p o t", o=1).to_broadcast([P, KD, TOK]), MUL))
                sh, scl = mT[:, 8 * part_shift:8 * part_shift + 8, :], mT[:, 8 * part_shift + 8:8 * part_shift + 16, :]
                link(tt(dst[:, :, SEQ:TOK], dst[:, :, SEQ:TOK], scl[:, :, 1:9], MUL))
                link(tt(dst[:, :, SEQ:TOK], dst[:, :, SEQ:TOK], sh[:, :, 1:9], ADD))
                link(*[ts(dst[:, k, 0:SEQ], dst[:, k, 0:SEQ], scl[:, k, 0:1], sh[:, k, 0:1], MUL, ADD)
                       for k in range(KD)])
                dve.sem_inc(S["h_ready"], 1)
            modulate(hT, 1, 0)
            for n in range(0, ZC, 2):
                dve.wait_ge(S["z_ready"], n + 1)
                if n:
                    dve.wait_ge(S["z_moved"], n)
                b = 2 * (n % 3)
                ts(zT[:, n, :].rearrange("p (h t) -> p h t", h=2), ps[:, b:b + 2, 0:HALF],
                   0.125 if QC <= n < QC + 4 else 1.0, None, MUL).then_inc(S["z_moved"], 1)
            dve.wait_ge(S["z_moved"], ZC)
            link(dve.memset(wlru, 0.0))
            dve.sem_inc(S["hi_ready"], 1)
            cp(X[:, 8192:8704], zT[:, KC, 0:SEQ]).then_inc(S["x_filled"], 1)

            dve.wait_ge(S["lrus_loaded"], 32)

            def cw(k, c):
                return par[:, CW + 4 * k + c:CW + 4 * k + c + 1]
            for c in range(4):
                x = zT[:, XR + c, :]
                link(ts(xcT[:, c, :], x, cw(3, c), par[:, CB + c:CB + c + 1], MUL, ADD))
                for k in (2, 1, 0):
                    s = 3 - k
                    link(stt(xcT[:, c, s:SEQ], x[:, 0:SEQ - s], cw(k, c), xcT[:, c, s:SEQ], MUL, ADD),
                         stt(xcT[:, c, SEQ:TOK], stc[:, c, k * NB:(k + 1) * NB], cw(k, c), xcT[:, c, SEQ:TOK], MUL, ADD))
                dve.sem_inc(S["xc_ready"], 1)
            oc = outc.rearrange("p c (k s) -> p c k s", s=9)
            link(cp(oc[:, :, :, 0], zT[:, XR:XR + 4, SEQ - 3:SEQ]),
                 cp(oc[:, :, 0:2, 1:9], stc.rearrange("p c (k s) -> p c k s", s=NB)[:, :, 1:3, :]),
                 cp(oc[:, :, 2, 1:9], zT[:, XR:XR + 4, SEQ:TOK]))
            lam = par[:, LAM:LAM + 4]
            link(ts(lr(0), lam, -1.0, None, MUL))
            link(tt(lr(0), lr(0), lam, MAX))
            dve.sem_inc(S["lru_prep"], 1)
            dve.wait_ge(S["exp_ready"], 1)
            link(ts(lr(2), lr(1), 1.0, None, ADD))
            dve.sem_inc(S["lru_prep"], 1)
            link(ts(lr(4), lr(2), 1.0, None, SUB))
            link(ts(lr(5), lr(4), 0.0, None, EQ))
            link(tt(lr(4), lr(4), lr(5), ADD))
            link(dve.reciprocal(lr(4), lr(4)))
            link(tt(lr(4), lr(4), lr(1), MUL))
            link(tt(lr(5), lr(5), lr(1), MUL))
            dve.wait_ge(S["exp_ready"], 2)
            link(tt(lr(3), lr(3), lr(4), MUL))
            link(tt(lr(3), lr(3), lr(5), ADD))
            link(ts(lr(6), lam, -1.0, 0.0, MUL, MAX))
            link(tt(lr(3), lr(3), lr(6), ADD))
            link(ts(lr(8), lr(3), 8.0, None, MUL), ts(lr(9), lr(3), -8.0, None, MUL))
            dve.sem_inc(S["lru_prep"], 1)
            dve.wait_ge(S["exp_ready"], 3)
            link(ts(uT, rT, 1.0, None, ADD))
            link(dve.reciprocal(uT, uT))
            link(stt(rT, rT, 2.0, uT, MUL, MUL))
            dve.sem_inc(S["lru_prep"], 1)
            link(tt(iT_, iT_, xcT, MUL))
            dve.wait_ge(S["exp_ready"], 4)
            link(tt(uT, rT, iT_, MUL))
            link(*[dve.tensor_tensor_scan(xcT[:, c, 0:SEQ], aT[:, c, 0:SEQ], uT[:, c, 0:SEQ], 0.0, MUL, ADD)
                   for c in range(4)])
            link(tt(xcT[:, :, SEQ:TOK], aT[:, :, SEQ:TOK], h0T, MUL))
            link(tt(xcT[:, :, SEQ:TOK], xcT[:, :, SEQ:TOK], uT[:, :, SEQ:TOK], ADD))
            link(cp(outh, xcT[:, :, SEQ - 1:TOK]))
            dve.wait_ge(S["yg_ready"], 1)
            link(tt(zT[:, 0:4, :], xcT, zT[:, YG:YG + 4, :], MUL))
            link(tt(aT, zT[:, 0:4, :], zT[:, 0:4, :], MUL))
            dve.sem_inc(S["lru_ready"], 1)
            dve.wait_ge(S["hid_ready"], 1)
            cp(X[:, 8192:8704], zT[:, VC_, 0:SEQ]).then_inc(S["x_filled"], 1)
            dve.wait_ge(S["mix_sum"], 1)
            inverse_ms(512, 2)
            dve.wait_ge(S["rstd_ready"], 2)
            link(*[stt(zT[:, c, :], zT[:, c, :], par[:, NLG + c:NLG + c + 1], rstd, MUL, MUL) for c in range(4)])
            dve.wait_ge(S["lru_stored"], 32)
            dve.sem_inc(S["lru_norm"], 1)

            dve.wait_ge(S["x_filled"], 2)
            dve.wait_ge(S["hid_ready"], 2)
            link(dve.memset(qz, 0.0), dve.memset(qpad, 0.0), dve.memset(qs, 0.0))
            qpf = qpad.rearrange("p b r -> p (b r)")
            grp = []
            for g in range(2):
                rows = slice(g * HD, (g + 1) * HD)
                for r in range(GRP):
                    c = g * GRP + r
                    grp.append(cp(qz[rows, c, :], zT[rows, QC + r, 0:SEQ]))
                    grp.append(cp(qs[rows, c:ROWS:NH], zT[rows, QC + r, SEQ:TOK]))
                    grp.append(cp(qpf[rows, c:NB * ROWS:ROWS + NH], zT[rows, QC + r, SEQ:TOK]))
            link(*grp)
            dve.sem_inc(S["qpad_ready"], 1)
            dve.wait_ge(S["vt_ready"], 1)
            grp = []
            for br in range(2):
                grp.append(cp(vn[:, br * 4:(br + 1) * 4, :].rearrange("p k c -> p (k c)"), ps[:, br, 0:512]))
            grp.append(cp(vnew[0:NB].rearrange("p a b -> p (a b)"), ps[0:NB, 6, 64:64 + 2 * P]))
            link(*grp)
            dve.sem_inc(S["vt_done"], 1)

            R = slice(0, ROWS)
            dve.wait_ge(S["const_loaded"], 64)
            dve.wait_ge(S["gate_moved"], 16)
            dve.wait_ge(S["sc_ready"], 1)
            link(cp(sc[R, 0:NCMP_S], ps[R, 7, 0:NCMP_S]))
            link(dve.tensor_reduce(sm(0), sc[R, 0:NCMP_S], AX.X, MAX, negate=True))
            dve.sem_inc(S["sc_exp"], 1)
            dve.wait_ge(S["sc_exp"], 2)
            link(dve.reciprocal(sm(2), sm(1)))
            link(ts(gs[R, 0:NCMP_S], sc[R, 0:NCMP_S], sm(2), None, MUL))
            dve.sem_inc(S["sc_soft"], 1)
            link(ts(sc[R, 0:NCMP_S], gs[R, 0:NCMP_S], gate_rows[:, 0:1], None, MUL))
            dve.wait_ge(S["sum_done"], 1)
            link(cp(gs[R, 0:NCMP_S], ps[R, 5, 0:NCMP_S]))
            bs, flag, pen = small[R, 220:234], small[R, 240:254], small[R, 260:274]

            def cover(t):
                return gs[R, 3 + t:3 + t + 4 * (NSELB - 1) + 1:4]
            link(tt(bs, cover(0), cover(1), ADD))
            for t in range(2, 5):
                link(tt(bs, bs, cover(t), ADD))
            link(dve.tensor_reduce(sm(12), bs, AX.X, MIN))
            link(ts(flag, bs, sm(12), None, EQ))
            link(tt(flag, flag, blkno[R, 0:NSELB], MUL))
            link(dve.tensor_reduce(sm(13), flag, AX.X, MAX))
            link(ts(pen, blkno[R, 0:NSELB], sm(13), NEG, EQ, MUL))
            dve.wait_ge(S["ss_ready"], 1)
            link(cp(ss[R, 0:1024], ps[R, 0:2, 0:512]), tt(ss[R, 1024:1032], ps[R, 2, 0:NB], newmask[R], ADD))
            mid = ss[R, 64:64 + NSELB * 64].rearrange("p (j s) -> p j s", s=64)
            link(tt(mid, mid, pen.to_broadcast([ROWS, NSELB, 64]), ADD))
            link(dve.tensor_reduce(sm(4), ss[R, 0:1032], AX.X, MAX, negate=True))
            dve.sem_inc(S["ss_max"], 1)
            dve.wait_ge(S["ss_exp"], 1)
            link(dve.reciprocal(sm(6), sm(5)))
            link(tt(sm(6), sm(6), gate_rows[:, 1:2], MUL))
            link(ts(ss[R, 0:1032], ss[R, 0:1032], sm(6), None, MUL))
            dve.sem_inc(S["ss_p"], 1)
            dve.wait_ge(S["pts_ready"], 1)
            link(cp(pts[0:NCMP_S, 0, :], ps[0:NCMP_S, 3, 0:ROWS]), cp(pts[0:NB, 1, :], ps[0:NB, 3, ROWS:2 * ROWS]),
                 cp(pts[:, 2:10, :].rearrange("p a b -> p (a b)"), ps[:, 4, 0:512]))
            dve.sem_inc(S["pts_done"], 1)
            dve.wait_ge(S["sw_ready"], 1)
            link(cp(sw[R, 0:512], ps[R, 0, 0:512]), tt(sw[R, 512:520], ps[R, 1, 0:NB], newmask[R], ADD))
            link(dve.tensor_reduce(sm(8), sw[R, 0:520], AX.X, MAX, negate=True))
            dve.sem_inc(S["sw_max"], 1)
            dve.wait_ge(S["sw_exp"], 1)
            link(dve.reciprocal(sm(10), sm(9)))
            link(tt(sm(10), sm(10), gate_rows[:, 2:3], MUL))
            link(ts(sw[R, 0:520], sw[R, 0:520], sm(10), None, MUL))
            dve.sem_inc(S["sw_p"], 1)
            dve.wait_ge(S["ptw_ready"], 1)
            link(cp(pts[0:NB, 10, :], ps[0:NB, 2, 0:ROWS]),
                 cp(pts[:, 11:15, :].rearrange("p a b -> p (a b)"), ps[:, 3, 0:256]))
            dve.sem_inc(S["ptw_done"], 1)
            dve.wait_ge(S["os_ready"], 1)
            grp, grp2 = [], []
            for g in range(2):
                rows = slice(g * HD, (g + 1) * HD)
                o_ = ps[rows, 6:8, 0:ROWS].rearrange("p a (b g r) -> p a g r b", g=2, r=GRP)
                dst = zT[rows, 4:8, SEQ:TOK]
                grp.append(cp(dst, o_[:, 0, g]))
                grp2.append((dst, o_[:, 1, g]))
            link(*grp)
            link(*[tt(a, a, b, ADD) for a, b in grp2])
            dve.sem_inc(S["os_done"], 1)

            dve.wait_ge(S["bias_loaded"], 16)

            def ttr(u):
                i, br, g = units[u]
                nk = (i + 1) * P
                if u >= 2:
                    dve.wait_ge(S["u_t"], sum(units[v][0] + 1 for v in range(u - 1)))
                for r in range(GRP):
                    dve.wait_ge(S["u_s"], GRP * u + r + 1)
                    dve.tensor_tensor_reduce(pbuf[:, (u % 2) * GRP + r, 0:nk], ps[:, r, 0:nk],
                                             biasT[:, g * GRP + r, 384 - P * i:384 - P * i + nk],
                                             1.0, -3e38, ADD, MAX, pst(u, 0)[:, r:r + 1]).then_inc(S["u_ttr"], 1)
                dve.wait_ge(S["u_ttr"], GRP * (u + 1))
                ts(pst(u, 1), pst(u, 0), -1.0, None, MUL).then_inc(S["u_max"], 1)

            def scale(u):
                i, br, g = units[u]
                dve.wait_ge(S["u_exp"], GRP * (u + 1))
                link(dve.reciprocal(pst(u, 3), pst(u, 2)))
                h = (br + 1) * NH + g * GRP
                tt(pst(u, 3), pst(u, 3), gates[:, i, h:h + GRP], MUL).then_inc(S["u_rs"], 1)

            tcount = [0]

            def evac(u):
                for kb in range(units[u][0] + 1):
                    tcount[0] += 1
                    dve.wait_ge(S["u_t"], tcount[0])
                    if u >= 1:
                        dve.wait_ge(S["u_pv"], u)
                    cp(ptb[:, kb, :], ps[:, 4 + (tcount[0] - 1) % 2, 0:512]).then_inc(S["u_tdone"], 1)

            for i in range(4):
                dve.wait_ge(S["pc_s"], i + 1)
                pv3 = pcb.rearrange("p (h n) -> p h n", h=NH)
                link(tt(pcb, ps[:, 0, 0:NH * NCMP_P], pbias[:, i, :], ADD))
                link(dve.tensor_reduce(pcm(0), pv3, AX.X, MAX))
                link(tt(pv3, pv3, pcm(0).to_broadcast([P, NH, NCMP_P]), SUB))
                dve.sem_inc(S["pc_max"], 1)
                dve.wait_ge(S["pc_exp"], i + 1)
                link(dve.tensor_reduce(pcm(1), pv3, AX.X, ADD))
                link(dve.reciprocal(pcm(1), pcm(1)))
                link(tt(pcm(1), pcm(1), gates[:, i, 0:NH], MUL))
                if i == 0:
                    link(ts(pcm(1), pcm(1), validq, None, MUL))
                link(tt(pv3, pv3, pcm(1).to_broadcast([P, NH, NCMP_P]), MUL))
                dve.sem_inc(S["pc_p"], 1)
                dve.wait_ge(S["pc_t"], i + 1)
                link(*[cp(ptcb[0:NCMP_P, q * 512:(q + 1) * 512], ps[0:NCMP_P, 4 + q, 0:512]) for q in range(2)])
                dve.sem_inc(S["pc_tdone"], 1)
                ttr(4 * i)
                for q in range(4):
                    u = 4 * i + q
                    scale(u)
                    if q < 3:
                        ttr(u + 1)
                    evac(u)
                dve.wait_ge(S["u_pv"], 4 * i + 4)
                link(*[cp(zT[g * HD:(g + 1) * HD, 4:8, i * P:(i + 1) * P],
                          ps[g * HD:(g + 1) * HD, 6 + g, 0:512].rearrange("p (r q) -> p r q", q=P)) for g in range(2)])
                dve.sem_inc(S["o_done"], 1)
            dve.wait_ge(S["mix_sum"], 2)
            inverse_ms(512, 0)
            dve.wait_ge(S["rstd_ready"], 3)
            link(*[stt(zT[:, 4 + c, :], zT[:, 4 + c, :], par[:, NAG + c:NAG + c + 1], rstd, MUL, MUL) for c in range(4)])
            dve.sem_inc(S["mix_ready"], 1)

            def add_gated(x, c, src0, src1, part):
                gcol = mT[:, 8 * part + c, :]
                link(*[stt(x[:, c, a:b], s, gcol[:, 0:1], x[:, c, a:b], MUL, ADD) for a, b, s in src0])
                link(tt(small[:, 0:NB], src1, gcol[:, 1:9], MUL))
                link(tt(x[:, c, SEQ:TOK], x[:, c, SEQ:TOK], small[:, 0:NB], ADD))
            for c in range(KD):
                dve.wait_ge(S["pe_step"], c + 1)
                b = 2 + 2 * (c % 3)
                add_gated(xT, c, [(0, HALF, ps[:, b, 0:HALF]), (HALF, SEQ, ps[:, b + 1, 0:SEQ - HALF])],
                          ps[:, b + 1, SEQ - HALF:HALF], 2)
                dve.sem_inc(S["proj_ready"], 1)
            dve.sem_inc(S["proj_done"], 1)
            dve.wait_ge(S["kv_stored"], 16)
            modulate(h2T, 2, 3)
            link(cp(hh[:, :, :], h2T))
            link(tt(hl[:, :, :], h2T, hh[:, :, :].bitcast(F32), SUB))

            def low(dst, hi, slot, item):
                dve.wait_ge(S["hi_done"], item + 1)
                tt(dst, raw[:, slot, :], hi.bitcast(F32), SUB).then_inc(S["lo_done"], 1)

            def low_u(jj, item):
                r = slice((jj % 2) * KD, (jj % 2 + 1) * KD)
                low(ul[:, r, :].rearrange("p k i -> p (k i)"), uh[:, r, :].rearrange("p k i -> p (k i)"), jj % 4, item)

            def low_v(par_, jj, item):
                low(vl[:, par_ * EXP_J + jj, :], vh[:, par_ * EXP_J + jj, :], jj, item)
            low_u(0, 0)
            low_u(1, 1)

            for n in range(16):
                dve.wait_ge(S["s_ready"], n + 1)
                b = 4 + 2 * (n % 2)
                tiles = []
                for t in range(5):
                    m = P if t < 4 else NB
                    tiles.append((slice(0, m), t, ps[0:m, b + t // 4, (t % 4) * P:(t % 4 + 1) * P]))
                link(*[dve.max(sv[r, 16 * t + n, 0:8], s) for r, t, s in tiles])
                link(*[dve.max_index(si[r, 16 * t + n, 0:8], sv[r, 16 * t + n, 0:8], s) for r, t, s in tiles])
                link(*[dve.match_replace(tmpk[r, t, :], sv[r, 16 * t + n, 0:8], s, -3e38) for r, t, s in tiles])
                dve.sem_inc(S["s_free"], 1)
                link(*[dve.max(sv[r, 16 * t + n, 8:16], tmpk[r, t, :]) for r, t, s in tiles])
                low_u(n + 2, n + 2)
                link(*[dve.max_index(si[r, 16 * t + n, 8:16], sv[r, 16 * t + n, 8:16], tmpk[r, t, :]) for r, t, s in tiles])
            dve.wait_ge(S["bias_ready"], 2)
            for t in range(5):
                r = slice(0, P if t < 4 else NB)
                m = r.stop

                def split_next(point):
                    n = TILE_U[t] - (2 if t == 4 else 0)
                    for q in range(n):
                        if q * 8 // n == point:
                            item = 18 + sum(TILE_U[:t]) + q
                            low_u(item, item)
                link(cp(sif[r, 16 * t:16 * t + 16, :], si[r, 16 * t:16 * t + 16, :]))
                s0, s1 = sv[r, 16 * t:16 * t + 16:2, :], sv[r, 16 * t + 1:16 * t + 16:2, :]
                link(*[tt(cand[r, h, :].rearrange("p (a b) -> p a b", a=16), s0[:, h, :].to_broadcast([m, 16, 16]),
                          s1[:, h, :].rearrange("p (o b) -> p o b", o=1).to_broadcast([m, 16, 16]), ADD) for h in range(NH)])
                split_next(0)
                ci3 = ci[r].rearrange("p (h k) -> p h k", k=16)
                link(*[dve.max(best[r, h, 0:8], cand[r, h, :]) for h in range(NH)])
                link(*[dve.max_index(ci3[:, h, 0:8], best[r, h, 0:8], cand[r, h, :]) for h in range(NH)])
                split_next(1)
                link(*[dve.match_replace(cand2[r, h, :], best[r, h, 0:8], cand[r, h, :], -3e38) for h in range(NH)])
                link(*[dve.max(best[r, h, 8:16], cand2[r, h, :]) for h in range(NH)])
                split_next(2)
                link(*[dve.max_index(ci3[:, h, 8:16], best[r, h, 8:16], cand2[r, h, :]) for h in range(NH)])
                split_next(3)
                link(ts(cab[r, 0, :], ci[r], 4, None, ALU.logical_shift_right), ts(cab[r, 1, :], ci[r], 15, None, ALU.bitwise_and))
                link(cp(cabf[r], cab[r]))
                for w in range(2):
                    eqv = cand[r].rearrange("p h (k a) -> p (h k) a", a=16)
                    link(tt(eqv, cabf[r, w, :].to_broadcast([m, P, 16]),
                            iota16[r].rearrange("p (o a) -> p o a", o=1).to_broadcast([m, P, 16]), EQ))
                    link(*[tt(cand2[r, h, :].rearrange("p (k a) -> p k a", a=16), cand[r, h, :].rearrange("p (k a) -> p k a", a=16),
                              sif[r, 16 * t + 2 * h + w, :].rearrange("p (o a) -> p o a", o=1).to_broadcast([m, 16, 16]), MUL)
                           for h in range(NH)])
                    split_next(4 + 2 * w)
                    if t and w == 0:
                        dve.wait_ge(S["tr_ready"], t)
                    link(dve.tensor_reduce(isel[r, w, :], cand2[r].rearrange("p h (k a) -> p (h k) a", a=16), AX.X, ADD))
                    split_next(5 + 2 * w)
                link(cp(gden[r, 0, :], best[r, :, 0]))
                link(tt(best[r], best[r], gden[r, 0, :].to_broadcast([m, NH, 16]), SUB))
                dve.sem_inc(S["rexp"], 1)
                dve.wait_ge(S["rexp_done"], t + 1)
                link(dve.tensor_reduce(gden[r, 1, :], best[r], AX.X, ADD))
                link(dve.reciprocal(gden[r, 1, :], gden[r, 1, :]))
                link(tt(isel[r, 2, :].rearrange("p (h k) -> p h k", k=16), best[r], gden[r, 1, :].to_broadcast([m, NH, 16]), MUL))
                dve.sem_inc(S["tr_in"], 1)
                dve.wait_ge(S["tr_ready"], t + 1)
                link(cp(routeT[:, :, t * P:t * P + m], ps[:, 4:7, 0:m]))
                dve.sem_inc(S["tr_done"], 1)

            def quad(n, q, tok0):
                dve.wait_ge(S["g_ready"], n + 1)
                for t in range(4):
                    tok = tok0 + t
                    dst = oh[:, 4 * q + t, :]
                    ts(dst[:, 0:P], iota, routeT[:, 0, bass.ds(tok, 1)], None, EQ).then_inc(S["oh_ready"], 1)
                    ts(dst[:, P:2 * P], iota, routeT[:, 1, bass.ds(tok, 1)], routeT[:, 2, bass.ds(tok, 1)],
                       EQ, MUL).then_inc(S["oh_ready"], 1)
            with dve.Fori(0, 4) as it:
                for b in range(8):
                    for q in range(4):
                        quad(it * 32 + (4 * b + q), q, it * 128 + (16 * b + 4 * q))
                        if q == 0:
                            low_u(TOPK_U + b, it * 8 + (TOPK_U + b))
            for q in range(2):
                quad(128 + q, q, 512 + 4 * q)
            for b in range(TAIL_U - 2):
                low_u(b, HOT_U + b)

            dve.wait_ge(S["x_spilled"], 16)
            link(dve.memset(acc, 0.0))
            dve.sem_inc(S["ff_free"], 2)

            def weigh(s, par_, jj):
                w = EXP_J * TC
                blk = s * EXP_J + jj
                z = zbuf[:, jj % 2, :]
                g = gr[:, par_, 0:8 * w].rearrange("p (c j t) -> p c j t", j=EXP_J, t=TC)[:, :, jj, :]
                zp = z[:, 0:SEQ].rearrange("p (c t) -> p c t", t=TC)
                tt(zp, zp, g, MUL).then_inc(S["a_step"], 1)
                tt(z[:, SEQ:TOK], z[:, SEQ:TOK], gr[:, par_, 8 * w + 8 * jj:8 * w + 8 * jj + 8], MUL).then_inc(S["a_step"], 1)
                dve.wait_ge(S["a_step"], blk * 3 + 2)
                hi = ah[:, par_ * EXP_J + jj, :]
                cp(hi, z).then_inc(S["a_step"], 1)
                dve.wait_ge(S["a_step"], blk * 3 + 3)
                tt(al[:, par_ * EXP_J + jj, :], z, hi.bitcast(F32), SUB).then_inc(S["a_ready"], 1)

            def collect(s, dc):
                dve.wait_ge(S["ff_ready"], s * KD + dc + 2)
                dve.wait_ge(S["ff_free"], s * KD + dc + 1)
                a = acc[:, dc, :].rearrange("p (h t) -> p h t", h=2)
                tt(a, a, ps[:, 4 + 2 * (dc % 2):6 + 2 * (dc % 2), 0:HALF], ADD).then_inc(S["ff_free"], 1)

            def group_in(par_, rnd):
                dve.wait_ge(g_l[par_], rnd * 16)
                dve.wait_ge(gt_l[par_], rnd * 16)

            def spilled(s, par_, rnd, item, zr):
                group_in(par_, rnd)
                for jj in range(EXP_J):
                    low_v(par_, jj, item + jj)
                    if jj < 2:
                        dve.wait_ge(S["ff_ready"], (s - 1) * KD + 1)
                    dve.wait_ge(zl[jj % 2], (zr + jj // 2) * 16)
                    weigh(s, par_, jj)
                    collect(s - 1, 2 * jj)
                    collect(s - 1, 2 * jj + 1)
            group_in(0, 1)
            for jj in range(2):
                dve.wait_ge(zl[jj], 16)
                weigh(0, 0, jj)
                low_u(TAIL_U - 2 + jj, SPILL - 2 + jj)
            for jj in range(EXP_J):
                low_v(0, jj, SPILL + jj)
            for jj in range(2, EXP_J):
                dve.wait_ge(zl[jj % 2], 32)
                weigh(0, 0, jj)
            with dve.Fori(0, SPILL_G // 2) as it:
                spilled(it * 2 + 1, 1, it + 1, it * 8 + (SPILL + 4), it * 4 + 3)
                spilled(it * 2 + 2, 0, it + 2, it * 8 + (SPILL + 8), it * 4 + 5)
            low_u(0, 2 * SPILL)
            low_u(1, 2 * SPILL + 1)

            def live(s, par_, rnd, item, more):
                group_in(par_, rnd)
                for jj in range(EXP_J):
                    if jj < 2:
                        low_u(jj + 2, item + (jj + 2))
                    dve.wait_ge(S["gelu_done"], s * EXP_J + jj + 1)
                    weigh(s, par_, jj)
                    if jj >= 2:
                        low_v(par_, jj - 2, item + (jj + 2))
                for q in range(4):
                    collect(s - 1, 2 * q)
                    collect(s - 1, 2 * q + 1)
                    if q < 2:
                        low_v(par_, q + 2, item + (q + 6))
                    elif more:
                        low_u(q - 2, item + (q + 6))
            n_live = GROUPS - SPILL_G
            with dve.Fori(0, (n_live - 1) // 2) as it:
                live(it * 2 + SPILL_G, 1, it + (SPILL_G // 2 + 1), it * 16 + 2 * SPILL, True)
                live(it * 2 + (SPILL_G + 1), 0, it + (SPILL_G // 2 + 2), it * 16 + (2 * SPILL + 8), True)
            live(GROUPS - 1, 1, GROUPS // 2, 2 * SPILL + 8 * (n_live - 1), False)
            for dc in range(KD):
                collect(GROUPS - 1, dc)
            dve.wait_ge(S["ff_free"], 2 + GROUPS * KD)
            dve.wait_ge(S["x_back"], 16)
            for c in range(KD):
                add_gated(x2, c, [(0, SEQ, acc[:, c, 0:SEQ])], acc[:, c, SEQ:TOK], 5)
            link(tt(sq, x2, x2, MUL))
            dve.sem_inc(S["sq_done"], 1)
            dve.wait_ge(S["sum_ready"], 3)
            inverse_ms(D, 0)
            dve.wait_ge(S["rstd_ready"], 5)
            link(*[stt(h2T[:, k, :], x2[:, k, :], par[:, FG + k:FG + k + 1], rstd, MUL, MUL) for k in range(KD)])
            dve.sem_inc(S["fin_ready"], 1)


def one_hot_buckets(dist):
    dist = np.asarray(dist)
    b = np.where(dist < 16, dist, 16 + np.searchsorted(EDGES, dist, side="right"))
    b = np.where(dist < 0, 32, b)
    return (np.arange(33)[:, None] == b[None, :]).astype(np.float32)


def kernel(**a):
    import concourse.bacc as bacc
    from concourse.bass_utils import run_bass_kernel_spmd

    a = {k: np.asarray(v) for k, v in a.items()}
    cols = np.cumsum((0, 512, 512, 512, 256, 256, 256, 24))

    def feat(v):
        return v.reshape(-1, P).T

    def chunks(w):
        return w.reshape(KD, P, -1, P).transpose(2, 1, 0, 3)

    w = a["w_in"][0]
    qw = w[:, cols[2]:cols[3]].reshape(D, NKV, GRP, HD).transpose(0, 2, 1, 3).reshape(D, 512)
    kvw = [w[:, cols[i]:cols[i + 1]].reshape(D, NKV, 2, HD).transpose(0, 2, 1, 3).reshape(D, 256) for i in (3, 4, 5)]
    w_all = np.concatenate([w[:, :1024], qw] + kvw, axis=1)
    wout = a["w_out"][0]
    wout = np.concatenate([wout[:512], wout[512:].reshape(NKV, GRP, HD, D).transpose(1, 0, 2, 3).reshape(512, D)])
    nag = a["out_norm_att"][0].reshape(NKV, GRP, HD).transpose(1, 0, 2).reshape(512)
    par = np.concatenate([feat(v) for v in (a["norm1_g"][0], a["norm2_g"][0], a["final_g"], a["out_norm_lru"][0], nag,
                          a["conv_w"][0].reshape(-1), a["conv_b"][0], a["lru_ba"][0], a["lru_bi"][0],
                          a["lru_lambda"][0], a["peer_bq"][0])], axis=1)
    x = np.concatenate([a["x_prompt"].reshape(SEQ, D), a["x_sample"].reshape(NB, D)])
    c = np.concatenate([a["c_prompt"], a["c_sample"]])

    def pool(cache, which):
        return cache[0, :, :, :, which].transpose(0, 2, 3, 1).reshape(POOL * P, P)

    selk, selv = pool(a["cache_sel_kv"], 0), a["cache_sel_kv"][0, :, :, :, 1].reshape(POOL * P, P)
    win = a["cache_win_kv"][0]
    cw1 = a["cmp_w1"][0].transpose(0, 2, 1, 3)
    pos = np.concatenate([a["cmp_pos"][0].transpose(0, 2, 1)] * 2, axis=1)
    rows = np.arange(ROWS)
    ins = {
        "xT": x.T.reshape(KD, P, TOK).transpose(1, 0, 2), "cT": c.T.reshape(KD, P, 9).transpose(1, 0, 2),
        "par": par, "adab": feat(a["ada_b"][0]), "rel_bias": a["rel_bias"],
        "ada_w": a["ada_w"][0].reshape(KD, P, 6 * D).transpose(1, 0, 2),
        "w_in": chunks(w_all), "w_gate": w[:, cols[6]:].reshape(KD, P, 24).transpose(1, 0, 2),
        "w_out": wout.reshape(KD, P, D).transpose(1, 0, 2), "wq": chunks(a["peer_wq"][0]),
        "sk": a["peer_subkeys"][0].reshape(16, P, P).transpose(2, 0, 1),
        "state_conv": a["state_conv"][0].reshape(NB, 3, 4, P).transpose(3, 2, 1, 0).reshape(P, 4, 3 * NB),
        "state_h": a["state_lru_h"][0].reshape(NB, 4, P).transpose(2, 1, 0),
        "wlru": np.stack([a["lru_wa"][0].reshape(4, 2, HD, HD), a["lru_wi"][0].reshape(4, 2, HD, HD)])
                  .transpose(2, 3, 0, 1, 4).reshape(2, HD, 8, HD),
        "cmp_w1": cw1, "cmp_w2": a["cmp_w2"][0], "posT": pos, "page_table": a["page_table"].reshape(1, NB * PAGES),
        "pool_k": pool(a["cache_cmp_kv"], 0), "pool_v": pool(a["cache_cmp_kv"], 1),
        "pool_s": np.concatenate([selk, selv], axis=1),
        "win_kT": win[:, :, :, 0].transpose(2, 3, 0, 1).reshape(P, NB, 512), "win_v": win[:, :, :, 1].reshape(NB, 512, P),
        "uT": a["peer_u"][0].reshape(P, P, KD, P).transpose(1, 3, 2, 0), "v": a["peer_v"][0].reshape(P, P, D),
        "ohd": one_hot_buckets(np.concatenate([1024 - np.arange(1153), np.zeros(8, np.int64)])),
        "oha": one_hot_buckets(np.arange(OHA_W) - 511),
        "ohw": one_hot_buckets(np.concatenate([[-1], 512 - np.arange(1, 512)])),
        "newmask": np.where(rows[:, None] // NH == np.arange(NB)[None, :], 0.0, NEG).astype(np.float32),
        "gsum": (rows[:, None] // GRP == rows[None, :] // GRP).astype(np.float32),
        "validq": (np.arange(P)[:, None] >= 31).astype(np.float32),
        "blkno": np.broadcast_to(np.arange(1, NSELB + 1, dtype=np.float32), (ROWS, NSELB)),
    }
    ins = {k: np.ascontiguousarray(v) for k, v in ins.items()}
    outs = {"o_y": (P, KD, TOK), "o_kv": (P, 6, TOK), "o_h": (P, 4, 9), "o_conv": (P, 4, 27),
            "o_wink": (P, NB, 512), "o_winv": (NB, 512, P)}
    nc = bacc.Bacc("TRN2", target_bir_lowering=False, num_devices=1)
    io = {k: nc.dram_tensor("in_" + k, v.shape, mybir.dt.from_np(v.dtype), kind="ExternalInput").ap() for k, v in ins.items()}
    for k, shape in outs.items():
        io[k] = nc.dram_tensor("out_" + k, shape, F32, kind="ExternalOutput").ap()
    io["rscratch"] = nc.dram_tensor("rscratch", (NH, 640), F32).ap()
    io["rrows"] = nc.dram_tensor("rrows", (P, NH, 640), F32).ap()
    io["gscratch"] = nc.dram_tensor("gscratch", (ROWS, 3), F32).ap()
    io["gw"] = nc.dram_tensor("gw", (SEQ // TC, P, P * TC), F32).ap()
    io["gwt"] = nc.dram_tensor("gwt", (P, P * NB), F32).ap()
    io["zs"] = nc.dram_tensor("zs", (SPILL, P, TOK), F32).ap()
    io["xspill"] = nc.dram_tensor("xspill", (P, KD, TOK), F32).ap()
    build(nc, io)
    got = run_bass_kernel_spmd(nc, [{"in_" + k: v for k, v in ins.items()}], core_ids=[0]).results[0]
    r = {k: got["out_" + k] for k in outs}

    y = r["o_y"].transpose(2, 1, 0).reshape(TOK, D)
    kv = r["o_kv"].reshape(NKV, HD, 3, 2, TOK).transpose(2, 4, 0, 3, 1)
    wk = r["o_wink"].reshape(NKV, HD, NB, 512).transpose(2, 3, 0, 1)
    wv = r["o_winv"].reshape(NB, 512, NKV, HD)
    old = np.stack([wk, wv], axis=3)[:, :511]
    new_win = np.concatenate([old, kv[2, SEQ:][:, None]], axis=1)
    h = r["o_h"].transpose(2, 1, 0).reshape(9, 512)
    conv = r["o_conv"].reshape(P, 4, 3, 9).transpose(3, 2, 1, 0).reshape(9, 3, 512)
    return (y[:SEQ][None], y[SEQ:][:, None],
            kv[0, :SEQ][None, None], kv[0, SEQ:][None, :, None],
            kv[1, :SEQ][None, None], kv[1, SEQ:][None, :, None],
            kv[2, :SEQ][None, None], new_win[None],
            h[0:1][None], h[1:][None], conv[0:1][None], conv[1:][None])
```

```python
from contextlib import ExitStack

import concourse.bass as bass
from concourse import mybir
import numpy as np

F32 = mybir.dt.float32
U32 = mybir.dt.uint32
ALU = mybir.AluOpType
ACT = mybir.ActivationFunctionType
AX = mybir.AxisListType
ADD, MUL, SUB, MAX, MIN, EQ = ALU.add, ALU.mult, ALU.subtract, ALU.max, ALU.min, ALU.is_equal

P = 128
D = 1024
KD = D // P
SEQ = 512
NB = 8
TOK = SEQ + NB
HALF = TOK // 2
PAST = 1024
PAGE = 128
PAGES = PAST // PAGE
POOL = 5 * NB * PAGES // 4
HD = 64
NH = 8
NKV = 2
GRP = NH // NKV
ROWS = NB * NH
NCMP_P = SEQ // 16 - 1
NCMP_S = PAST // 16 - 1
NSELB = 14
NEG = -1e30
EPS = 1e-6
ZC = 18
XR, YG, QC, KC, VC_, KS, VS, KW, VW = 0, 4, 8, 12, 13, 14, 15, 16, 17
F32R = mybir.dt.float32r
EXP_J = 4
GROUPS = P // EXP_J
TILE_U = (9, 9, 9, 9, 8)
TOPK_U = 16 + sum(TILE_U)
HOT_U = TOPK_U + 32
TAIL_U = 8
SPILL = HOT_U + TAIL_U
SPILL_G = SPILL // EXP_J
AW = 384
AN = 6 * D // AW
QM = NCMP_P + 24
AK, AV = 6, 9
TC = 64
OHD_W, OHA_W, OHW_W = 1161, 1024, 512
EDGES = [21, 27, 35, 46, 59, 77, 99, 128, 166, 216, 280, 363, 470, 609, 790]


def tile_splits(t, point):
    n = TILE_U[t] - (4 if t == 4 else 0)
    return [q for q in range(n) if q * 8 // n == point]


def build(nc, io):
    ctx = ExitStack()
    with ctx:
        def sem(name):
            return ctx.enter_context(nc.semaphore(name))

        def sb(name, shape, dt=F32):
            return ctx.enter_context(nc.sbuf_tensor(name, shape, dt))

        xT = sb("xT", [P, KD, TOK])
        mT = sb("mT", [P, 48, 9])
        ident = sb("ident", [P, P])
        ones = sb("ones", [P, P])
        par = sb("par", [P, 128])
        posb = sb("posb", [P, 2])
        gates = sb("gates", [P, 5, 24])
        gate_rows = sb("gate_rows", [ROWS, 3])
        cst = sb("cst", [P, 540])
        with nc.sbuf_tensor("arena", [P, 46700], F32) as arena:
            pass
        uh, ul = sb("uh", [P, 2 * KD, P], F32R), sb("ul", [P, 2 * KD, P], F32R)
        with nc.sbuf_tensor("wq", [P, 3 * KD, P], F32) as wq:
            pass
        vh, vl = sb("vh", [P, 2 * EXP_J, D], F32R), sb("vl", [P, 2 * EXP_J, D], F32R)
        ah, al = sb("ah", [P, 2 * EXP_J, TOK], F32R), sb("al", [P, 2 * EXP_J, TOK], F32R)
        hh, hl = sb("hh", [P, KD, TOK], F32R), sb("hl", [P, KD, TOK], F32R)
        raw = sb("raw", [P, 4, D])
        zbuf = sb("zbuf", [P, 2, TOK])
        gr = sb("gr", [P, 2, EXP_J * TOK])
        ztail = gr[:, 1, 0:2 * TOK].rearrange("p (s t) -> p s t", t=TOK)
        uhs = [uh[:, 0:KD, :], uh[:, KD:2 * KD, :]] + [vl[:, q, :].rearrange("p (k i) -> p k i", i=P) for q in (5, 7)]
        uls = [ul[:, 0:KD, :], ul[:, KD:2 * KD, :], vl[:, 6, :].rearrange("p (k i) -> p k i", i=P),
               al.rearrange("p a b -> p (a b)")[:, 2944:2944 + D].rearrange("p (k i) -> p k i", i=P)]
        wqh = [q.rearrange("p (k i) -> p k i", i=P) for q in (vh[:, 7, :], vl[:, 0, :])]
        wql = [vl[:, q, :].rearrange("p (k i) -> p k i", i=P) for q in (1, 2)]
        ps = ctx.enter_context(nc.psum_tensor("ps", [P, 8, 512], F32))

        N1G, N2G, FG, NLG, NAG, CW, CB, BA, BI, LAM, BQ, ADB = 0, 8, 16, 24, 28, 32, 48, 52, 56, 60, 64, 80
        rbx, rb, newmask, gsum = cst[:, 0:64], cst[:, 64:72], cst[:, 72:80], cst[:, 80:144]
        validq, blkno, small = cst[:, 144:145], cst[:, 145:161], cst[:, 161:441]
        lrt, pstt = cst[:, 441:481], cst[:, 481:513]

        def lr(n):
            return lrt[:, 4 * n:4 * n + 4]

        def sm(n):
            return small[0:ROWS, 200 + n:201 + n]

        def pst(u, n):
            return pstt[:, (u % 2) * 16 + 4 * n:(u % 2) * 16 + 4 * n + 4]

        def at(off, *shape):
            n = int(np.prod(shape))
            assert off + n <= 46700
            a = arena[:, off:off + n]
            return a.rearrange("p (a b) -> p a b", b=shape[1]) if len(shape) == 2 else a

        zT = at(0, ZC, TOK)
        hT = at(9360, KD, TOK)
        ada = at(13520, 2 * KD, AW)
        win_w = at(13520, 2 * KD, P)
        xpool = [at(0, 32 * 256), at(19664, 33 * 256)]
        zeros = at(28112, 272)
        w1 = at(34064, 32, P)
        ohd = at(38160, OHD_W)
        oha = at(39321, OHA_W)
        hid = at(40345, 546)
        ckT = at(40891, 544)
        vc = at(41435, 9, P)
        w2 = at(42587, 2, P)
        pbias = at(42843, NH, QM)
        rstd = at(43835, TOK)
        wgate = at(44355, KD, 24)
        stc = at(44547, 4, 3 * NB)
        h0T = at(44643, 4, NB)
        m9 = at(44675, 2, AW)
        cT = at(45443, KD, 9)
        rsb = at(45515, 640)
        rT, iT_ = at(9360, 4, TOK), at(11440, 4, TOK)
        xcT, aT, uT = at(15600, 4, TOK), at(13520, 4, TOK), zT[:, XR:XR + 4, :]
        wlru = at(44675, 8, P)
        outh = at(46155, 4, 9)
        outc = at(46191, 4, 27)
        sel = at(17680, NB * PAGES, 256)
        gT = at(39321, TOK)
        qpad = at(39321, NB, ROWS)
        qs = at(39833, ROWS)
        vnew = at(39897, 2, P)
        vn = at(44675, 8, P)
        ohw = at(34064, OHW_W)
        ss = at(34576, 1032)
        sw = at(35608, 520)
        sc = at(45699, 64)
        gs = at(45763, 64)
        pts = at(36256, 15, ROWS)
        osb = at(34064, NB * P)
        kwin = at(13520, NB, 512)
        vwin = at(9360, NB * 4, P)
        wout = at(21712, KD, D)
        qz = at(29904, 2 * GRP, SEQ)
        biasT = at(17616, NH, 512)
        pbuf = at(34064, 2 * GRP, SEQ)
        ptb = at(13520, 4, GRP * P)
        pcb = at(15568, 4 * NH, NCMP_P)
        pcm = at(16560, 2, 4 * NH)
        ptcb = at(9360, 4, 1024)
        x1sq = at(13520, KD, TOK)
        h2T = at(20480, KD, TOK)
        qT = at(7168, TOK)
        sk = at(8208, 16, P)
        tmpk = at(10256, 5, P)
        cand = at(10896, NH, 256)
        cand2 = at(12944, NH, 256)
        best = at(14992, NH, 16)
        cabf = at(15120, 2, P)
        isel = at(15376, 3, P)
        gden = at(15760, 2, NH)
        sif = at(15776, 5 * 16, 16)
        sv = at(24640, 5 * 16, 16)
        si = arena[:, 25920:27200].bitcast(U32).rearrange("p (a b) -> p a b", b=16)
        ci = arena[:, 27200:27328].bitcast(U32)
        cab = arena[:, 27328:27584].bitcast(U32).rearrange("p (a b) -> p a b", b=P)
        routeT = at(42256, 3, TOK)
        iota = at(46155, P)
        iota16 = at(46283, 16)
        oh = at(20480, 4 * 4, 2 * P)
        stage = at(4096, 2, P * TC)
        acc = xT[:, :, :]
        x2 = at(28800, KD, TOK)
        sq = at(37120, KD, TOK)

        names = """c_loaded par_loaded table_loaded const_loaded x_loaded ada_ready z_ready wgate_loaded
            lrus_loaded hi_ready lruw_loaded z_moved kv_stored lru_ready lru_stored lru_norm ohw_loaded
            gates_ready gate_stored gate_moved sel_free win_loaded wout_loaded out_stored proj_done
            sk_loaded h_ready x_spilled q_ready lo_done zz_ready x_back fin_ready pool_done memset_done
            w2_loaded w1k_loaded pos_loaded page_loaded gather_k hid_ready w1v_loaded gather_s rs_copied
            mt_done scratch_stored rows_stored bias_loaded bias_ready ck_moved zero_done qz_ready chunk_sq rounded wql_done
            gelu_done g_moved g_ready a_ready rb_ready rs_ready pb_ready silu_done m9_ready mt_ready
            sq_done sum_ready zg_ready xc_ready ri_ready gate_ready gelu_ready ck_ready mix_sum cmp_done
            vt_ready vt_done qpad_ready sc_ready ss_ready sc_soft sum_done ss_p pts_ready pts_done
            sw_ready sw_p ptw_ready ptw_done os_ready os_done u_ttr u_s pc_s pc_p u_tdone pc_t pc_tdone
            o_done u_p u_t u_pv mix_sq mix_ready proj_ready pe_step q_moved s_free s_ready tr_in
            tr_ready tr_done oh_ready ff_free ff_ready act_step root_in rstd_ready lru_prep exp_ready
            yg_ready sc_exp ss_max ss_exp sw_max sw_exp pc_max pc_exp u_max u_exp u_rs hi_done rexp
            rexp_done dve_step a_step""".split()
        S = {n: sem(n) for n in names}
        ada_l = [sem(f"ada_loaded{i}") for i in range(2)]
        w_l = [sem(f"w_loaded{i}") for i in range(2)]
        wq_l = [sem(f"wq_loaded{i}") for i in range(3)]
        raw_l = [sem(f"raw_loaded{i}") for i in range(4)]
        gt_l = [sem(f"g_tail_loaded{i}") for i in range(2)]
        zst = [sem(f"z_stored{i}") for i in range(2)]
        zl = [sem(f"z_loaded{i}") for i in range(2)]
        g_l = [sem(f"g_loaded{i}") for i in range(2)]
        st_l = [sem(f"stage_stored{i}") for i in range(2)]

        rscratch = io["rscratch"]
        block = ctx.enter_context(nc.Block())
        units = [(i, br, g) for i in range(4) for br in range(2) for g in range(2)]

        def load_w1(engine, c, s):
            for g in range(2):
                engine.dma_start(w1[g * HD:(g + 1) * HD, :, g * HD:(g + 1) * HD], io["cmp_w1"][c]).then_inc(s, 16)

        @block.sync
        def _(sp):
            def load(dst, src, s):
                sp.dma_start(dst, src).then_inc(s, 16)

            load(cT, io["cT"], S["c_loaded"])
            load(par[:, 0:80], io["par"], S["par_loaded"])
            load(par[:, 80:128], io["adab"], S["par_loaded"])
            load(ohd[0:33], io["ohd"], S["table_loaded"])
            load(oha[0:33], io["oha"], S["table_loaded"])
            load(rb[0:32], io["rel_bias"], S["table_loaded"])
            load(rbx[0:32].rearrange("p (b h) -> p b h", h=NH),
                 io["rel_bias"].rearrange("a (o h) -> a o h", o=1).to_broadcast([32, NB, NH]), S["table_loaded"])
            load(newmask[0:ROWS], io["newmask"], S["const_loaded"])
            load(gsum[0:ROWS], io["gsum"], S["const_loaded"])
            load(validq, io["validq"], S["const_loaded"])
            load(blkno[0:ROWS, 0:NSELB], io["blkno"], S["const_loaded"])
            for n in range(2):
                load(ada[:, n * KD:(n + 1) * KD, :], io["ada_w"][:, :, n * AW:(n + 1) * AW], ada_l[n])
            load(xT[:, :, :], io["xT"], S["x_loaded"])
            sp.wait_ge(S["zero_done"], 1)
            load_w1(sp, 0, S["w1k_loaded"])
            for c in range(2):
                for g in range(2):
                    load(w2[g * HD:(g + 1) * HD, c, g * HD:(g + 1) * HD], io["cmp_w2"][c], S["w2_loaded"])
            for n in range(2, AN):
                sp.wait_ge(S["ada_ready"], n - 1)
                load(ada[:, (n % 2) * KD:(n % 2 + 1) * KD, :], io["ada_w"][:, :, n * AW:(n + 1) * AW], ada_l[n % 2])
            sp.wait_ge(S["ada_ready"], AN - 1)
            load(wgate, io["w_gate"], S["wgate_loaded"])
            for n in range(2):
                load(win_w[:, n * KD:(n + 1) * KD, :], io["w_in"][n], w_l[n])
            load(stc, io["state_conv"], S["lrus_loaded"])
            load(h0T, io["state_h"], S["lrus_loaded"])
            for n in range(2, ZC):
                sp.wait_ge(S["z_ready"], n - 1)
                load(win_w[:, (n % 2) * KD:(n % 2 + 1) * KD, :], io["w_in"][n], w_l[n % 2])
                if n == 5:
                    sp.wait_ge(S["hi_ready"], 1)
                    for e in range(2):
                        load(wlru[e * HD:(e + 1) * HD, :, e * HD:(e + 1) * HD],
                             io["wlru"][e], S["lruw_loaded"])
            sp.wait_ge(S["z_moved"], ZC)
            load(io["o_kv"], zT[:, KC:ZC, :], S["kv_stored"])
            sp.wait_ge(S["hid_ready"], 3)
            load_w1(sp, 0, S["w1k_loaded"])
            sp.wait_ge(S["gates_ready"], 2)
            load(io["gscratch"].rearrange("(b h) r -> b (h r)", h=NH), gates[0:NB, 4, :], S["gate_stored"])
            sp.wait_ge(S["gate_stored"], 16)
            load(gate_rows[:, :], io["gscratch"], S["gate_moved"])
            sp.wait_ge(S["hid_ready"], 4)
            load(ohw[0:33], io["ohw"], S["ohw_loaded"])
            sp.wait_ge(S["lru_ready"], 1)
            load(io["o_h"], outh, S["lru_stored"])
            load(io["o_conv"], outc, S["lru_stored"])
            load(vwin, io["win_v"].rearrange("b (c p) f -> p (b c) f", p=P), S["win_loaded"])
            sp.wait_ge(S["mix_sum"], 1)
            load(kwin, io["win_kT"], S["win_loaded"])
            sp.wait_ge(S["sel_free"], 1)
            load(wout, io["w_out"], S["wout_loaded"])
            for b in range(NB):
                load(io["o_winv"][b, 0:511], io["win_v"][b, 1:512], S["out_stored"])
            load(io["o_wink"][:, :, 0:511], io["win_kT"][:, :, 1:512], S["out_stored"])
            sp.wait_ge(S["proj_done"], 1)
            load(sk, io["sk"], S["sk_loaded"])
            sp.wait_ge(S["kv_stored"], 16)
            for n in range(3):
                load(wq[:, n * KD:(n + 1) * KD, :], io["wq"][n], wq_l[n])

            def load_raw(slot, src):
                sp.dma_start(raw[:, slot, :], src).then_inc(raw_l[slot], 16)

            def u_block(blk):
                return io["uT"][blk]

            def v_block(blk):
                return io["v"][:, blk, :]

            for b in range(4):
                load_raw(b, u_block(b))
            sp.wait_ge(S["h_ready"], 2 * KD)
            sp.dma_start(io["xspill"], xT[:, :, :]).then_inc(S["x_spilled"], 16)
            for b in range(4, 7):
                sp.wait_ge(S["lo_done"], b - 3)
                load_raw(b % 4, u_block(b))
            for n in range(3, 16):
                sp.wait_ge(S["q_ready"], n - 2)
                load(wq[:, (n % 3) * KD:(n % 3 + 1) * KD, :], io["wq"][n], wq_l[n % 3])
                sp.wait_ge(S["lo_done"], n + 1)
                load_raw(n % 4, u_block(n + 4))
            with sp.Fori(5, SPILL // 4) as it:
                for b in range(4):
                    sp.wait_ge(S["lo_done"], it * 4 + (b - 3))
                    load_raw(b, u_block(it * 4 + b))
            with sp.Fori(0, SPILL_G) as it:
                for b in range(4):
                    sp.wait_ge(S["lo_done"], it * 4 + (SPILL + b - 3))
                    load_raw(b, v_block(it * 4 + b))
            with sp.Fori(0, GROUPS - SPILL_G) as it:
                for w, block_of in enumerate((u_block, v_block)):
                    for b in range(4):
                        sp.wait_ge(S["lo_done"], it * 8 + (2 * SPILL + 4 * w + b - 3))
                        load_raw(b, block_of(it * 4 + (SPILL + b)))
            sp.wait_ge(S["zz_ready"], P)
            load(x2, io["xspill"], S["x_back"])
            for k in range(KD):
                sp.wait_ge(S["fin_ready"], k + 1)
                load(io["o_y"][:, k], h2T[:, k, :], S["out_stored"])
            sp.wait_ge(S["out_stored"], 16 * (NB + 1 + KD))

        @block.gpsimd
        def _(pool):
            def load(dst, src, s):
                pool.dma_start(dst, src).then_inc(s, 16)

            pool.memset(ident[:, :], 0.0).then_inc(S["pool_done"], 1)
            pool.memset(xpool[1][:, 32 * 256:33 * 256], 0.0).then_inc(S["pool_done"], 1)
            pool.wait_ge(S["pool_done"], 2)
            for c in range(2):
                load(xpool[1][:, 32 * 256 + P * c:32 * 256 + P * c + 32], io["posT"][c], S["pos_loaded"])
            pgi = small[:, 0:64].bitcast(mybir.dt.int32)
            pid = small[:, 64:65].bitcast(mybir.dt.int32)
            idx = small[:, 128:192].bitcast(mybir.dt.int32)
            pool.dma_start(pgi, io["page_table"].to_broadcast([P, NB * PAGES])).then_inc(S["page_loaded"], 16)
            pool.iota(pid, pattern=[[0, 1]], base=0, channel_multiplier=1).then_inc(S["pool_done"], 1)
            pool.wait_ge(S["pool_done"], 3)
            pool.affine_select(out=ident[:, :], in_=ident[:, :], compare_op=ALU.not_equal, fill=1.0,
                               base=0, pattern=[[-1, P]], channel_multiplier=1).then_inc(S["memset_done"], 1)
            pool.wait_ge(S["page_loaded"], 16)
            pool.tensor_scalar(pgi, pgi, float(P), None, MUL).then_inc(S["pool_done"], 1)
            pool.wait_ge(S["pool_done"], 4)
            pool.tensor_tensor(idx, pgi, pid.to_broadcast([P, 64]), ADD).then_inc(S["pool_done"], 1)
            pool.wait_ge(S["pool_done"], 5)

            def gather(dst, src, s):
                for n in range(NB * PAGES):
                    pool.indirect_dma_start(
                        out=dst(n), out_offset=None, in_=src,
                        in_offset=bass.IndirectOffsetOnAxis(ap=idx[:, n:n + 1].bitcast(U32), axis=0)).then_inc(s, 16)
            gather(lambda n: xpool[n // 32][:, (n % 32) * 256:(n % 32 + 1) * 256], io["pool_c"], S["gather_k"])
            pool.wait_ge(S["rs_copied"], 1)
            pool.dma_start(rscratch, rsb[0:NH]).then_inc(S["scratch_stored"], 16)
            pool.wait_ge(S["scratch_stored"], 16)
            rows = io["rrows"]
            pool.dma_start(rows.rearrange("p h c -> p (h c)"),
                           rscratch.rearrange("h (o c) -> o (h c)", o=1).to_broadcast([P, NH * 640])
                           ).then_inc(S["rows_stored"], 16)
            pool.wait_ge(S["hid_ready"], 1)
            load_w1(pool, 1, S["w1v_loaded"])
            pool.wait_ge(S["hid_ready"], 2)
            pool.wait_ge(S["ada_ready"], AN)
            gather(lambda n: sel[:, n, :], io["pool_s"], S["gather_s"])
            pool.wait_ge(S["sel_free"], 1)
            pool.wait_ge(S["rows_stored"], 16)
            pool.dma_start(biasT, bass.AP(rows.tensor, 127, [[NH * 640 - 1, P], [640, NH], [1, 512]])
                           ).then_inc(S["bias_loaded"], 16)
            pool.wait_ge(S["proj_done"], 1)
            pool.iota(iota, pattern=[[1, P]], base=0, channel_multiplier=0,
                      allow_small_or_imprecise_dtypes=True).then_inc(S["bias_ready"], 1)
            pool.iota(iota16, pattern=[[1, 16]], base=0, channel_multiplier=0,
                      allow_small_or_imprecise_dtypes=True).then_inc(S["bias_ready"], 1)

            def store_z(b, slot):
                pool.wait_ge(S["gelu_done"], b + 1)
                pool.dma_start(io["zs"][b], zbuf[:, slot, :]).then_inc(zst[slot], 16)

            def store_stage(ch, par_):
                pool.wait_ge(S["g_moved"], ch * 16 + 20)
                pool.dma_start(io["gw"][ch], stage[:, par_, :]).then_inc(st_l[par_], 16)
            for b in range(TOPK_U):
                store_z(b, b % 2)
            with pool.Fori(0, 4) as it:
                for c in range(2):
                    for b in range(4):
                        store_z(it * 8 + (TOPK_U + 4 * c + b), b % 2)
                    store_stage(it * 2 + c, c)
            pool.wait_ge(S["g_moved"], 134)
            pool.dma_start(io["gwt"], stage[:, 0, 0:8 * P]).then_inc(st_l[0], 16)

            def store_tail(b):
                pool.wait_ge(S["gelu_done"], HOT_U + b + 1)
                pool.dma_start(io["zs"][HOT_U + b], ztail[:, b % 2, :]).then_inc(zst[b % 2], 16)
            store_tail(0)
            store_tail(1)
            pool.wait_ge(st_l[0], 80)
            pool.wait_ge(st_l[1], 64)
            pool.wait_ge(zst[0], 16 * HOT_U // 2)
            pool.wait_ge(zst[1], 16 * HOT_U // 2)
            pool.wait_ge(S["g_ready"], 134)

            def load_g(s, par_):
                w = EXP_J * TC
                pool.dma_start(gr[:, par_, 0:8 * w].rearrange("p (c w) -> p c w", w=w),
                               io["gw"][:, :, bass.ds(s * w, w)].rearrange("c i w -> i c w")).then_inc(g_l[par_], 16)
                pool.dma_start(gr[:, par_, 8 * w:8 * w + 8 * EXP_J],
                               io["gwt"][:, bass.ds(s * (8 * EXP_J), 8 * EXP_J)]).then_inc(gt_l[par_], 16)

            def load_z(s, jj):
                pool.dma_start(zbuf[:, jj % 2, :], io["zs"][s * EXP_J + jj]).then_inc(zl[jj % 2], 16)

            def load_step(s, par_):
                for jj in range(EXP_J):
                    pool.wait_ge(S["a_ready"], s * EXP_J + (jj - 1))
                    load_z(s, jj)
                    if jj == 1:
                        load_g(s + 1, 1 - par_)
            load_g(0, 0)
            load_z(0, 0)
            load_z(0, 1)
            for b in range(2, TAIL_U - 2):
                store_tail(b)
            for jj in range(2, EXP_J):
                pool.wait_ge(S["a_ready"], jj - 1)
                load_z(0, jj)
            for b in range(TAIL_U - 2, TAIL_U):
                store_tail(b)
            pool.wait_ge(zst[0], 16 * SPILL // 2)
            pool.wait_ge(zst[1], 16 * SPILL // 2)
            load_g(1, 1)
            with pool.Fori(0, SPILL_G // 2) as it:
                load_step(it * 2 + 1, 1)
                load_step(it * 2 + 2, 0)
            with pool.Fori(0, (GROUPS - SPILL_G - 1) // 2) as it:
                pool.wait_ge(S["a_ready"], it * 8 + (SPILL_G * EXP_J + 4))
                load_g(it * 2 + (SPILL_G + 1), 0)
                pool.wait_ge(S["a_ready"], it * 8 + (SPILL_G * EXP_J + 8))
                load_g(it * 2 + (SPILL_G + 2), 1)

        @block.tensor
        def _(pe):
            mm = pe.matmul

            def two(b, lhs, rhs_k, ks):
                for n, k in enumerate(ks):
                    for h in range(2):
                        last = mm(ps[:, b + h, 0:HALF], lhs(k), rhs_k(k)[:, h * HALF:(h + 1) * HALF],
                                  start=(n == 0), stop=(n == len(ks) - 1))
                return last

            pe.wait_ge(S["table_loaded"], 64)
            pe.wait_ge(S["rb_ready"], 1)
            mm(ps[0:NH, 0, 0:512], rb[0:33], ohd[0:33, 513:1025], start=True, stop=True)
            mm(ps[0:NH, 1, 0:128], rb[0:33], ohd[0:33, 1025:1153], start=True, stop=True).then_inc(S["rs_ready"], 1)

            def offset_bias(q):
                for m in range(14 * q, min(14 * q + 14, QM)):
                    st = 16 * (QM - 1 - m)
                    last = mm(ps[:, 2, m * NH:(m + 1) * NH], oha[0:33, st:st + P], rb[0:33], start=True, stop=True)
                if q == 3:
                    last.then_inc(S["pb_ready"], 1)

            pe.wait_ge(S["silu_done"], 1)
            pe.wait_ge(S["memset_done"], 1)

            def turn_m9(n):
                pe.wait_ge(S["m9_ready"], n + 1)
                if n >= 2:
                    pe.wait_ge(S["mt_done"], n - 1)
                for q in range(AW // P):
                    last = pe.transpose(ps[:, 6 + n % 2, q * 9:(q + 1) * 9], m9[0:9, n % 2, q * P:(q + 1) * P],
                                        ident[0:9, 0:9])
                last.then_inc(S["mt_ready"], 1)

            def hidden_pages(c):
                pe.wait_ge(S["w1k_loaded"] if c == 0 else S["w1v_loaded"], 32)
                if c == 0:
                    pe.wait_ge(S["pos_loaded"], 32)
                    pe.wait_ge(S["gather_k"], 16 * NB * PAGES)
                    pe.wait_ge(S["rs_copied"], 1)
                else:
                    pe.wait_ge(S["gelu_ready"], 1)
                for h in range(2):
                    xv = xpool[h].rearrange("p (g c n s) -> p g c n s", c=2, n=8, s=16)
                    n = 256 + 8 * h
                    mm(ps[:, h, 0:1 + n], zeros[:, 0:P], zeros[:, 0:1 + n], start=True, stop=False)
                    for ms in range(32):
                        m, s = ms // 16, ms % 16
                        last = mm(ps[:, h, 1 - m:1 - m + n], w1[:, ms, :], xv[:, :, c, :, s],
                                  start=False, stop=(ms == 31))
                last.then_inc(S["hid_ready"], 1)

            def keys_pages():
                pe.wait_ge(S["gelu_ready"], 1)
                pe.wait_ge(S["w2_loaded"], 64)
                pe.wait_ge(S["mt_done"], 4)
                mm(ps[:, 2, 0:512], w2[:, 0, :], hid[:, 0:512], start=True, stop=True).then_inc(S["ck_ready"], 1)

            def values_pages():
                pe.wait_ge(S["gelu_ready"], 2)
                pe.wait_ge(S["ck_moved"], 1)
                for b in range(NB):
                    last = mm(ps[0:NCMP_S, 2 + b // 4, (b % 4) * P:(b % 4 + 1) * P], hid[:, b * 64:b * 64 + NCMP_S],
                              w2[:, 1, :], start=True, stop=True)
                last.then_inc(S["ck_ready"], 1)
            for n in range(AN):
                pe.wait_ge(ada_l[n % 2], 16 * (n // 2 + 1))
                if n >= 2:
                    pe.wait_ge(S["m9_ready"], n - 1)
                for k in range(KD):
                    last = mm(ps[0:9, 4 + n % 2, 0:AW], cT[:, k, :], ada[:, (n % 2) * KD + k, :],
                              start=(k == 0), stop=(k == KD - 1))
                last.then_inc(S["ada_ready"], 1)
                if n >= 1:
                    turn_m9(n - 1)
                if n < 4:
                    offset_bias(n)
                if n == AK:
                    hidden_pages(0)
                if n == AK + 1:
                    keys_pages()
                if n == AV:
                    hidden_pages(1)
                if n == AV + 1:
                    values_pages()
                    pe.wait_ge(S["sq_done"], 1)
                    two(0, lambda k: ones[:, :], lambda k: hT[:, k, :], range(KD)).then_inc(S["sum_ready"], 1)
            turn_m9(AN - 1)

            pe.wait_ge(S["h_ready"], KD)
            pe.wait_ge(S["ck_moved"], 2)
            pe.wait_ge(S["wgate_loaded"], 16)
            pe.wait_ge(S["mt_done"], AN)
            for k in range(KD):
                for h in range(2):
                    last = mm(ps[0:24, 6 + h, 0:HALF], wgate[:, k, :], hT[:, k, h * HALF:(h + 1) * HALF],
                              start=(k == 0), stop=(k == KD - 1))
            last.then_inc(S["zg_ready"], 1)
            for n in range(ZC):
                pe.wait_ge(w_l[n % 2], 16 * (n // 2 + 1))
                if n >= 3:
                    pe.wait_ge(S["z_moved"], n - 2)
                two(2 * (n % 3), lambda k: win_w[:, (n % 2) * KD + k, :], lambda k: hT[:, k, :],
                    range(KD)).then_inc(S["z_ready"], 1)
                if n == 0:
                    pe.wait_ge(S["gates_ready"], 1)
                    for t in range(5):
                        m = P if t < 4 else NB
                        last = pe.transpose(ps[0:m, 7, 320 + t * 24:344 + t * 24], gT[0:24, t * P:t * P + m], ident[0:24, 0:24])
                    last.then_inc(S["zg_ready"], 1)
            def hidden_prompt(c, col):
                xv = zT[:, VC_ if c else KC, 0:SEQ].rearrange("p (n s) -> p n s", s=16)
                for ms in range(32):
                    m, s = ms // 16, ms % 16
                    last = mm(ps[:, 7, col:col + NCMP_P], w1[:, ms, :], xv[:, m:m + NCMP_P, s],
                              start=(ms == 0), stop=(ms == 31))
                last.then_inc(S["hid_ready"], 1)
            pe.wait_ge(S["z_moved"], ZC)
            pe.wait_ge(S["lruw_loaded"], 32)
            for c in range(4):
                pe.wait_ge(S["xc_ready"], c + 1)
                if c >= 1:
                    pe.wait_ge(S["ri_ready"], c)
                for w in range(2):
                    last = two(2 * w, lambda k: wlru[:, 4 * w + c, :], lambda k: xcT[:, c, :], [0])
                last.then_inc(S["gate_ready"], 1)
            hidden_prompt(1, 128)
            pe.wait_ge(S["ri_ready"], 4)
            for br in range(2):
                for kb in range(4):
                    pe.transpose(ps[:, 4 + br, kb * P:(kb + 1) * P], zT[:, (VS, VW)[br], kb * P:(kb + 1) * P], ident[:, :])
            for br in range(2):
                last = pe.transpose(ps[0:NB, 6, (2 + br) * P:(3 + br) * P], zT[:, (VS, VW)[br], SEQ:TOK], ident[:, :])
            last.then_inc(S["vt_ready"], 1)

            pe.wait_ge(S["qpad_ready"], 1)
            for b in range(NB):
                mm(ps[0:ROWS, 3, 0:NCMP_S], qpad[:, b, :], ckT[:, b * 64:b * 64 + NCMP_S], start=(b == 0), stop=False)
            mm(ps[0:ROWS, 3, 0:NCMP_S], rbx[0:33], ohd[0:33, 31:31 + 16 * (NCMP_S - 1) + 1:16],
               start=False, stop=True).then_inc(S["sc_ready"], 1)
            pe.wait_ge(S["gather_s"], 16 * NB * PAGES)
            for h in range(2):
                for b in range(NB):
                    mm(ps[0:ROWS, h, 0:512], qpad[:, b, :], sel[:, b * 8 + h * 4:b * 8 + h * 4 + 4, 0:P],
                       start=(b == 0), stop=False)
                mm(ps[0:ROWS, h, 0:512], rbx[0:33], ohd[0:33, h * 512:(h + 1) * 512], start=False, stop=True)
            mm(ps[0:ROWS, 2, 0:NB], qs, zT[:, KS, SEQ:TOK], start=True, stop=False)
            mm(ps[0:ROWS, 2, 0:NB], rbx[0:33], ohd[0:33, 1153:1161], start=False, stop=True).then_inc(S["ss_ready"], 1)
            pe.wait_ge(S["gelu_ready"], 3)
            pe.wait_ge(S["vt_done"], 1)
            mm(ps[0:NCMP_P, 6, P:2 * P], hid[:, 512:512 + NCMP_P], w2[:, 1, :], start=True, stop=True).then_inc(S["ck_ready"], 1)
            pe.wait_ge(S["w1k_loaded"], 64)
            hidden_prompt(0, 160)
            pe.wait_ge(S["gelu_ready"], 4)
            mm(ps[:, 7, 192:192 + NCMP_P], w2[:, 0, :], hid[:, 512:512 + NCMP_P], start=True, stop=True).then_inc(S["ck_ready"], 1)
            pe.wait_ge(S["cmp_done"], 1)
            pe.wait_ge(S["vt_done"], 1)
            pe.wait_ge(S["lru_ready"], 1)
            two(4, lambda k: ones[:, :], lambda k: aT[:, k, :], range(4)).then_inc(S["mix_sum"], 1)
            pe.wait_ge(S["sc_soft"], 1)
            mm(ps[0:ROWS, 2, 64:64 + NCMP_S], gsum[0:ROWS], gs[0:ROWS, 0:NCMP_S], start=True, stop=True).then_inc(S["sum_done"], 1)
            pe.wait_ge(S["ss_p"], 1)
            pe.transpose(ps[0:NCMP_S, 3, 0:ROWS], sc[0:ROWS, 0:NCMP_S], ident[0:ROWS, 0:ROWS])
            pe.transpose(ps[0:NB, 3, ROWS:2 * ROWS], ss[0:ROWS, 1024:1032], ident[0:ROWS, 0:ROWS])
            for kb in range(8):
                last = pe.transpose(ps[:, 6, kb * ROWS:(kb + 1) * ROWS], ss[0:ROWS, kb * P:(kb + 1) * P], ident[0:ROWS, 0:ROWS])
            last.then_inc(S["pts_ready"], 1)
            pe.wait_ge(S["pts_done"], 1)

            def paged_output(b):
                r = slice(b * NH, (b + 1) * NH)
                o = ps[0:NH, 6 + b // 4, (b % 4) * P:(b % 4 + 1) * P]
                mm(o, pts[0:NCMP_S, 0, r], vc[0:NCMP_S, b, :], start=True, stop=False)
                mm(o, pts[0:NB, 1, r], vnew[0:NB, 0, :], start=False, stop=False)
                for kb in range(8):
                    last = mm(o, pts[:, 2 + kb, r], sel[:, b * 8 + kb, P:2 * P], start=False, stop=(kb == 7))
                return last
            for b in range(3):
                paged_output(b)
            pe.wait_ge(S["win_loaded"], 32)
            pe.wait_ge(S["ohw_loaded"], 16)
            for b in range(NB):
                mm(ps[0:ROWS, 0, 0:512], qpad[:, b, :], kwin[:, b, :], start=(b == 0), stop=False)
            mm(ps[0:ROWS, 0, 0:512], rbx[0:33], ohw[0:33], start=False, stop=True)
            mm(ps[0:ROWS, 1, 0:NB], qs, zT[:, KW, SEQ:TOK], start=True, stop=False)
            mm(ps[0:ROWS, 1, 0:NB], rbx[0:33], ohd[0:33, 1153:1161], start=False, stop=True).then_inc(S["sw_ready"], 1)
            for b in range(3, NB):
                last = paged_output(b)
            last.then_inc(S["sel_free"], 1)
            pe.wait_ge(S["sw_p"], 1)
            pe.transpose(ps[0:NB, 2, 0:ROWS], sw[0:ROWS, 512:520], ident[0:ROWS, 0:ROWS])
            for kb in range(4):
                last = pe.transpose(ps[:, 3, kb * ROWS:(kb + 1) * ROWS], sw[0:ROWS, kb * P:(kb + 1) * P], ident[0:ROWS, 0:ROWS])
            last.then_inc(S["ptw_ready"], 1)
            pe.wait_ge(S["ptw_done"], 1)
            pe.wait_ge(S["lru_norm"], 1)
            for b in range(NB):
                r = slice(b * NH, (b + 1) * NH)
                o = ps[0:NH, 4 + b // 4, (b % 4) * P:(b % 4 + 1) * P]
                mm(o, pts[0:NB, 10, r], vnew[0:NB, 1, :], start=True, stop=False)
                for kb in range(4):
                    last = mm(o, pts[:, 11 + kb, r], vwin[:, b * 4 + kb, :], start=False, stop=(kb == 3))
            last.then_inc(S["os_ready"], 1)

            pe.wait_ge(S["qz_ready"], 1)

            def scores(u):
                i, br, g = units[u]
                nk = (i + 1) * P
                for r in range(GRP):
                    if u >= 1:
                        pe.wait_ge(S["u_ttr"], GRP * (u - 1) + r + 1)
                    mm(ps[:, r, 0:nk], qz[:, g * GRP + r, i * P:(i + 1) * P], zT[:, (KS, KW)[br], 0:nk],
                       start=True, stop=True).then_inc(S["u_s"], 1)

            for i in range(4):
                for h in range(NH):
                    last = mm(ps[:, 2 + i // 2, ((i % 2) * NH + h) * NCMP_P:((i % 2) * NH + h + 1) * NCMP_P],
                              qz[:, h, i * P:(i + 1) * P], ckT[:, 512:512 + NCMP_P], start=True, stop=True)
            last.then_inc(S["pc_s"], 1)
            pe.wait_ge(S["os_done"], 1)
            for b in range(NB):
                last = pe.transpose(ps[:, 6, b * NH:(b + 1) * NH], osb[0:NH, b * P:(b + 1) * P], ident[0:NH, 0:NH])
            last.then_inc(S["os_ready"], 1)
            pe.wait_ge(S["pc_max"], 1)
            scores(0)
            pe.wait_ge(S["pc_p"], 1)
            for i in range(4):
                if i == 1:
                    pe.wait_ge(S["os_done"], 2)
                if i >= 2:
                    pe.wait_ge(S["pc_tdone"], i - 1)
                for h in range(NH):
                    last = pe.transpose(ps[0:NCMP_P, 4 + 2 * (i % 2) + h // 4, (h % 4) * P:(h % 4 + 1) * P],
                                        pcb[:, i * NH + h, :], ident[:, :])
                last.then_inc(S["pc_t"], 1)

            tcount = [0]

            def apply(u):
                i, br, g = units[u]
                pe.wait_ge(S["u_p"], GRP * (u + 1))
                for kb in range(i + 1):
                    n = tcount[0]
                    if n >= 2:
                        pe.wait_ge(S["u_tdone"], n - 1)
                    for r in range(GRP):
                        last = pe.transpose(ps[:, 4 + n % 2, r * P:(r + 1) * P],
                                            pbuf[:, (u % 2) * GRP + r, kb * P:(kb + 1) * P], ident[:, :])
                    last.then_inc(S["u_t"], 1)
                    tcount[0] += 1
                for kb in range(i + 1):
                    pe.wait_ge(S["u_tdone"], tcount[0] - i + kb)
                    last = mm(ps[:, 6 + g, 0:512], vn[:, br * 4 + kb, :], ptb[:, kb, :],
                              start=False, stop=(br == 1 and kb == i))
                last.then_inc(S["u_pv"], 1)

            pe.wait_ge(S["pc_tdone"], 4)
            for i in range(4):
                for q in range(4):
                    u = 4 * i + q
                    if u < 15:
                        scores(u + 1)
                    if q == 0:
                        if i:
                            pe.wait_ge(S["o_done"], i)
                        for g in range(2):
                            mm(ps[:, 6 + g, 0:512], vc[0:NCMP_P, 8, :], ptcb[0:NCMP_P, i, g * 512:(g + 1) * 512],
                               start=True, stop=False)
                    apply(u)

            def project(c, ks):
                for k in ks:
                    for h in range(2):
                        last = mm(ps[:, 2 + 2 * (c % 3) + h, 0:HALF], wout[:, k, c * P:(c + 1) * P],
                                  zT[:, k, h * HALF:(h + 1) * HALF], start=(k == 0), stop=(k == KD - 1))
                if ks[-1] == KD - 1:
                    last.then_inc(S["pe_step"], 1)
            pe.wait_ge(S["wout_loaded"], 16)
            pe.wait_ge(S["o_done"], 4)
            for c in range(2):
                project(c, range(4))
            pe.wait_ge(S["mix_sq"], 1)
            two(0, lambda k: ones[:, :], lambda k: hT[:, k, :], range(4)).then_inc(S["mix_sum"], 1)
            project(2, range(4))
            pe.wait_ge(S["mix_ready"], 1)
            for c in range(KD):
                if c < 3:
                    project(c, range(4, KD))
                else:
                    pe.wait_ge(S["proj_ready"], c - 2)
                    project(c, range(KD))

            def chunk_sums(x, base):
                for k in range(KD):
                    pe.wait_ge(S["chunk_sq"], base + k + 1)
                    for h in range(2):
                        last = mm(ps[:, h, 0:HALF], ones[:, :], x[:, k, h * HALF:(h + 1) * HALF],
                                  start=(k == 0), stop=(k == KD - 1))
                last.then_inc(S["sum_ready"], 1)
            chunk_sums(x1sq, 0)

            pe.wait_ge(S["sk_loaded"], 16)

            def products(b, weights, moving, ks, first=True, stop=True):
                for n, k in enumerate(ks):
                    for w, m in ((0, 0), (0, 1), (1, 0)):
                        for h in range(2):
                            last = mm(ps[:, b + h, 0:HALF], weights[w](k), moving[m](k)[:, h * HALF:(h + 1) * HALF],
                                      start=(first and n == 0 and w == 0 and m == 0),
                                      stop=(stop and n == len(ks) - 1 and w == 1))
                return last

            def up(blk, slot, item, b, moved, part=0, parts=1):
                if part == 0:
                    pe.wait_ge(S["lo_done"], item + 1)
                    if moved is not None:
                        pe.wait_ge(S["gelu_done"], moved)
                n = KD // parts
                last = products(b, [lambda k: uhs[slot][:, k, :], lambda k: uls[slot][:, k, :]],
                                [lambda k: hh[:, k, :], lambda k: hl[:, k, :]], range(n * part, n * part + n),
                                part == 0, part == parts - 1)
                if part == parts - 1:
                    last.then_inc(S["zz_ready"], 1)

            def up_topk(b):
                if b < 16:
                    up(b, b % 4, b, 2, b if b else None)
                else:
                    up(b, b % 4, b, 2 * (b % 2), b - 1)

            def sub_scores(n):
                pe.wait_ge(S["q_moved"], n + 1)
                if n >= 2:
                    pe.wait_ge(S["s_free"], n - 1)
                b = 4 + 2 * (n % 2)
                for t in range(5):
                    m = P if t < 4 else NB
                    last = mm(ps[0:m, b + t // 4, (t % 4) * P:(t % 4 + 1) * P], qT[:, t * P:t * P + m],
                              sk[:, n, :], start=True, stop=True)
                last.then_inc(S["s_ready"], 1)
            for n in range(16):
                pe.wait_ge(wq_l[n % 3], 16 * (n // 3 + 1))
                if n >= 1:
                    pe.wait_ge(S["q_moved"], n)
                if n == 0:
                    for k in range(KD):
                        pe.wait_ge(S["h_ready"], KD + k + 1)
                        for h in range(2):
                            last = mm(ps[:, h, 0:HALF], wq[:, k, :], h2T[:, k, h * HALF:(h + 1) * HALF],
                                      start=(k == 0), stop=(k == KD - 1))
                else:
                    pe.wait_ge(S["wql_done"], n)
                    last = products(0, [lambda k: wqh[n % 2][:, k, :], lambda k: wql[n % 2][:, k, :]],
                                    [lambda k: hh[:, k, :], lambda k: hl[:, k, :]], range(KD))
                last.then_inc(S["q_ready"], 1)
                up_topk(n)
                sub_scores(n)

            def turn_routes(t):
                m = P if t < 4 else NB
                pe.wait_ge(S["tr_in"], t + 1)
                if t == 0:
                    pe.wait_ge(S["s_free"], 16)
                else:
                    pe.wait_ge(S["tr_done"], t)
                for q in range(3):
                    last = pe.transpose(ps[:, 4 + q, 0:m], isel[0:m, q, :], ident[0:m, 0:m])
                last.then_inc(S["tr_ready"], 1)
            for t in range(5):
                for q in range(TILE_U[t]):
                    up_topk(16 + sum(TILE_U[:t]) + q)
                    if t and q == 2:
                        turn_routes(t - 1)
            turn_routes(4)

            pe.wait_ge(S["tr_done"], 5)
            pe.sem_inc(S["g_ready"], 4)

            def quad(n, q):
                pe.wait_ge(S["oh_ready"], n * 8 + 8)
                pe.wait_ge(S["g_moved"], n + 1)
                for t in range(4):
                    last = mm(ps[:, 4 + q, t * P:(t + 1) * P], oh[:, q * 4 + t, 0:P], oh[:, q * 4 + t, P:2 * P],
                              start=True, stop=True)
                last.then_inc(S["g_ready"], 1)
            with pe.Fori(0, 4) as it:
                for b in range(8):
                    blk = it * 8 + (TOPK_U + b)
                    for q in range(4):
                        quad(it * 32 + (4 * b + q), q)
                        up(blk, b % 2, blk, 2 * (b % 2), blk - 1, q, 4)
            for q in range(2):
                quad(128 + q, q)
            for b in range(TAIL_U):
                blk = HOT_U + b
                up(blk, b % 2, blk, 2 * (b % 2), blk - 1)
            pe.wait_ge(S["g_moved"], 134)

            def up_live(s, jj):
                blk = s * EXP_J + jj
                up(blk, jj % 2, (s - SPILL_G) * 8 + (2 * SPILL + jj), 2 * (jj % 2), blk - 1)

            def down(s, par_, item):
                pe.wait_ge(S["lo_done"], item)
                pe.wait_ge(S["a_ready"], (s + 1) * EXP_J)
                for dc in range(KD):
                    pe.wait_ge(S["ff_free"], s * KD + dc + 1)
                    cols = slice(dc * P, (dc + 1) * P)
                    products(4 + 2 * (dc % 2), [lambda j: vh[:, par_ * EXP_J + j, cols], lambda j: vl[:, par_ * EXP_J + j, cols]],
                             [lambda j: ah[:, par_ * EXP_J + j, :], lambda j: al[:, par_ * EXP_J + j, :]],
                             range(EXP_J)).then_inc(S["ff_ready"], 1)

            pe.sem_inc(S["ff_ready"], 1)
            with pe.Fori(0, SPILL_G // 2) as it:
                for q in range(2):
                    down(it * 2 + q, q, it * 8 + (SPILL + 4 * (q + 1)))
            with pe.Fori(0, (GROUPS - SPILL_G - 1) // 2) as it:
                for q in range(2):
                    s = it * 2 + (SPILL_G + q)
                    for jj in range(EXP_J):
                        up_live(s, jj)
                    down(s - 1, q, it * 16 + (2 * SPILL + 8 * q))
            last = GROUPS - 1
            for jj in range(EXP_J):
                up_live(last, jj)
            down(last - 1, 0, 2 * SPILL + 8 * (last - SPILL_G))
            down(last, 1, 2 * SPILL + 8 * (last - SPILL_G + 1))
            chunk_sums(sq, KD)

        @block.scalar
        def _(act):
            steps = [0]

            def link(ins):
                steps[0] += 1
                ins.then_inc(S["act_step"], 1)
                act.wait_ge(S["act_step"], steps[0])

            def fn(out, in_, f, **kw):
                return act.activation(out, in_, f, **kw)

            act.wait_ge(S["c_loaded"], 16)
            fn(cT, cT, ACT.Silu).then_inc(S["silu_done"], 1)
            act.wait_ge(S["rs_ready"], 1)
            act.wait_ge(S["silu_done"], 1)
            link(fn(rsb[0:NH, 0:512], ps[0:NH, 0, 0:512], ACT.Copy))
            fn(rsb[0:NH, 512:640], ps[0:NH, 1, 0:128], ACT.Copy).then_inc(S["rs_copied"], 1)
            def root(n):
                act.wait_ge(S["root_in"], n)
                fn(rstd, rstd, ACT.Sqrt).then_inc(S["rstd_ready"], 1)
            for n in range(AN):
                act.wait_ge(S["ada_ready"], n + 1)
                if n >= 2:
                    act.wait_ge(S["mt_ready"], n - 1)
                fn(m9[0:9, n % 2, :], ps[0:9, 4 + n % 2, 0:AW], ACT.Copy).then_inc(S["m9_ready"], 1)
                if n == 1:
                    act.wait_ge(S["x_loaded"], 16)
                    fn(hT, xT[:, :, :], ACT.Square).then_inc(S["sq_done"], 1)
                if n in (AK, AV):
                    c = int(n == AV)
                    act.wait_ge(S["hid_ready"], c + 1)
                    link(fn(posb[:, c:c + 1], ps[:, 1, 257:258], ACT.Copy))
                    if c:
                        act.wait_ge(S["ck_ready"], 1)
                    link(fn(hid[:, 0:256], ps[:, 0, 1:257], ACT.Gelu_apprx_tanh, bias=posb[:, c:c + 1]))
                    fn(hid[:, 256:512], ps[:, 1, 1:257], ACT.Gelu_apprx_tanh, bias=posb[:, c:c + 1]).then_inc(S["gelu_ready"], 1)
                if n == AK + 1:
                    act.wait_ge(S["ck_ready"], 1)
                    fn(ckT[:, 0:512], ps[:, 2, 0:512], ACT.Copy).then_inc(S["ck_moved"], 1)
                if n == AV + 1:
                    act.wait_ge(S["ck_ready"], 2)
                    fn(vc[0:NCMP_S, 0:8, :].rearrange("p (q a) b -> p q (a b)", q=2), ps[0:NCMP_S, 2:4, 0:512],
                       ACT.Copy).then_inc(S["ck_moved"], 1)
                if n == AV + 3:
                    root(1)

            act.wait_ge(S["zg_ready"], 1)
            fn(gT[0:24].rearrange("p (h t) -> p h t", h=2), ps[0:24, 6:8, 0:HALF], ACT.Sigmoid).then_inc(S["gates_ready"], 1)
            for n in range(1, ZC, 2):
                act.wait_ge(S["z_ready"], n + 1)
                act.wait_ge(S["z_moved"], n)
                b = 2 * (n % 3)
                fn(zT[:, n, :].rearrange("p (h t) -> p h t", h=2), ps[:, b:b + 2, 0:HALF], ACT.Copy,
                   scale=0.125 if QC <= n < QC + 4 else 1.0).then_inc(S["z_moved"], 1)
                if n == 1:
                    act.wait_ge(S["zg_ready"], 2)
                    link(fn(gates[:, 0:4, :], ps[:, 7, 320:416].rearrange("p (t c) -> p t c", c=24), ACT.Copy))
                    fn(gates[0:NB, 4, :].rearrange("p (h r) -> p h r", r=3),
                       ps[0:NB, 7, 416:440].rearrange("p (r h) -> p h r", h=NH), ACT.Copy).then_inc(S["gates_ready"], 1)
                if n == 13:
                    act.wait_ge(S["lru_prep"], 1)
                    fn(lr(1), lr(0), ACT.Exp, scale=-1.0).then_inc(S["exp_ready"], 1)
                    act.wait_ge(S["lru_prep"], 2)
                    fn(lr(3), lr(2), ACT.Ln).then_inc(S["exp_ready"], 1)
            for c in range(4):
                act.wait_ge(S["gate_ready"], c + 1)
                link(fn(rT[:, c, :].rearrange("p (h t) -> p h t", h=2), ps[:, 0:2, 0:HALF], ACT.Sigmoid,
                        bias=par[:, BA + c:BA + c + 1]))
                fn(iT_[:, c, :].rearrange("p (h t) -> p h t", h=2), ps[:, 2:4, 0:HALF], ACT.Sigmoid,
                   bias=par[:, BI + c:BI + c + 1]).then_inc(S["ri_ready"], 1)
            act.wait_ge(S["lru_prep"], 3)
            act.wait_ge(S["ri_ready"], 4)
            for c in range(4):
                link(fn(aT[:, c, :], rT[:, c, :], ACT.Exp, scale=lr(9)[:, c:c + 1]))
                link(fn(rT[:, c, :], rT[:, c, :], ACT.Tanh, scale=lr(8)[:, c:c + 1]))
            act.sem_inc(S["exp_ready"], 1)
            act.wait_ge(S["hid_ready"], 3)
            fn(hid[:, 512:512 + NCMP_P], ps[:, 7, 128:128 + NCMP_P], ACT.Gelu_apprx_tanh, bias=posb[:, 1:2]).then_inc(S["gelu_ready"], 1)
            fn(zT[:, YG:YG + 4, :], zT[:, YG:YG + 4, :], ACT.Gelu_apprx_tanh).then_inc(S["yg_ready"], 1)
            act.wait_ge(S["lru_prep"], 4)
            fn(rT, rT, ACT.Sqrt).then_inc(S["exp_ready"], 1)
            act.wait_ge(S["ck_ready"], 3)
            link(fn(vc[0:NCMP_P, 8, :], ps[0:NCMP_P, 6, P:2 * P], ACT.Copy))
            act.wait_ge(S["hid_ready"], 4)
            fn(hid[:, 512:512 + NCMP_P], ps[:, 7, 160:160 + NCMP_P], ACT.Gelu_apprx_tanh, bias=posb[:, 0:1]).then_inc(S["gelu_ready"], 1)
            act.wait_ge(S["ck_ready"], 4)
            fn(ckT[:, 512:512 + NCMP_P], ps[:, 7, 192:192 + NCMP_P], ACT.Copy).then_inc(S["cmp_done"], 1)
            act.wait_ge(S["sc_exp"], 1)
            fn(sc[0:ROWS, 0:NCMP_S], sc[0:ROWS, 0:NCMP_S], ACT.Exp, bias=sm(0), accum_out=sm(1)).then_inc(S["sc_exp"], 1)
            act.wait_ge(S["ss_max"], 1)
            fn(ss[0:ROWS], ss[0:ROWS], ACT.Exp, bias=sm(4), accum_out=sm(5)).then_inc(S["ss_exp"], 1)
            root(2)
            act.wait_ge(S["sw_max"], 1)
            fn(sw[0:ROWS], sw[0:ROWS], ACT.Exp, bias=sm(8), accum_out=sm(9)).then_inc(S["sw_exp"], 1)
            act.wait_ge(S["pc_max"], 1)
            fn(pcb, pcb, ACT.Exp).then_inc(S["pc_exp"], 1)
            for u, (i, br, g) in enumerate(units):
                nk = (i + 1) * P
                act.wait_ge(S["u_max"], u + 1)
                for r in range(GRP):
                    fn(pbuf[:, (u % 2) * GRP + r, 0:nk], pbuf[:, (u % 2) * GRP + r, 0:nk], ACT.Exp,
                       bias=pst(u, 1)[:, r:r + 1], accum_out=pst(u, 2)[:, r:r + 1]).then_inc(S["u_exp"], 1)
                act.wait_ge(S["u_exp"], GRP * (u + 1))
                act.wait_ge(S["u_rs"], u + 1)
                for r in range(GRP):
                    fn(pbuf[:, (u % 2) * GRP + r, 0:nk], pbuf[:, (u % 2) * GRP + r, 0:nk], ACT.Copy,
                       scale=pst(u, 3)[:, r:r + 1]).then_inc(S["u_p"], 1)
            act.wait_ge(S["o_done"], 4)
            fn(hT[:, 0:4, :], zT[:, 4:8, :], ACT.Square).then_inc(S["mix_sq"], 1)
            root(3)
            for k in range(KD):
                act.wait_ge(S["proj_ready"], k + 1)
                fn(x1sq[:, k, :], xT[:, k, :], ACT.Square).then_inc(S["chunk_sq"], 1)
            root(4)
            def high(dst, slot, item_round):
                act.wait_ge(raw_l[slot], item_round * 16)
                fn(dst, raw[:, slot, :], ACT.Copy).then_inc(S["hi_done"], 1)

            def high_u(b, jj, item_round):
                act.wait_ge(S["zz_ready"], b - 1)
                high(uhs[jj % 2].rearrange("p k i -> p (k i)"), jj % 4, item_round)

            def high_topk(b):
                if b >= 4:
                    act.wait_ge(S["zz_ready"], b - 3)
                slot = b % 4 if b < TOPK_U else b % 2
                high(uhs[slot].rearrange("p k i -> p (k i)"), b % 4, b // 4 + 1)

            def gelu(blk, slot, b, dst=zbuf):
                act.wait_ge(S["zz_ready"], blk + 1)
                fn(dst[:, slot, :].rearrange("p (h t) -> p h t", h=2),
                   ps[:, b:b + 2, 0:HALF], ACT.Gelu_apprx_tanh).then_inc(S["gelu_done"], 1)

            def topk_block(b):
                if b >= 2:
                    act.wait_ge(zst[b % 2], 16 * (b // 2))
                gelu(b, b % 2, 2 if b < 16 else 2 * (b % 2))
                if b + 4 < TOPK_U + 2:
                    high_topk(b + 4)
            act.wait_ge(S["proj_done"], 1)
            for b in range(4):
                high_topk(b)
            act.wait_ge(S["h_ready"], 2 * KD)
            fn(hh[:, :, :], h2T, ACT.Copy).then_inc(S["rounded"], 1)

            def high_wq(n):
                act.wait_ge(wq_l[n % 3], 16 * (n // 3 + 1))
                fn(wqh[n % 2], wq[:, (n % 3) * KD:(n % 3 + 1) * KD, :], ACT.Copy).then_inc(S["rounded"], 1)
            high_wq(1)
            for n in range(16):
                act.wait_ge(S["q_ready"], n + 1)
                if n >= 1:
                    act.wait_ge(S["s_ready"], n)
                fn(qT.rearrange("p (h t) -> p h t", h=2), ps[:, 0:2, 0:HALF],
                   ACT.Identity, bias=par[:, BQ + n:BQ + n + 1]).then_inc(S["q_moved"], 1)
                if n + 2 < 16:
                    high_wq(n + 2)
                topk_block(n)
            for t in range(5):
                m = P if t < 4 else NB
                early = sum(len(tile_splits(t, point)) for point in range(4))
                for q in range(early):
                    topk_block(16 + sum(TILE_U[:t]) + q)
                act.wait_ge(S["rexp"], t + 1)
                fn(best[0:m], best[0:m], ACT.Exp).then_inc(S["rexp_done"], 1)
                for q in range(early, TILE_U[t]):
                    topk_block(16 + sum(TILE_U[:t]) + q)
            act.wait_ge(S["tr_done"], 5)
            act.sem_inc(S["g_moved"], 4)

            def move_quad(n, q, dst):
                act.wait_ge(S["g_ready"], n + 5)
                fn(dst, ps[:, 4 + q, 0:512].rearrange("p (t j) -> p j t", j=P), ACT.Copy).then_inc(S["g_moved"], 1)

            def stage_round(it, c, first=False):
                st = stage[:, c, :].rearrange("p (j t) -> p j t", t=TC)
                if not first:
                    act.wait_ge(st_l[c], it * 16)
                for b in range(4):
                    for q in range(4):
                        t0 = 16 * b + 4 * q
                        move_quad(it * 32 + (16 * c + 4 * b + q), q, st[:, :, t0:t0 + 4])
                    blk = it * 8 + (TOPK_U + 4 * c + b)
                    act.wait_ge(zst[b % 2], it * 64 + (8 * (TOPK_U + 4 * c + b - b % 2)))
                    gelu(blk, b % 2, 2 * (b % 2))
                    high_u(blk + 2, b + 2, it * 2 + ((TOPK_U + 4 * c + b + 2) // 4 + 1))
            for c in range(2):
                stage_round(0, c, first=True)
            with act.Fori(1, 4) as it:
                for c in range(2):
                    stage_round(it, c)
            act.wait_ge(st_l[0], 64)
            for q in range(2):
                move_quad(128 + q, q, stage[:, 0, 0:8 * P].rearrange("p (j t) -> p j t", t=8)[:, :, 4 * q:4 * q + 4])

            def high_v(s, par_, jj, item_round):
                high(vh[:, par_ * EXP_J + jj, :], jj, item_round)

            def tail_gelu(b):
                act.wait_ge(zst[b % 2], 16 * ((HOT_U + b) // 2))
                gelu(HOT_U + b, b % 2, 2 * (b % 2), ztail)
            for b in range(TAIL_U - 2):
                tail_gelu(b)
                high_u(HOT_U + b + 2, b + 2, (HOT_U + b + 2) // 4 + 1)
            act.wait_ge(st_l[0], 80)
            act.wait_ge(st_l[1], 64)
            for jj in range(EXP_J):
                high_v(0, 0, jj, SPILL // 4 + 1)
            for b in range(TAIL_U - 2, TAIL_U):
                tail_gelu(b)

            def free_v(s):
                act.wait_ge(S["ff_ready"], (s - 1) * KD + 1)
            with act.Fori(0, SPILL_G // 2) as it:
                for q in range(2):
                    s = it * 2 + (q + 1)
                    free_v(s)
                    for jj in range(EXP_J):
                        high_v(s, 1 - q, jj, it * 2 + (SPILL // 4 + q + 2))
            r0 = 2 * SPILL // 4 + 1
            for jj in range(2):
                high_u(SPILL + jj, jj, r0)

            def live(s, par_, rnd, more):
                for jj in range(EXP_J):
                    blk = s * EXP_J + jj
                    act.wait_ge(S["a_ready"], blk - 1)
                    gelu(blk, jj % 2, 2 * (jj % 2))
                    if jj < 2:
                        high_u(blk + 2, jj + 2, rnd)
                    else:
                        if jj == 2:
                            free_v(s)
                        high_v(s, par_, jj - 2, rnd + 1)
                for jj in range(2, EXP_J):
                    high_v(s, par_, jj, rnd + 1)
                if more:
                    for jj in range(2):
                        high_u((s + 1) * EXP_J + jj, jj, rnd + 2)
            with act.Fori(0, (GROUPS - SPILL_G - 1) // 2) as it:
                for q in range(2):
                    live(it * 2 + (SPILL_G + q), 1 - q, it * 4 + (r0 + 2 * q), True)
            live(GROUPS - 1, 1, r0 + 2 * (GROUPS - 1 - SPILL_G), False)
            root(5)

        @block.vector
        def _(dve):
            steps = [0]

            def link(*group):
                for ins in group:
                    steps[0] += 1
                    ins.then_inc(S["dve_step"], 1)
                dve.wait_ge(S["dve_step"], steps[0])

            tt, ts, cp = dve.tensor_tensor, dve.tensor_scalar, dve.tensor_copy
            stt = dve.scalar_tensor_tensor

            link(dve.memset(w1, 0.0), dve.memset(w2, 0.0), dve.memset(zeros, 0.0), dve.memset(ones[:, :], 1.0))
            dve.sem_inc(S["zero_done"], 1)
            dve.wait_ge(S["table_loaded"], 64)
            link(dve.memset(rb[32:33], NEG), dve.memset(rbx[32:33], NEG))
            dve.sem_inc(S["rb_ready"], 1)
            dve.wait_ge(S["par_loaded"], 32)
            def whole_scale(part, gain):
                v = mT[:, 8 * part:8 * part + 8, :]
                link(ts(v, v, 1.0, None, ADD))
                link(tt(v, v, par[:, gain:gain + 8].to_broadcast([P, 8, 9]), MUL))

            def inverse_ms(width, b):
                r = rstd.rearrange("p (h t) -> p h t", h=2)
                link(ts(r, ps[:, b:b + 2, 0:HALF], 1.0 / width, EPS, MUL, ADD))
                dve.reciprocal(rstd, rstd).then_inc(S["root_in"], 1)

            def normed(dst, sums, roots):
                dve.wait_ge(S["sum_ready"], sums)
                inverse_ms(D, 0)
                dve.wait_ge(S["rstd_ready"], roots)
                link(tt(dst, xT[:, :, :], rstd.rearrange("p (o t) -> p o t", o=1).to_broadcast([P, KD, TOK]), MUL))

            def shifted(dst, part):
                sh, scl = mT[:, 8 * part:8 * part + 8, :], mT[:, 8 * part + 8:8 * part + 16, :]
                link(tt(dst[:, :, SEQ:TOK], dst[:, :, SEQ:TOK], scl[:, :, 1:9], MUL))
                link(tt(dst[:, :, SEQ:TOK], dst[:, :, SEQ:TOK], sh[:, :, 1:9], ADD))
                for k in range(KD):
                    ts(dst[:, k, 0:SEQ], dst[:, k, 0:SEQ], scl[:, k, 0:1], sh[:, k, 0:1], MUL, ADD).then_inc(S["h_ready"], 1)
            for n in range(AN):
                dve.wait_ge(S["mt_ready"], n + 1)
                tt(mT[:, 3 * n:3 * n + 3, :], ps[:, 6 + n % 2, 0:27].rearrange("p (q c) -> p q c", c=9),
                   par[:, ADB + 3 * n:ADB + 3 * n + 3].to_broadcast([P, 3, 9]), ADD).then_inc(S["mt_done"], 1)
                if n == 2:
                    dve.wait_ge(S["pb_ready"], 1)
                    link(cp(pbias, ps[:, 2, 0:QM * NH].rearrange("p (m h) -> p h m", h=NH)))
                if n == AV + 2:
                    dve.wait_ge(S["mt_done"], n + 1)
                    whole_scale(1, N1G)
                    normed(hT, 1, 1)
                if n == AV + 3:
                    shifted(hT, 0)
            dve.wait_ge(S["mt_done"], AN)
            whole_scale(4, N2G)
            dve.wait_ge(S["scratch_stored"], 16)
            link(dve.memset(wlru, 0.0))
            dve.sem_inc(S["hi_ready"], 1)
            def cw(k, c):
                return par[:, CW + 4 * k + c:CW + 4 * k + c + 1]

            def convolve(c):
                x = zT[:, XR + c, :]
                link(ts(xcT[:, c, :], x, cw(3, c), par[:, CB + c:CB + c + 1], MUL, ADD))
                for k in (2, 1, 0):
                    s = 3 - k
                    link(stt(xcT[:, c, s:SEQ], x[:, 0:SEQ - s], cw(k, c), xcT[:, c, s:SEQ], MUL, ADD),
                         stt(xcT[:, c, SEQ:TOK], stc[:, c, k * NB:(k + 1) * NB], cw(k, c), xcT[:, c, SEQ:TOK], MUL, ADD))
                dve.sem_inc(S["xc_ready"], 1)

            def conv_state():
                oc = outc.rearrange("p c (k s) -> p c k s", s=9)
                link(cp(oc[:, :, :, 0], zT[:, XR:XR + 4, SEQ - 3:SEQ]),
                     cp(oc[:, :, 0:2, 1:9], stc.rearrange("p c (k s) -> p c k s", s=NB)[:, :, 1:3, :]),
                     cp(oc[:, :, 2, 1:9], zT[:, XR:XR + 4, SEQ:TOK]))

            def queries():
                dve.wait_ge(S["zg_ready"], 2)
                link(dve.memset(qpad, 0.0), dve.memset(qs, 0.0))
                qpf = qpad.rearrange("p b r -> p (b r)")
                grp = []
                for g in range(2):
                    rows = slice(g * HD, (g + 1) * HD)
                    for r in range(GRP):
                        c = g * GRP + r
                        grp.append(cp(qs[rows, c:ROWS:NH], zT[rows, QC + r, SEQ:TOK]))
                        grp.append(cp(qpf[rows, c:NB * ROWS:ROWS + NH], zT[rows, QC + r, SEQ:TOK]))
                link(*grp)
                dve.sem_inc(S["qpad_ready"], 1)

            def decay():
                lam = par[:, LAM:LAM + 4]
                link(ts(lr(0), lam, -1.0, None, MUL))
                link(tt(lr(0), lr(0), lam, MAX))
                dve.sem_inc(S["lru_prep"], 1)
                dve.wait_ge(S["exp_ready"], 1)
                link(ts(lr(2), lr(1), 1.0, None, ADD))
                dve.sem_inc(S["lru_prep"], 1)
                link(ts(lr(4), lr(2), 1.0, None, SUB))
                link(ts(lr(5), lr(4), 0.0, None, EQ))
                link(tt(lr(4), lr(4), lr(5), ADD))
                link(dve.reciprocal(lr(4), lr(4)))
                link(tt(lr(4), lr(4), lr(1), MUL))
                link(tt(lr(5), lr(5), lr(1), MUL))
                dve.wait_ge(S["exp_ready"], 2)
                link(tt(lr(3), lr(3), lr(4), MUL))
                link(tt(lr(3), lr(3), lr(5), ADD))
                link(ts(lr(6), lam, -1.0, 0.0, MUL, MAX))
                link(tt(lr(3), lr(3), lr(6), ADD))
                link(ts(lr(8), lr(3), 8.0, None, MUL), ts(lr(9), lr(3), -8.0, None, MUL))
                dve.sem_inc(S["lru_prep"], 1)

            for n in range(0, ZC, 2):
                dve.wait_ge(S["z_ready"], n + 1)
                if n:
                    dve.wait_ge(S["z_moved"], n)
                b = 2 * (n % 3)
                ts(zT[:, n, :].rearrange("p (h t) -> p h t", h=2), ps[:, b:b + 2, 0:HALF],
                   0.125 if QC <= n < QC + 4 else 1.0, None, MUL).then_inc(S["z_moved"], 1)
                if n == 4:
                    dve.wait_ge(S["lrus_loaded"], 32)
                if 4 <= n <= 10:
                    convolve((n - 4) // 2)
                if n == 12:
                    queries()
                if n == 14:
                    decay()
                if n == 16:
                    conv_state()
            dve.wait_ge(S["z_moved"], ZC)
            dve.wait_ge(S["vt_ready"], 1)
            grp = []
            for br in range(2):
                grp.append(cp(vn[:, br * 4:(br + 1) * 4, :].rearrange("p k c -> p (k c)"), ps[:, 4 + br, 0:512]))
            grp.append(cp(vnew[0:NB].rearrange("p a b -> p (a b)"), ps[0:NB, 6, 2 * P:4 * P]))
            link(*grp)
            dve.sem_inc(S["vt_done"], 1)
            dve.wait_ge(S["exp_ready"], 3)
            link(ts(uT, rT, 1.0, None, ADD))
            link(dve.reciprocal(uT, uT))
            link(stt(rT, rT, 2.0, uT, MUL, MUL))
            dve.sem_inc(S["lru_prep"], 1)
            link(tt(iT_, iT_, xcT, MUL))
            dve.wait_ge(S["exp_ready"], 4)
            link(tt(uT, rT, iT_, MUL))
            link(*[dve.tensor_tensor_scan(xcT[:, c, 0:SEQ], aT[:, c, 0:SEQ], uT[:, c, 0:SEQ], 0.0, MUL, ADD)
                   for c in range(4)])
            link(tt(xcT[:, :, SEQ:TOK], aT[:, :, SEQ:TOK], h0T, MUL))
            link(tt(xcT[:, :, SEQ:TOK], xcT[:, :, SEQ:TOK], uT[:, :, SEQ:TOK], ADD))
            link(cp(outh, xcT[:, :, SEQ - 1:TOK]))
            dve.wait_ge(S["yg_ready"], 1)
            link(tt(zT[:, 0:4, :], xcT, zT[:, YG:YG + 4, :], MUL))
            link(tt(aT, zT[:, 0:4, :], zT[:, 0:4, :], MUL))
            dve.sem_inc(S["lru_ready"], 1)
            R = slice(0, ROWS)
            dve.wait_ge(S["const_loaded"], 64)
            dve.wait_ge(S["gate_moved"], 16)
            dve.wait_ge(S["sc_ready"], 1)
            link(cp(sc[R, 0:NCMP_S], ps[R, 3, 0:NCMP_S]))
            link(dve.tensor_reduce(sm(0), sc[R, 0:NCMP_S], AX.X, MAX, negate=True))
            dve.sem_inc(S["sc_exp"], 1)
            dve.wait_ge(S["sc_exp"], 2)
            link(dve.reciprocal(sm(2), sm(1)))
            link(ts(gs[R, 0:NCMP_S], sc[R, 0:NCMP_S], sm(2), None, MUL))
            dve.sem_inc(S["sc_soft"], 1)
            link(ts(sc[R, 0:NCMP_S], gs[R, 0:NCMP_S], gate_rows[:, 0:1], None, MUL))
            dve.wait_ge(S["sum_done"], 1)
            link(cp(gs[R, 0:NCMP_S], ps[R, 2, 64:64 + NCMP_S]))
            bs, flag, pen = small[R, 220:234], small[R, 240:254], small[R, 260:274]

            def cover(t):
                return gs[R, 3 + t:3 + t + 4 * (NSELB - 1) + 1:4]
            link(tt(bs, cover(0), cover(1), ADD))
            for t in range(2, 5):
                link(tt(bs, bs, cover(t), ADD))
            link(dve.tensor_reduce(sm(12), bs, AX.X, MIN))
            link(ts(flag, bs, sm(12), None, EQ))
            link(tt(flag, flag, blkno[R, 0:NSELB], MUL))
            link(dve.tensor_reduce(sm(13), flag, AX.X, MAX))
            link(ts(pen, blkno[R, 0:NSELB], sm(13), NEG, EQ, MUL))
            dve.wait_ge(S["hid_ready"], 4)
            dve.wait_ge(S["ss_ready"], 1)
            link(cp(ss[R, 0:1024], ps[R, 0:2, 0:512]), tt(ss[R, 1024:1032], ps[R, 2, 0:NB], newmask[R], ADD))
            mid = ss[R, 64:64 + NSELB * 64].rearrange("p (j s) -> p j s", s=64)
            link(tt(mid, mid, pen.to_broadcast([ROWS, NSELB, 64]), ADD))
            link(dve.tensor_reduce(sm(4), ss[R, 0:1032], AX.X, MAX, negate=True))
            dve.sem_inc(S["ss_max"], 1)
            dve.wait_ge(S["ss_exp"], 1)
            link(dve.reciprocal(sm(6), sm(5)))
            link(tt(sm(6), sm(6), gate_rows[:, 1:2], MUL))
            link(ts(ss[R, 0:1032], ss[R, 0:1032], sm(6), None, MUL))
            dve.sem_inc(S["ss_p"], 1)
            dve.wait_ge(S["pts_ready"], 1)
            link(cp(pts[0:NCMP_S, 0, :], ps[0:NCMP_S, 3, 0:ROWS]), cp(pts[0:NB, 1, :], ps[0:NB, 3, ROWS:2 * ROWS]),
                 cp(pts[:, 2:10, :].rearrange("p a b -> p (a b)"), ps[:, 6, 0:512]))
            dve.sem_inc(S["pts_done"], 1)
            dve.wait_ge(S["mix_sum"], 1)
            inverse_ms(512, 4)
            dve.wait_ge(S["rstd_ready"], 2)
            link(*[stt(zT[:, c, :], zT[:, c, :], par[:, NLG + c:NLG + c + 1], rstd, MUL, MUL) for c in range(4)])
            dve.wait_ge(S["lru_stored"], 32)
            dve.sem_inc(S["lru_norm"], 1)
            dve.wait_ge(S["sw_ready"], 1)
            link(cp(sw[R, 0:512], ps[R, 0, 0:512]), tt(sw[R, 512:520], ps[R, 1, 0:NB], newmask[R], ADD))
            link(dve.tensor_reduce(sm(8), sw[R, 0:520], AX.X, MAX, negate=True))
            dve.sem_inc(S["sw_max"], 1)
            dve.wait_ge(S["sw_exp"], 1)
            link(dve.reciprocal(sm(10), sm(9)))
            link(tt(sm(10), sm(10), gate_rows[:, 2:3], MUL))
            link(ts(sw[R, 0:520], sw[R, 0:520], sm(10), None, MUL))
            dve.sem_inc(S["sw_p"], 1)
            dve.wait_ge(S["ptw_ready"], 1)
            link(cp(pts[0:NB, 10, :], ps[0:NB, 2, 0:ROWS]),
                 cp(pts[:, 11:15, :].rearrange("p a b -> p (a b)"), ps[:, 3, 0:256]))
            dve.sem_inc(S["ptw_done"], 1)
            dve.wait_ge(S["sel_free"], 1)
            link(dve.memset(qz, 0.0))
            link(*[cp(qz[g * HD:(g + 1) * HD, g * GRP + r, :], zT[g * HD:(g + 1) * HD, QC + r, 0:SEQ])
                   for g in range(2) for r in range(GRP)])
            dve.sem_inc(S["qz_ready"], 1)
            dve.wait_ge(S["os_ready"], 1)
            o2 = osb[0:NH].rearrange("p (a f) -> p a f", a=2)
            link(cp(o2, ps[0:NH, 6:8, 0:512]))
            link(tt(o2, o2, ps[0:NH, 4:6, 0:512], ADD))
            dve.sem_inc(S["os_done"], 1)


            def ttr(u):
                i, br, g = units[u]
                nk = (i + 1) * P
                if u >= 2:
                    dve.wait_ge(S["u_t"], sum(units[v][0] + 1 for v in range(u - 1)))
                for r in range(GRP):
                    dve.wait_ge(S["u_s"], GRP * u + r + 1)
                    dve.tensor_tensor_reduce(pbuf[:, (u % 2) * GRP + r, 0:nk], ps[:, r, 0:nk],
                                             biasT[:, g * GRP + r, 384 - P * i:384 - P * i + nk],
                                             1.0, -3e38, ADD, MAX, pst(u, 0)[:, r:r + 1]).then_inc(S["u_ttr"], 1)
                dve.wait_ge(S["u_ttr"], GRP * (u + 1))
                ts(pst(u, 1), pst(u, 0), -1.0, None, MUL).then_inc(S["u_max"], 1)

            def scale(u):
                i, br, g = units[u]
                dve.wait_ge(S["u_exp"], GRP * (u + 1))
                link(dve.reciprocal(pst(u, 3), pst(u, 2)))
                h = (br + 1) * NH + g * GRP
                tt(pst(u, 3), pst(u, 3), gates[:, i, h:h + GRP], MUL).then_inc(S["u_rs"], 1)

            tcount = [0]

            def evac(u):
                for kb in range(units[u][0] + 1):
                    tcount[0] += 1
                    dve.wait_ge(S["u_t"], tcount[0])
                    if u >= 1:
                        dve.wait_ge(S["u_pv"], u)
                    cp(ptb[:, kb, :], ps[:, 4 + (tcount[0] - 1) % 2, 0:512]).then_inc(S["u_tdone"], 1)

            dve.wait_ge(S["pc_s"], 1)
            link(*[tt(pcb[:, i * NH:(i + 1) * NH, :],
                      ps[:, 2 + i // 2, (i % 2) * NH * NCMP_P:(i % 2 + 1) * NH * NCMP_P].rearrange("p (h n) -> p h n", n=NCMP_P),
                      pbias[:, :, 24 - 8 * i:24 - 8 * i + NCMP_P], ADD) for i in range(4)])
            link(dve.tensor_reduce(pcm[:, 0, :], pcb, AX.X, MAX))
            link(tt(pcb, pcb, pcm[:, 0, :].to_broadcast([P, 4 * NH, NCMP_P]), SUB))
            dve.sem_inc(S["pc_max"], 1)
            dve.wait_ge(S["os_ready"], 2)
            grp = []
            for g in range(2):
                rows = slice(g * HD, (g + 1) * HD)
                o_ = ps[rows, 6, 0:ROWS].rearrange("p (b g r) -> p g r b", g=2, r=GRP)
                grp.append(cp(zT[rows, 4:8, SEQ:TOK], o_[:, g]))
            link(*grp)
            dve.sem_inc(S["os_done"], 1)
            dve.wait_ge(S["pc_exp"], 1)
            link(dve.tensor_reduce(pcm[:, 1, :], pcb, AX.X, ADD))
            link(dve.reciprocal(pcm[:, 1, :], pcm[:, 1, :]))
            inv = pcm[:, 1, :].rearrange("p (i h) -> p i h", h=NH)
            link(tt(inv, inv, gates[:, 0:4, 0:NH], MUL))
            link(ts(inv[:, 0, :], inv[:, 0, :], validq, None, MUL))
            link(tt(pcb, pcb, pcm[:, 1, :].to_broadcast([P, 4 * NH, NCMP_P]), MUL))
            dve.sem_inc(S["pc_p"], 1)
            dve.wait_ge(S["bias_loaded"], 16)
            ttr(0)
            for i in range(4):
                dve.wait_ge(S["pc_t"], i + 1)
                link(*[cp(ptcb[0:NCMP_P, i, q * 512:(q + 1) * 512], ps[0:NCMP_P, 4 + 2 * (i % 2) + q, 0:512]) for q in range(2)])
                dve.sem_inc(S["pc_tdone"], 1)
            for i in range(4):
                for q in range(4):
                    u = 4 * i + q
                    scale(u)
                    if u < 15:
                        ttr(u + 1)
                    evac(u)
                dve.wait_ge(S["u_pv"], 4 * i + 4)
                link(*[cp(zT[g * HD:(g + 1) * HD, 4:8, i * P:(i + 1) * P],
                          ps[g * HD:(g + 1) * HD, 6 + g, 0:512].rearrange("p (r q) -> p r q", q=P)) for g in range(2)])
                dve.sem_inc(S["o_done"], 1)
            dve.wait_ge(S["mix_sum"], 2)
            inverse_ms(512, 0)
            dve.wait_ge(S["rstd_ready"], 3)
            link(*[stt(zT[:, 4 + c, :], zT[:, 4 + c, :], par[:, NAG + c:NAG + c + 1], rstd, MUL, MUL) for c in range(4)])
            dve.sem_inc(S["mix_ready"], 1)

            def add_gated(x, c, src0, src1, part):
                gcol = mT[:, 8 * part + c, :]
                link(*[stt(x[:, c, a:b], s, gcol[:, 0:1], x[:, c, a:b], MUL, ADD) for a, b, s in src0])
                link(tt(small[:, 0:NB], src1, gcol[:, 1:9], MUL))
                link(tt(x[:, c, SEQ:TOK], x[:, c, SEQ:TOK], small[:, 0:NB], ADD))
            for c in range(KD):
                dve.wait_ge(S["pe_step"], c + 1)
                b = 2 + 2 * (c % 3)
                add_gated(xT, c, [(0, HALF, ps[:, b, 0:HALF]), (HALF, SEQ, ps[:, b + 1, 0:SEQ - HALF])],
                          ps[:, b + 1, SEQ - HALF:HALF], 2)
                dve.sem_inc(S["proj_ready"], 1)
            dve.sem_inc(S["proj_done"], 1)
            dve.wait_ge(S["kv_stored"], 16)
            normed(h2T, 2, 4)
            shifted(h2T, 3)
            dve.wait_ge(S["h_ready"], 2 * KD)
            dve.wait_ge(S["rounded"], 1)
            link(tt(hl[:, :, :], h2T, hh[:, :, :].bitcast(F32), SUB))

            def low(dst, hi, slot, item):
                dve.wait_ge(S["hi_done"], item + 1)
                tt(dst, raw[:, slot, :], hi.bitcast(F32), SUB).then_inc(S["lo_done"], 1)

            def low_u(jj, item, slots=2):
                low(uls[jj % slots].rearrange("p k i -> p (k i)"), uhs[jj % slots].rearrange("p k i -> p (k i)"),
                    jj % 4, item)

            def low_v(par_, jj, item):
                low(vl[:, par_ * EXP_J + jj, :], vh[:, par_ * EXP_J + jj, :], jj, item)
            for b in range(4):
                low_u(b, b, 4)

            def low_wq(n):
                dve.wait_ge(S["rounded"], n + 1)
                tt(wql[n % 2], wq[:, (n % 3) * KD:(n % 3 + 1) * KD, :], wqh[n % 2].bitcast(F32), SUB).then_inc(S["wql_done"], 1)
            low_wq(1)

            for n in range(16):
                dve.wait_ge(S["s_ready"], n + 1)
                b = 4 + 2 * (n % 2)
                tiles = []
                for t in range(5):
                    m = P if t < 4 else NB
                    tiles.append((slice(0, m), t, ps[0:m, b + t // 4, (t % 4) * P:(t % 4 + 1) * P]))
                link(*[dve.max(sv[r, 16 * t + n, 0:8], s) for r, t, s in tiles])
                link(*[dve.max_index(si[r, 16 * t + n, 0:8], sv[r, 16 * t + n, 0:8], s) for r, t, s in tiles])
                link(*[dve.match_replace(tmpk[r, t, :], sv[r, 16 * t + n, 0:8], s, -3e38) for r, t, s in tiles])
                dve.sem_inc(S["s_free"], 1)
                if n + 2 < 16:
                    low_wq(n + 2)
                link(*[dve.max(sv[r, 16 * t + n, 8:16], tmpk[r, t, :]) for r, t, s in tiles])
                low_u(n + 4, n + 4, 4)
                link(*[dve.max_index(si[r, 16 * t + n, 8:16], sv[r, 16 * t + n, 8:16], tmpk[r, t, :]) for r, t, s in tiles])

            def routes_in(t):
                m = P if t < 4 else NB
                dve.wait_ge(S["tr_ready"], t + 1)
                link(cp(routeT[:, :, t * P:t * P + m], ps[:, 4:7, 0:m]))
                dve.sem_inc(S["tr_done"], 1)
            dve.wait_ge(S["bias_ready"], 2)
            for t in range(5):
                r = slice(0, P if t < 4 else NB)
                m = r.stop

                def split_next(point):
                    for q in tile_splits(t, point):
                        item = 20 + sum(TILE_U[:t]) + q
                        low_u(item, item, 4)
                link(cp(sif[r, 16 * t:16 * t + 16, :], si[r, 16 * t:16 * t + 16, :]))
                s0, s1 = sv[r, 16 * t:16 * t + 16:2, :], sv[r, 16 * t + 1:16 * t + 16:2, :]
                link(*[tt(cand[r, h, :].rearrange("p (a b) -> p a b", a=16), s0[:, h, :].to_broadcast([m, 16, 16]),
                          s1[:, h, :].rearrange("p (o b) -> p o b", o=1).to_broadcast([m, 16, 16]), ADD) for h in range(NH)])
                split_next(0)
                ci3 = ci[r].rearrange("p (h k) -> p h k", k=16)
                link(*[dve.max(best[r, h, 0:8], cand[r, h, :]) for h in range(NH)])
                link(*[dve.max_index(ci3[:, h, 0:8], best[r, h, 0:8], cand[r, h, :]) for h in range(NH)])
                split_next(1)
                link(*[dve.match_replace(cand2[r, h, :], best[r, h, 0:8], cand[r, h, :], -3e38) for h in range(NH)])
                link(*[dve.max(best[r, h, 8:16], cand2[r, h, :]) for h in range(NH)])
                split_next(2)
                link(*[dve.max_index(ci3[:, h, 8:16], best[r, h, 8:16], cand2[r, h, :]) for h in range(NH)])
                split_next(3)
                link(cp(gden[r, 0, :], best[r, :, 0]))
                link(tt(best[r], best[r], gden[r, 0, :].to_broadcast([m, NH, 16]), SUB))
                dve.sem_inc(S["rexp"], 1)
                link(ts(cab[r, 0, :], ci[r], 4, None, ALU.logical_shift_right), ts(cab[r, 1, :], ci[r], 15, None, ALU.bitwise_and))
                link(cp(cabf[r], cab[r]))
                for w in range(2):
                    eqv = cand[r].rearrange("p h (k a) -> p (h k) a", a=16)
                    link(tt(eqv, cabf[r, w, :].to_broadcast([m, P, 16]),
                            iota16[r].rearrange("p (o a) -> p o a", o=1).to_broadcast([m, P, 16]), EQ))
                    link(*[tt(cand2[r, h, :].rearrange("p (k a) -> p k a", a=16), cand[r, h, :].rearrange("p (k a) -> p k a", a=16),
                              sif[r, 16 * t + 2 * h + w, :].rearrange("p (o a) -> p o a", o=1).to_broadcast([m, 16, 16]), MUL)
                           for h in range(NH)])
                    split_next(4 + 2 * w)
                    if t and w == 0:
                        routes_in(t - 1)
                    link(dve.tensor_reduce(isel[r, w, :], cand2[r].rearrange("p h (k a) -> p (h k) a", a=16), AX.X, ADD))
                    split_next(5 + 2 * w)
                dve.wait_ge(S["rexp_done"], t + 1)
                link(dve.tensor_reduce(gden[r, 1, :], best[r], AX.X, ADD))
                link(dve.reciprocal(gden[r, 1, :], gden[r, 1, :]))
                link(tt(isel[r, 2, :].rearrange("p (h k) -> p h k", k=16), best[r], gden[r, 1, :].to_broadcast([m, NH, 16]), MUL))
                dve.sem_inc(S["tr_in"], 1)
            routes_in(4)

            def quad(n, q, tok0):
                dve.wait_ge(S["g_ready"], n + 1)
                for t in range(4):
                    tok = tok0 + t
                    dst = oh[:, 4 * q + t, :]
                    ts(dst[:, 0:P], iota, routeT[:, 0, bass.ds(tok, 1)], None, EQ).then_inc(S["oh_ready"], 1)
                    ts(dst[:, P:2 * P], iota, routeT[:, 1, bass.ds(tok, 1)], routeT[:, 2, bass.ds(tok, 1)],
                       EQ, MUL).then_inc(S["oh_ready"], 1)
            with dve.Fori(0, 4) as it:
                for b in range(8):
                    for q in range(4):
                        quad(it * 32 + (4 * b + q), q, it * 128 + (16 * b + 4 * q))
                        if q == 0:
                            low_u(TOPK_U + b, it * 8 + (TOPK_U + b))
            for q in range(2):
                quad(128 + q, q, 512 + 4 * q)
            for b in range(TAIL_U - 2):
                low_u(b, HOT_U + b)

            dve.wait_ge(S["x_spilled"], 16)
            link(dve.memset(acc, 0.0))
            dve.sem_inc(S["ff_free"], 2)

            def weigh(s, par_, jj):
                w = EXP_J * TC
                blk = s * EXP_J + jj
                z = zbuf[:, jj % 2, :]
                g = gr[:, par_, 0:8 * w].rearrange("p (c j t) -> p c j t", j=EXP_J, t=TC)[:, :, jj, :]
                zp = z[:, 0:SEQ].rearrange("p (c t) -> p c t", t=TC)
                tt(zp, zp, g, MUL).then_inc(S["a_step"], 1)
                tt(z[:, SEQ:TOK], z[:, SEQ:TOK], gr[:, par_, 8 * w + 8 * jj:8 * w + 8 * jj + 8], MUL).then_inc(S["a_step"], 1)
                dve.wait_ge(S["a_step"], blk * 3 + 2)
                hi = ah[:, par_ * EXP_J + jj, :]
                cp(hi, z).then_inc(S["a_step"], 1)
                dve.wait_ge(S["a_step"], blk * 3 + 3)
                tt(al[:, par_ * EXP_J + jj, :], z, hi.bitcast(F32), SUB).then_inc(S["a_ready"], 1)

            def collect(s, dc):
                dve.wait_ge(S["ff_ready"], s * KD + dc + 2)
                dve.wait_ge(S["ff_free"], s * KD + dc + 1)
                a = acc[:, dc, :].rearrange("p (h t) -> p h t", h=2)
                tt(a, a, ps[:, 4 + 2 * (dc % 2):6 + 2 * (dc % 2), 0:HALF], ADD).then_inc(S["ff_free"], 1)

            def group_in(par_, rnd):
                dve.wait_ge(g_l[par_], rnd * 16)
                dve.wait_ge(gt_l[par_], rnd * 16)

            def spilled(s, par_, rnd, item, zr):
                group_in(par_, rnd)
                for jj in range(EXP_J):
                    low_v(par_, jj, item + jj)
                    if jj < 2:
                        dve.wait_ge(S["ff_ready"], (s - 1) * KD + 1)
                    dve.wait_ge(zl[jj % 2], (zr + jj // 2) * 16)
                    weigh(s, par_, jj)
                    collect(s - 1, 2 * jj)
                    collect(s - 1, 2 * jj + 1)
            group_in(0, 1)
            for jj in range(2):
                dve.wait_ge(zl[jj], 16)
                weigh(0, 0, jj)
                low_u(TAIL_U - 2 + jj, SPILL - 2 + jj)
            for jj in range(EXP_J):
                low_v(0, jj, SPILL + jj)
            for jj in range(2, EXP_J):
                dve.wait_ge(zl[jj % 2], 32)
                weigh(0, 0, jj)
            with dve.Fori(0, SPILL_G // 2) as it:
                spilled(it * 2 + 1, 1, it + 1, it * 8 + (SPILL + 4), it * 4 + 3)
                spilled(it * 2 + 2, 0, it + 2, it * 8 + (SPILL + 8), it * 4 + 5)
            low_u(0, 2 * SPILL)
            low_u(1, 2 * SPILL + 1)

            def live(s, par_, rnd, item, more):
                group_in(par_, rnd)
                for jj in range(EXP_J):
                    if jj < 2:
                        low_u(jj + 2, item + (jj + 2))
                    dve.wait_ge(S["gelu_done"], s * EXP_J + jj + 1)
                    weigh(s, par_, jj)
                    if jj >= 2:
                        low_v(par_, jj - 2, item + (jj + 2))
                for q in range(4):
                    collect(s - 1, 2 * q)
                    collect(s - 1, 2 * q + 1)
                    if q < 2:
                        low_v(par_, q + 2, item + (q + 6))
                    elif more:
                        low_u(q - 2, item + (q + 6))
            n_live = GROUPS - SPILL_G
            with dve.Fori(0, (n_live - 1) // 2) as it:
                live(it * 2 + SPILL_G, 1, it + (SPILL_G // 2 + 1), it * 16 + 2 * SPILL, True)
                live(it * 2 + (SPILL_G + 1), 0, it + (SPILL_G // 2 + 2), it * 16 + (2 * SPILL + 8), True)
            live(GROUPS - 1, 1, GROUPS // 2, 2 * SPILL + 8 * (n_live - 1), False)
            dve.wait_ge(S["x_back"], 16)
            for c in range(KD):
                collect(GROUPS - 1, c)
                dve.wait_ge(S["ff_free"], 2 + (GROUPS - 1) * KD + c + 1)
                add_gated(x2, c, [(0, SEQ, acc[:, c, 0:SEQ])], acc[:, c, SEQ:TOK], 5)
                tt(sq[:, c, :], x2[:, c, :], x2[:, c, :], MUL).then_inc(S["chunk_sq"], 1)
            dve.wait_ge(S["sum_ready"], 3)
            inverse_ms(D, 0)
            dve.wait_ge(S["rstd_ready"], 5)
            for k in range(KD):
                stt(h2T[:, k, :], x2[:, k, :], par[:, FG + k:FG + k + 1], rstd, MUL, MUL).then_inc(S["fin_ready"], 1)


def one_hot_buckets(dist):
    dist = np.asarray(dist)
    b = np.where(dist < 16, dist, 16 + np.searchsorted(EDGES, dist, side="right"))
    b = np.where(dist < 0, 32, b)
    return (np.arange(33)[:, None] == b[None, :]).astype(np.float32)


def kernel(**a):
    import concourse.bacc as bacc
    from concourse.bass_utils import run_bass_kernel_spmd

    a = {k: np.asarray(v) for k, v in a.items()}
    cols = np.cumsum((0, 512, 512, 512, 256, 256, 256, 24))

    def feat(v):
        return v.reshape(-1, P).T

    def chunks(w):
        return w.reshape(KD, P, -1, P).transpose(2, 1, 0, 3)

    w = a["w_in"][0]
    qw = w[:, cols[2]:cols[3]].reshape(D, NKV, GRP, HD).transpose(0, 2, 1, 3).reshape(D, 512)
    kvw = [w[:, cols[i]:cols[i + 1]].reshape(D, NKV, 2, HD).transpose(0, 2, 1, 3).reshape(D, 256) for i in (3, 4, 5)]
    w_all = np.concatenate([w[:, :1024], qw] + kvw, axis=1)
    wout = a["w_out"][0]
    wout = np.concatenate([wout[:512], wout[512:].reshape(NKV, GRP, HD, D).transpose(1, 0, 2, 3).reshape(512, D)])
    nag = a["out_norm_att"][0].reshape(NKV, GRP, HD).transpose(1, 0, 2).reshape(512)
    par = np.concatenate([feat(v) for v in (a["norm1_g"][0], a["norm2_g"][0], a["final_g"], a["out_norm_lru"][0], nag,
                          a["conv_w"][0].reshape(-1), a["conv_b"][0], a["lru_ba"][0], a["lru_bi"][0],
                          a["lru_lambda"][0], a["peer_bq"][0])], axis=1)
    x = np.concatenate([a["x_prompt"].reshape(SEQ, D), a["x_sample"].reshape(NB, D)])
    c = np.concatenate([a["c_prompt"], a["c_sample"]])

    def pool(cache, which):
        return cache[0, :, :, :, which].transpose(0, 2, 3, 1).reshape(POOL * P, P)

    selk, selv = pool(a["cache_sel_kv"], 0), a["cache_sel_kv"][0, :, :, :, 1].reshape(POOL * P, P)
    win = a["cache_win_kv"][0]
    cw1 = a["cmp_w1"][0].transpose(0, 2, 1, 3)
    pos = np.concatenate([a["cmp_pos"][0].transpose(0, 2, 1)] * 2, axis=1)
    rows = np.arange(ROWS)
    ins = {
        "xT": x.T.reshape(KD, P, TOK).transpose(1, 0, 2), "cT": c.T.reshape(KD, P, 9).transpose(1, 0, 2),
        "par": par, "adab": feat(a["ada_b"][0]), "rel_bias": a["rel_bias"],
        "ada_w": a["ada_w"][0].reshape(KD, P, 6 * D).transpose(1, 0, 2),
        "w_in": chunks(w_all), "w_gate": w[:, cols[6]:].reshape(KD, P, 24).transpose(1, 0, 2),
        "w_out": wout.reshape(KD, P, D).transpose(1, 0, 2), "wq": chunks(a["peer_wq"][0]),
        "sk": a["peer_subkeys"][0].reshape(16, P, P).transpose(2, 0, 1),
        "state_conv": a["state_conv"][0].reshape(NB, 3, 4, P).transpose(3, 2, 1, 0).reshape(P, 4, 3 * NB),
        "state_h": a["state_lru_h"][0].reshape(NB, 4, P).transpose(2, 1, 0),
        "wlru": np.stack([a["lru_wa"][0].reshape(4, 2, HD, HD), a["lru_wi"][0].reshape(4, 2, HD, HD)])
                  .transpose(2, 3, 0, 1, 4).reshape(2, HD, 8, HD),
        "cmp_w1": cw1, "cmp_w2": a["cmp_w2"][0], "posT": pos, "page_table": a["page_table"].reshape(1, NB * PAGES),
        "pool_c": np.concatenate([pool(a["cache_cmp_kv"], 0), pool(a["cache_cmp_kv"], 1)], axis=1),
        "pool_s": np.concatenate([selk, selv], axis=1),
        "win_kT": win[:, :, :, 0].transpose(2, 3, 0, 1).reshape(P, NB, 512), "win_v": win[:, :, :, 1].reshape(NB, 512, P),
        "uT": a["peer_u"][0].reshape(P, P, KD, P).transpose(1, 3, 2, 0), "v": a["peer_v"][0].reshape(P, P, D),
        "ohd": one_hot_buckets(np.concatenate([1024 - np.arange(1153), np.zeros(8, np.int64)])),
        "oha": one_hot_buckets(np.arange(OHA_W) - 511),
        "ohw": one_hot_buckets(np.concatenate([[-1], 512 - np.arange(1, 512)])),
        "newmask": np.where(rows[:, None] // NH == np.arange(NB)[None, :], 0.0, NEG).astype(np.float32),
        "gsum": (rows[:, None] // GRP == rows[None, :] // GRP).astype(np.float32),
        "validq": (np.arange(P)[:, None] >= 31).astype(np.float32),
        "blkno": np.broadcast_to(np.arange(1, NSELB + 1, dtype=np.float32), (ROWS, NSELB)),
    }
    ins = {k: np.ascontiguousarray(v) for k, v in ins.items()}
    outs = {"o_y": (P, KD, TOK), "o_kv": (P, 6, TOK), "o_h": (P, 4, 9), "o_conv": (P, 4, 27),
            "o_wink": (P, NB, 512), "o_winv": (NB, 512, P)}
    nc = bacc.Bacc("TRN2", target_bir_lowering=False, num_devices=1)
    io = {k: nc.dram_tensor("in_" + k, v.shape, mybir.dt.from_np(v.dtype), kind="ExternalInput").ap() for k, v in ins.items()}
    for k, shape in outs.items():
        io[k] = nc.dram_tensor("out_" + k, shape, F32, kind="ExternalOutput").ap()
    io["rscratch"] = nc.dram_tensor("rscratch", (NH, 640), F32).ap()
    io["rrows"] = nc.dram_tensor("rrows", (P, NH, 640), F32).ap()
    io["gscratch"] = nc.dram_tensor("gscratch", (ROWS, 3), F32).ap()
    io["gw"] = nc.dram_tensor("gw", (SEQ // TC, P, P * TC), F32).ap()
    io["gwt"] = nc.dram_tensor("gwt", (P, P * NB), F32).ap()
    io["zs"] = nc.dram_tensor("zs", (SPILL, P, TOK), F32).ap()
    io["xspill"] = nc.dram_tensor("xspill", (P, KD, TOK), F32).ap()
    build(nc, io)
    got = run_bass_kernel_spmd(nc, [{"in_" + k: v for k, v in ins.items()}], core_ids=[0]).results[0]
    r = {k: got["out_" + k] for k in outs}

    y = r["o_y"].transpose(2, 1, 0).reshape(TOK, D)
    kv = r["o_kv"].reshape(NKV, HD, 3, 2, TOK).transpose(2, 4, 0, 3, 1)
    wk = r["o_wink"].reshape(NKV, HD, NB, 512).transpose(2, 3, 0, 1)
    wv = r["o_winv"].reshape(NB, 512, NKV, HD)
    old = np.stack([wk, wv], axis=3)[:, :511]
    new_win = np.concatenate([old, kv[2, SEQ:][:, None]], axis=1)
    h = r["o_h"].transpose(2, 1, 0).reshape(9, 512)
    conv = r["o_conv"].reshape(P, 4, 3, 9).transpose(3, 2, 1, 0).reshape(9, 3, 512)
    return (y[:SEQ][None], y[SEQ:][:, None],
            kv[0, :SEQ][None, None], kv[0, SEQ:][None, :, None],
            kv[1, :SEQ][None, None], kv[1, SEQ:][None, :, None],
            kv[2, :SEQ][None, None], new_win[None],
            h[0:1][None], h[1:][None], conv[0:1][None], conv[1:][None])
```
